# Optimizing a Trainium2 kernel written in Bass

```python
import math
import jax, jax.numpy as jnp
from jax import lax
import numpy as np

D_MODEL = 1024
BATCH = 1
SEQ = 256
DEPTH = 2

GRID_W = 64
CTX_LEN = 256
N_MIXERS = 2
EPS = 1e-6
N_MOD = 6

POOL_WINDOWS = (2, 4, 8, 16)
N_POOL_GROUPS = len(POOL_WINDOWS)
POOL_GROUP = D_MODEL // N_POOL_GROUPS

SSD_EXPAND = 2
D_INNER = SSD_EXPAND * D_MODEL
HEAD_DIM = 64
N_SSD_HEADS = D_INNER // HEAD_DIM
N_SSD_GROUPS = 4
HEADS_PER_GROUP = N_SSD_HEADS // N_SSD_GROUPS
D_STATE = 128
D_CONV = 4
CONV_PAD_LEFT = 2
CONV_PAD_RIGHT = D_CONV - 1 - CONV_PAD_LEFT
CHUNK = 128
BC_DIM = N_SSD_GROUPS * D_STATE
CONV_DIM = D_INNER + 2 * BC_DIM
IN_PROJ_DIM = D_INNER + CONV_DIM + 2 * N_SSD_HEADS

D_FF = 2816
N_EXPERTS = 8
TOP_K = 2
D_FF_EXPERT = 3584

N_EVEN_LAYERS = (DEPTH + 1) // 2
N_ODD_LAYERS = DEPTH // 2

kernel_name = "hybrid_pool_ssd_moe_dit_prefix"

def rmsnorm(x, w):
    xf = x.astype(jnp.float32)
    y = xf * lax.rsqrt(jnp.mean(xf * xf, axis=-1, keepdims=True) + EPS)
    return (y * w.astype(jnp.float32)).astype(x.dtype)

def modulate(h, shift, scale):
    return h * (1 + scale) + shift

def window_mean_minus_self(x, w):
    L = x.shape[1]
    lo = w // 2
    hi = w - 1 - lo
    cs = jnp.pad(jnp.cumsum(x.astype(jnp.float32), axis=1), ((0, 0), (1, 0), (0, 0)))
    t = jnp.arange(L)
    end = jnp.minimum(t + hi + 1, L)
    start = jnp.maximum(t - lo, 0)
    s = jnp.take(cs, end, axis=1) - jnp.take(cs, start, axis=1)
    cnt = (end - start).astype(jnp.float32)
    return (s / cnt[None, :, None]).astype(x.dtype) - x

def pool_mix(h, w_groups, scale):
    parts = [window_mean_minus_self(h[..., g * POOL_GROUP:(g + 1) * POOL_GROUP], w)
             for g, w in enumerate(POOL_WINDOWS)]
    p = jnp.stack(parts, axis=-2)
    y = jnp.einsum('nlgi,gio->nlgo', p, w_groups).reshape(h.shape)
    return y * scale

def dwconv_centred(x, w, b):
    L = x.shape[1]
    xp = jnp.pad(x, ((0, 0), (CONV_PAD_LEFT, CONV_PAD_RIGHT), (0, 0)))
    y = b
    for k in range(D_CONV):
        y = y + xp[:, k:k + L] * w[k]
    return y

def ssd_chunked(x, dt, A, B, C, h0, need_y):
    b, L = x.shape[:2]
    nc = L // CHUNK
    xd = (x * dt[..., None]).reshape(b, nc, CHUNK, N_SSD_GROUPS, HEADS_PER_GROUP, HEAD_DIM)
    a = (dt * A).astype(jnp.float32).reshape(b, nc, CHUNK, N_SSD_GROUPS, HEADS_PER_GROUP)
    a_cum = jnp.cumsum(jnp.transpose(a, (0, 3, 4, 1, 2)), axis=-1)
    Bc = B.reshape(b, nc, CHUNK, N_SSD_GROUPS, D_STATE)
    Cc = C.reshape(b, nc, CHUNK, N_SSD_GROUPS, D_STATE)
    decay_to_end = jnp.exp(a_cum[..., -1:] - a_cum)
    states = jnp.einsum('bcsgn,bgecs,bcsgep->cbgepn', Bc, decay_to_end, xd).astype(jnp.float32)
    chunk_decay = jnp.moveaxis(jnp.exp(a_cum[..., -1]), -1, 0)

    def step(h, inp):
        s, d = inp
        return h * d[..., None, None] + s, h

    h_final, h_init = lax.scan(step, h0, (states, chunk_decay))
    if not need_y:
        return None, h_final
    seg = a_cum[..., :, None] - a_cum[..., None, :]
    lower = jnp.tril(jnp.ones((CHUNK, CHUNK), dtype=bool))
    Lmat = jnp.exp(jnp.where(lower, seg, -jnp.inf))
    CB = jnp.einsum('bclgn,bcsgn->bgcls', Cc, Bc)
    y_diag = jnp.einsum('bgcls,bgecls,bcsgep->bclgep', CB, Lmat, xd)
    y_off = jnp.einsum('bclgn,cbgepn,bgecl->bclgep', Cc, h_init, jnp.exp(a_cum))
    y = (y_diag + y_off).reshape(b, L, N_SSD_HEADS, HEAD_DIM)
    return y, h_final

def ssd_mixer(u_ctx, u_lat, in_w, conv_w, conv_b, A_log, dt_bias, D_skip, norm_w, out_w, ctx_out):
    A = -jnp.exp(A_log.astype(jnp.float32))

    def flip(t):
        return jnp.flip(t, axis=1)

    def bidir(u, h0_f, h0_b, need_y):
        bsz, L = u.shape[:2]
        proj = u @ in_w
        z = proj[..., :D_INNER]
        xbc = jax.nn.silu(dwconv_centred(proj[..., D_INNER:D_INNER + CONV_DIM], conv_w, conv_b))
        dt = jax.nn.softplus(
            proj[..., D_INNER + CONV_DIM:].astype(jnp.float32).reshape(bsz, L, 2, N_SSD_HEADS) + dt_bias)
        xs = xbc[..., :D_INNER].reshape(bsz, L, N_SSD_HEADS, HEAD_DIM)
        Bm = xbc[..., D_INNER:D_INNER + BC_DIM].reshape(bsz, L, N_SSD_GROUPS, D_STATE)
        Cm = xbc[..., D_INNER + BC_DIM:].reshape(bsz, L, N_SSD_GROUPS, D_STATE)
        y_f, hf = ssd_chunked(xs, dt[:, :, 0], A[0], Bm, Cm, h0_f, need_y)
        y_b, hb = ssd_chunked(flip(xs), flip(dt[:, :, 1]), A[1], flip(Bm), flip(Cm), h0_b, need_y)
        if not need_y:
            return None, hf, hb
        y = y_f + flip(y_b) + xs * D_skip[:, None]
        y = y.reshape(bsz, L, D_INNER).astype(u.dtype)
        y = rmsnorm(y * jax.nn.silu(z), norm_w) @ out_w
        return y, hf, hb

    zero = jnp.zeros((u_ctx.shape[0], N_SSD_GROUPS, HEADS_PER_GROUP, HEAD_DIM, D_STATE), jnp.float32)
    y_ctx, hf, hb = bidir(u_ctx, zero, zero, ctx_out)
    y_lat, _, _ = bidir(u_lat, hf, hb, True)
    return y_ctx, y_lat

def swiglu(h, w1, w3, w2):
    return (jax.nn.silu(h @ w1) * (h @ w3)) @ w2

def moe_swiglu(h, router_w, w1, w3, w2):
    logits = (h @ router_w).astype(jnp.float32)
    top_v, top_i = lax.top_k(logits, TOP_K)
    gates = jax.nn.softmax(top_v, axis=-1)
    combine = jnp.sum(jax.nn.one_hot(top_i, N_EXPERTS, dtype=jnp.float32) * gates[..., None], axis=-2)
    combine = combine.astype(h.dtype)
    out = jnp.zeros_like(h)
    for e in range(N_EXPERTS):
        out = out + combine[..., e:e + 1] * swiglu(h, w1[e], w3[e], w2[e])
    return out

def setup_inputs(seed: int = 0) -> dict:
    key = jax.random.key(seed)
    ks = jax.random.split(key, 28)
    f32 = jnp.float32

    def nrm(k, shape, s):
        return jax.random.normal(k, shape, f32) * s

    dt0 = jnp.exp(jax.random.uniform(ks[14], (N_ODD_LAYERS, 2, N_SSD_HEADS), f32,
                                     math.log(1e-3), math.log(1e-1)))
    return {
        "x": nrm(ks[0], (BATCH, SEQ, D_MODEL), 1.0),
        "c": nrm(ks[1], (BATCH, D_MODEL), 1.0),
        "ctx": nrm(ks[2], (BATCH, CTX_LEN, D_MODEL), 1.0),
        "c_ctx": nrm(ks[3], (D_MODEL,), 1.0),
        "ada_w": nrm(ks[4], (DEPTH, D_MODEL, N_MOD * D_MODEL), 0.5 * D_MODEL ** -0.5),
        "ada_b": nrm(ks[5], (DEPTH, N_MOD * D_MODEL), 0.02),
        "norm_mix_w": 1.0 + nrm(ks[6], (DEPTH, D_MODEL), 0.01),
        "norm_ffn_w": 1.0 + nrm(ks[7], (DEPTH, D_MODEL), 0.01),
        "pool_w": nrm(ks[8], (N_EVEN_LAYERS, N_POOL_GROUPS, POOL_GROUP, POOL_GROUP), POOL_GROUP ** -0.5),
        "pool_scale": 1.0 + nrm(ks[9], (N_EVEN_LAYERS, D_MODEL), 0.1),
        "ssd_in_w": nrm(ks[10], (N_ODD_LAYERS, D_MODEL, IN_PROJ_DIM), D_MODEL ** -0.5),
        "ssd_conv_w": nrm(ks[11], (N_ODD_LAYERS, D_CONV, CONV_DIM), D_CONV ** -0.5),
        "ssd_conv_b": nrm(ks[12], (N_ODD_LAYERS, CONV_DIM), 0.02),
        "ssd_A_log": jnp.log(jax.random.uniform(ks[13], (N_ODD_LAYERS, 2, N_SSD_HEADS), f32, 1.0, 16.0)),
        "ssd_dt_bias": dt0 + jnp.log(-jnp.expm1(-dt0)),
        "ssd_D": 1.0 + nrm(ks[15], (N_ODD_LAYERS, N_SSD_HEADS), 0.1),
        "ssd_norm_w": 1.0 + nrm(ks[16], (N_ODD_LAYERS, D_INNER), 0.01),
        "ssd_out_w": nrm(ks[17], (N_ODD_LAYERS, D_INNER, D_MODEL), D_INNER ** -0.5),
        "ffn_w1": nrm(ks[18], (N_EVEN_LAYERS, D_MODEL, D_FF), D_MODEL ** -0.5),
        "ffn_w3": nrm(ks[19], (N_EVEN_LAYERS, D_MODEL, D_FF), D_MODEL ** -0.5),
        "ffn_w2": nrm(ks[20], (N_EVEN_LAYERS, D_FF, D_MODEL), D_FF ** -0.5),
        "moe_router_w": nrm(ks[21], (N_ODD_LAYERS, D_MODEL, N_EXPERTS), D_MODEL ** -0.5),
        "moe_w1": nrm(ks[22], (N_ODD_LAYERS, N_EXPERTS, D_MODEL, D_FF_EXPERT), D_MODEL ** -0.5),
        "moe_w3": nrm(ks[23], (N_ODD_LAYERS, N_EXPERTS, D_MODEL, D_FF_EXPERT), D_MODEL ** -0.5),
        "moe_w2": nrm(ks[24], (N_ODD_LAYERS, N_EXPERTS, D_FF_EXPERT, D_MODEL), D_FF_EXPERT ** -0.5),
        "final_norm_w": 1.0 + nrm(ks[25], (D_MODEL,), 0.01),
    }

def reference(x, c, ctx, c_ctx, ada_w, ada_b, norm_mix_w, norm_ffn_w, pool_w, pool_scale,
              ssd_in_w, ssd_conv_w, ssd_conv_b, ssd_A_log, ssd_dt_bias, ssd_D, ssd_norm_w, ssd_out_w,
              ffn_w1, ffn_w3, ffn_w2, moe_router_w, moe_w1, moe_w3, moe_w2, final_norm_w):
    bsz, n_lat, d = x.shape
    rows = n_lat // GRID_W
    c_act = jax.nn.silu(c)
    cc_act = jax.nn.silu(c_ctx)[None]
    h_lat, h_ctx = x, ctx
    for i in range(DEPTH):
        last = i == DEPTH - 1
        j = i // 2
        mod_lat = jnp.split((c_act @ ada_w[i] + ada_b[i])[:, None, :], N_MOD, axis=-1)
        mod_ctx = jnp.split((cc_act @ ada_w[i] + ada_b[i])[:, None, :], N_MOD, axis=-1)
        sh1, sc1, g1, sh2, sc2, g2 = mod_lat
        sh1c, sc1c, g1c, sh2c, sc2c, g2c = mod_ctx

        u_lat = modulate(rmsnorm(h_lat, norm_mix_w[i]), sh1, sc1)
        if i % N_MIXERS == 0:
            y_lat = pool_mix(u_lat.reshape(bsz * rows, GRID_W, d), pool_w[j], pool_scale[j]).reshape(bsz, n_lat, d)
            if not last:
                u_ctx = modulate(rmsnorm(h_ctx, norm_mix_w[i]), sh1c, sc1c)
                y_ctx = pool_mix(u_ctx, pool_w[j], pool_scale[j])
        else:
            u_ctx = modulate(rmsnorm(h_ctx, norm_mix_w[i]), sh1c, sc1c)
            y_ctx, y_lat = ssd_mixer(u_ctx, u_lat, ssd_in_w[j], ssd_conv_w[j], ssd_conv_b[j], ssd_A_log[j],
                                     ssd_dt_bias[j], ssd_D[j], ssd_norm_w[j], ssd_out_w[j], not last)
        h_lat = h_lat + g1 * y_lat
        if not last:
            h_ctx = h_ctx + g1c * y_ctx

        v_lat = modulate(rmsnorm(h_lat, norm_ffn_w[i]), sh2, sc2)
        if i % 2 == 0:
            h_lat = h_lat + g2 * swiglu(v_lat, ffn_w1[j], ffn_w3[j], ffn_w2[j])
        else:
            h_lat = h_lat + g2 * moe_swiglu(v_lat, moe_router_w[j], moe_w1[j], moe_w3[j], moe_w2[j])
        if not last:
            v_ctx = modulate(rmsnorm(h_ctx, norm_ffn_w[i]), sh2c, sc2c)
            if i % 2 == 0:
                h_ctx = h_ctx + g2c * swiglu(v_ctx, ffn_w1[j], ffn_w3[j], ffn_w2[j])
            else:
                h_ctx = h_ctx + g2c * moe_swiglu(v_ctx, moe_router_w[j], moe_w1[j], moe_w3[j], moe_w2[j])
    return rmsnorm(h_lat, final_norm_w)


_drawn_inputs = setup_inputs


def setup_inputs(seed=0):
    import zlib

    import numpy as np

    out = dict(_drawn_inputs(seed))
    spreads = {}
    factors = {'ctx': 2.811,
     'norm_mix_w': 6.637,
     'norm_ffn_w': 4.338,
     'ssd_conv_b': 19.056,
     'ssd_D': 42.952,
     'ssd_norm_w': 23.445,
     'final_norm_w': 32.917}
    for name, (base, spread) in spreads.items():
        noise = np.random.default_rng([zlib.crc32(name.encode()), seed]).standard_normal(out[name].shape)
        drawn = base * np.exp(spread * noise) if base else spread * noise
        out[name] = __import__('jax').numpy.asarray(drawn.astype(out[name].dtype))
    for name, factor in factors.items():
        out[name] = (out[name] * factor).astype(out[name].dtype)
    return out
```

```python
from contextlib import ExitStack

import numpy as np

import concourse.bass as bass
from concourse import mybir

F32 = mybir.dt.float32
F32R = mybir.dt.float32r
I32 = mybir.dt.int32
ALU = mybir.AluOpType
ACT = mybir.ActivationFunctionType
AX_X = mybir.AxisListType.X

P = 128
D = 1024
KD = D // P
NTOK = 256
NT2 = 2 * NTOK
GRID_W = 64
EPS = 1e-6
NMOD = 6
WINDOWS = (2, 4, 8, 16)
DI = 2048
NG = 4
NH = 32
HPG = NH // NG
BC = 512
DSTATE = 128
DFF = 2816
NE = 8
DFE = 3584
TILE = 2048

FF_BLOCKS = DFF // 256
A0 = 0
POOL0 = A0 + 24
FFN0 = POOL0 + 1
E0 = FFN0 + 3 * FF_BLOCKS
IN0 = E0 + 24
OUT0 = IN0 + 1 + 5 * NG
NTILES = OUT0 + 8
RAW1, SPL1 = 3, 2

EB = DFE // 512
TPI = 6 * EB
RAW2, SPL2 = 6, 3
MAX_ITEMS = NE + 3

PADW = 8 + 4 * (GRID_W + 8) + NTOK + 8


def hybrid_backbone(nc, a, out):
    ctx = ExitStack()
    with ctx:
        def sem(name):
            return ctx.enter_context(nc.semaphore(name))

        def sb(name, shape, dt=F32):
            return ctx.enter_context(nc.sbuf_tensor(name, shape, dt))

        bank = [ctx.enter_context(nc.psum_tensor(f"bank{i}", [P, 512], F32)) for i in range(8)]

        ident = sb("ident", [P, P])
        ones = sb("ones", [P, P])
        tri_le = sb("tri_le", [P, P])
        tri_ge = sb("tri_ge", [P, P])
        tri_lt = sb("tri_lt", [P, P])
        tri_gt = sb("tri_gt", [P, P])
        fold = sb("fold", [80, 32])
        slot_id = sb("slot_id", [P, P])
        before = sb("before", [P, NE, NE])
        expert_id = sb("expert_id", [P, NE])
        eps_col = sb("eps_col", [P, 1])
        va = sb("va", [P, 64])
        vb = sb("vb", [P, 120])
        mc = [sb(f"mc{i}", [P, 3, 2, 2, KD]) for i in range(2)]
        aff = sb("aff", [P, 4, 2, KD])
        dcol = sb("dcol", [P, 16])
        sel_row = sb("sel_row", [5, P])

        top = [(nc.sbuf_base + 31) // 32 * 32]
        origin = top[0]

        def at(name, off_kb, shape, dt=F32):
            size = int(np.prod(shape[1:])) * 4
            off = origin + int(off_kb * 1024)
            assert off + size <= nc.sbuf_usable_end, (name, off + size - nc.sbuf_usable_end)
            top[0] = max(top[0], off + size)
            return nc.alloc_sbuf_tensor_at(name, shape, dt, offset=off)

        raw = at("raw", 0, [P, RAW1, TILE])
        whi = at("whi", 24, [P, SPL1, TILE], F32R)
        wlo = at("wlo", 40, [P, SPL1, TILE], F32R)
        uh = at("uh", 56, [P, KD, NT2], F32R)
        ul = at("ul", 72, [P, KD, NT2], F32R)
        ht = at("ht", 88, [P, 2, KD, NTOK])
        sq = at("sq", 104, [P, 2, KD, NTOK])
        xtok = at("xtok", 120, [P, 4, D])
        tn = at("tn", 120, [P, 2, KD, NTOK])
        padded = at("padded", 136, [P, KD, PADW])
        win = at("win", 153.5, [P, 2, 2, PADW])
        wing = at("wing", 162.5, [P, 2, 2, PADW])
        inv_cnt = at("inv_cnt", 80, [P, 4, NT2])
        sg = at("sg", 136, [P, 2, NT2])
        gf = at("gf", 140, [P, 2, NT2])
        gh = at("gh", 144, [P, 2, 2, NT2], F32R)
        gl = at("gl", 152, [P, 2, 2, NT2], F32R)
        mrow = at("mrow", 171.5, [4, 2, 2048])
        rb = at("rb", 187.5, [80, 2, 3, P])
        rstd = at("rstd", 190.5, [P, NT2])
        cst = at("cst", 192.5, [P, KD, P], F32R)
        rows_in = at("rows_in", 104, [P, 2, P])

        y2 = at("y2", 104, [P, 16, NTOK])
        xs_tok = at("xs_tok", 120, [P, 2, 4, 512])
        b_tok = at("b_tok", 136, [P, 2, 4, P])
        bt = at("bt", 140, [P, 2, NTOK])
        ct = at("ct", 142, [P, 2, NTOK])
        xst = at("xst", 144, [P, 2, 4, NTOK])
        sz = at("sz", 152, [P, 2, 4, NTOK])
        xd = at("xd", 160, [P, 2, 2, 512])
        xdd = [at("xdd0", 168, [P, 512]), at("xdd1", 199.25, [P, 512])]
        seg = at("seg", 170, [P, 2, 512])
        ytmp = at("ytmp", 174, [P, 512])
        ysum = at("ysum", 198, [P, NTOK])
        csc = at("csc", 178, [P, 2, 512])
        cp = at("cp", 182, [P, 2, 2, 260])
        cacc = at("cacc", 186.25, [P, 2, 512])
        ccv = at("ccv", 190.25, [P, 2, NTOK])
        cb = at("cb", 192.25, [P, 2, 2, P])
        states = at("states", 96, [P, 4, 512])
        dt_tok = at("dt_tok", 194.25, [P, 4, 64])
        a_tok = at("a_tok", 195.25, [P, 4, 64])
        wdec = at("wdec", 196.25, [P, 8, NH])
        acs = at("acs", 197.25, [P, 4, NH])
        ry = at("ry", 197.875, [P, 8])
        dts = at("dts", 160, [P, 5, NT2])
        dpar = at("dpar", 197.8125, [P, 4])

        raw2 = at("raw2", 0, [P, RAW2, TILE])
        yh = uh[:].rearrange("p k (c n) -> p (k c) n", c=2)
        yl = ul[:].rearrange("p k (c n) -> p (k c) n", c=2)
        whi2 = at("whi2", 48, [P, SPL2, TILE], F32R)
        wlo2 = at("wlo2", 72, [P, SPL2, TILE], F32R)
        xgh = at("xgh", 96, [P, KD, P], F32R)
        xgl = at("xgl", 100, [P, KD, P], F32R)
        gth = at("gth", 104, [P, 4, P], F32R)
        gtl = at("gtl", 106, [P, 4, P], F32R)
        sge = at("sge", 108, [P, 512])
        gme = at("gme", 110, [P, 512])
        osb = at("osb", 112, [P, D])
        pick = at("pick", 116, [P, 2, P])
        pickg = at("pickg", 117, [P, 2, P])
        put = at("put", 118, [P, 2, P])
        hl = at("hl", 120, [P, 2, D])
        mods = at("mods", 128, [P, 4, D])
        nfw = at("nfw", 144, [P, D])
        fnw = at("fnw", 148, [P, D])
        v = at("v", 152, [P, 2, D])
        vt = at("vt", 160, [P, KD, NTOK])
        acc = at("acc", 168, [P, 2, D])
        mrow5 = at("mrow5", 176, [5, 4, D])
        rw = at("rw", 192, [P, KD, NE])
        lg = at("lg", 192.5, [P, 2, NE])
        cmp = at("cmp", 193, [P, 2, NE, NE])
        eqs = at("eqs", 193.5, [P, 2, NE, NE])
        sel = at("sel", 194, [P, 2, NE])
        gate = at("gate", 194.125, [P, 2, NE])
        pos = at("pos", 194.25, [P, 2, NE])
        rsc = at("rsc", 194.375, [P, 16])
        cnt = at("cnt", 194.5, [P, NE])
        over = at("over", 194.625, [P, NE])
        more = at("more", 194.75, [P, 3, NE])
        tmp3 = at("tmp3", 195, [P, 3, NE])
        pos_item = at("pos_item", 195.25, [P, 2, 12])
        gate_item = at("gate_item", 195.375, [P, 2, 12])
        ftab = at("ftab", 195.5, [P, 16])
        itab = at("itab", 195.75, [1, 16], I32)
        stat = at("stat", 196, [P, 16])
        sq2 = at("sq2", 160, [P, D])

        scr = nc.dram_tensor("mod_scratch", [2, 3, 4, 2048], F32, kind="Internal").ap()

        landed = [sem(f"landed{i}") for i in range(RAW1)]
        hi_done, lo_done, used = sem("hi_done"), sem("lo_done"), sem("used")
        consts_ready = sem("consts_ready")
        loaded_x, loaded_vec, loaded_bias, loaded_misc = sem("loaded_x"), sem("loaded_vec"), sem("loaded_bias"), sem("loaded_misc")
        vec_t, vec_cols, cst_ready = sem("vec_t"), sem("vec_cols"), sem("cst_ready")
        x_t, x_copied = sem("x_t"), sem("x_copied")
        sq_ready, ms_ready, sd_ready, tn_ready = sem("sq_ready"), sem("ms_ready"), sem("sd_ready"), sem("tn_ready")
        mod_row, mod_saved, mod_back = sem("mod_row"), sem("mod_saved"), sem("mod_back")
        fold_mm, mc_ready = sem("fold_mm"), sem("mc_ready")
        pads_zero, pad_ready, pool_g, pool_v = sem("pads_zero"), sem("pad_ready"), sem("pool_g"), sem("pool_v")
        uh_ready, ul_ready = sem("uh_ready"), sem("ul_ready")
        pool_mm, pool_added = sem("pool_mm"), sem("pool_added")
        ffn_h1, ffn_silu, ffn_h3, ffn_g = sem("ffn_h1"), sem("ffn_silu"), sem("ffn_h3"), sem("ffn_g")
        ffn_gh, ffn_gl, ffn_out, ffn_added = sem("ffn_gh"), sem("ffn_gl"), sem("ffn_out"), sem("ffn_added")
        in_mm, in_taken, landed_c, conv_acc, conv_out = sem("in_mm"), sem("in_taken"), sem("landed_c"), sem("conv_acc"), sem("conv_out")
        dt_steps, dt_act, a_ready = sem("dt_steps"), sem("dt_act"), sem("a_ready")
        aux_mm, aux_taken, wdec_ready = sem("aux_mm"), sem("aux_taken"), sem("wdec_ready")
        z_ready, cb_ready, st_ready = sem("z_ready"), sem("cb_ready"), sem("st_ready")
        xd_ready, xdd_ready = sem("xd_ready"), sem("xdd_ready")
        bc_mm, seg_ready, exp_ready, mix_ready = sem("bc_mm"), sem("seg_ready"), sem("exp_ready"), sem("mix_ready")
        y_mm, y_taken, ysum_ready, pads2 = sem("y_mm"), sem("y_taken"), sem("ysum_ready"), sem("pads2")
        yw_ready, yh_ready, yl_ready, ry_root, ry_ready = sem("yw_ready"), sem("yh_ready"), sem("yl_ready"), sem("ry_root"), sem("ry_ready")
        rows_back, hl_ready, mods_ready = sem("rows_back"), sem("hl_ready"), sem("mods_ready")
        h_ready, hsq_ready, v_ready, lg_mm, rt_dve, rt_act, rt_mm, tab_ready = (sem(n) for n in (
            "h_ready", "hsq_ready", "v_ready", "lg_mm", "rt_dve", "rt_act", "rt_mm", "tab_ready"))
        landed2 = [sem(f"expert_landed{i}") for i in range(RAW2)]
        hi2, lo2, used2 = sem("expert_hi"), sem("expert_lo"), sem("expert_used")
        pick_ready, put_mm, put_ready = sem("pick_ready"), sem("put_mm"), sem("put_ready")
        gather_mm, xgh_ready, xgl_ready = sem("gather_mm"), sem("xgh_ready"), sem("xgl_ready")
        silu2, gm_ready, turn_mm, gth_ready, gtl_ready = (sem(n) for n in ("silu2", "gm_ready", "turn_mm", "gth_ready", "gtl_ready"))
        osb_ready, scat_mm, acc_added, out_sq, out_ready, out_done = (sem(n) for n in (
            "osb_ready", "scat_mm", "acc_added", "out_sq", "out_ready", "out_done"))

        block = ctx.enter_context(nc.Block())

        c_tiles = [IN0 + 1 + 5 * g for g in range(NG)]

        def tile_ref(t):
            return t if isinstance(t, tuple) else (t, None)

        def val(const, coef, reg):
            return const if reg is None else reg * coef + const

        def val2(const, i, b, coef):
            x = const if i is None else i * TPI + const
            return x if b is None else b * coef + x

        def val3(const, i, b):
            x = const if i is None else i * EB + const
            return x if b is None else x + b

        def split_hi(e, t):
            k, reg = tile_ref(t)
            e.wait_ge(landed[k % RAW1], val(16 * (k // RAW1 + 1), 32, reg))
            if reg is None and k in c_tiles:
                e.wait_ge(landed_c, 16 * (c_tiles.index(k) + 1))
            if k >= SPL1:
                e.wait_ge(used, val(k - SPL1 + 1, 6, reg))
            e.activation(whi[:, k % SPL1, :], raw[:, k % RAW1, :], ACT.Copy).then_inc(hi_done, 1)

        def split_lo(e, t):
            k, reg = tile_ref(t)
            e.wait_ge(hi_done, val(k + 1, 6, reg))
            e.tensor_tensor(wlo[:, k % SPL1, :], raw[:, k % RAW1, :], whi[:, k % SPL1, :].bitcast(F32),
                            ALU.subtract).then_inc(lo_done, 1)

        def w_ready(e, t):
            k, reg = tile_ref(t)
            e.wait_ge(lo_done, val(k + 1, 6, reg))
            return k % SPL1

        def mod_src(layer, t):
            n, kh = t // 2, t % 2
            return a["ada_w"][layer, kh * 512:(kh + 1) * 512, n * 512:(n + 1) * 512].rearrange("(k p) n -> p k n", p=P)

        def cols_src(w, c0):
            return w[:, c0:c0 + 256].rearrange("(k p) n -> p k n", p=P)

        def pool_windows(e, g, w):
            src, n = padded[:, 2 * g:2 * g + 2, :], PADW
            e.tensor_tensor(w[:, 0, :, 1:n], src[:, :, 0:n - 1], src[:, :, 1:n], ALU.add)
            e.drain()
            cur, sh = 0, 1
            for _ in range(g):
                e.tensor_tensor(w[:, 1 - cur, :, sh:n - sh], w[:, cur, :, 0:n - 2 * sh], w[:, cur, :, 2 * sh:n], ALU.add)
                e.drain()
                cur, sh = 1 - cur, 2 * sh
            c0 = 8 + 4 * (GRID_W + 8)
            lat = lambda x: x[:, 8:c0].rearrange("p (r w) -> p r w", w=GRID_W + 8)[:, :, 0:GRID_W]
            rows = lambda x: x.rearrange("p (r w) -> p r w", w=GRID_W)
            for k in range(2):
                e.tensor_tensor(rows(tn[:, 0, 2 * g + k, :]), lat(w[:, cur, k, :]), rows(inv_cnt[:, g, 0:NTOK]), ALU.mult)
                e.tensor_tensor(tn[:, 1, 2 * g + k, :], w[:, cur, k, c0:c0 + NTOK], inv_cnt[:, g, NTOK:], ALU.mult)
            e.drain()
            for k in range(2):
                e.tensor_tensor(rows(tn[:, 0, 2 * g + k, :]), rows(tn[:, 0, 2 * g + k, :]), lat(padded[:, 2 * g + k, :]), ALU.subtract)
                e.tensor_tensor(tn[:, 1, 2 * g + k, :], tn[:, 1, 2 * g + k, :], padded[:, 2 * g + k, c0:c0 + NTOK], ALU.subtract)

        def two(x):
            return x.rearrange("p (s n) -> p s n", s=2)

        def split_u_hi(e, k):
            e.activation(two(uh[:, k, :]), tn[:, :, k, :], ACT.Copy).then_inc(uh_ready, 1)

        def split_u_lo(e, k, base):
            e.wait_ge(uh_ready, base + k + 1)
            e.tensor_tensor(two(ul[:, k, :]), tn[:, :, k, :], two(uh[:, k, :].bitcast(F32)), ALU.subtract).then_inc(ul_ready, 1)

        def w1_tile(j):
            return FFN0 + 2 + 3 * (j - 1) if j else FFN0

        def w2_tile(j):
            return E0 - 1 if j == FF_BLOCKS - 1 else FFN0 + 3 * j + 4

        def chunk_done(e, s, tile, j, c, it):
            if c == 0:
                e.wait_ge(s, val(j + 1, 2, it))
            else:
                e.wait_ge(used, val(tile + 1, 6, it))

        aux = [("dt", 0, 0), ("decay", 0, 0)]
        for g in range(NG + 1):
            if g:
                aux += [("cb", g - 1, 0)] + [("state", g - 1, i) for i in range(4)]
            if g < NG:
                aux += [("turn", g, i) for i in range(5)]
        aux += [("resid", 0, i) for i in range(4)] + [("mods", 0, i) for i in range(8)] + [("v", 0, i) for i in range(4)]
        aux_no = {key: n for n, key in enumerate(aux)}

        def in_tile(g, j):
            return IN0 + 1 + 5 * g + j

        def in_chunk(g, j, c):
            return 1 + 10 * g + 2 * j + c

        @block.sync
        def _(e):
            def load(t, src, shape):
                k, reg = tile_ref(t)
                if k >= RAW1:
                    e.wait_ge(lo_done, val(k - RAW1 + 1, 6, reg))
                dst = raw[:, k % RAW1, :].rearrange("p (k n) -> p k n", k=shape)
                e.dma_start(dst, src).then_inc(landed[k % RAW1], 16)

            for t in range(24):
                load(A0 + t, mod_src(0, t), 4)
            load(POOL0, a["pool_w"][0].rearrange("g (i p) o -> p (g i) o", p=P), 8)
            w1, w3, w2 = a["ffn_w1"][0], a["ffn_w3"][0], a["ffn_w2"][0]
            load(FFN0, cols_src(w1, 0), 8)
            load(FFN0 + 1, cols_src(w3, 0), 8)
            with e.Fori(0, FF_BLOCKS // 2) as it:
                for u in range(2):
                    k = FFN0 + 2 + 3 * u
                    c = it * 512 + (1 + u) * 256
                    load((k, it), w1[:, bass.ds(c, 256)].rearrange("(k p) n -> p k n", p=P), 8)
                    load((k + 1, it), w3[:, bass.ds(c, 256)].rearrange("(k p) n -> p k n", p=P), 8)
                    load((k + 2, it), w2[bass.ds(it * 512 + u * 256, 256), :].rearrange("(k p) n -> p k n", p=P), 2)
            load(E0 - 1, w2[DFF - 256:DFF, :].rearrange("(k p) n -> p k n", p=P), 2)
            for t in range(24):
                load(E0 + t, mod_src(1, t), 4)
            inw = a["ssd_in_w"][0]
            load(IN0, cols_src(inw, inw.shape[1] - 256), 8)
            for g in range(NG):
                k = in_tile(g, 0)
                e.wait_ge(lo_done, k - RAW1 + 1)
                dst = raw[:, k % RAW1, :].rearrange("p (k b n) -> p b k n", k=KD, b=2)
                for b_, done in ((0, landed[k % RAW1]), (1, landed_c)):
                    c0 = 2 * DI + b_ * BC + g * P
                    e.dma_start(dst[:, b_], inw[:, c0:c0 + P].rearrange("(k p) n -> p k n", p=P)).then_inc(done, 16)
                for j in (0, 1):
                    load(in_tile(g, 1 + j), cols_src(inw, DI + 512 * g + 256 * j), 8)
                for j in (0, 1):
                    load(in_tile(g, 3 + j), cols_src(inw, 512 * g + 256 * j), 8)
            for n in range(2):
                for kq in range(4):
                    load(OUT0 + 4 * n + kq, a["ssd_out_w"][0][kq * 512:(kq + 1) * 512, n * 512:(n + 1) * 512].rearrange("(k p) n -> p k n", p=P), 4)
            def load2(k, i, b, coef, src, kk):
                e.wait_ge(lo2, val2(k + 1, i, b, coef))
                e.dma_start(raw2[:, k % RAW2, :].rearrange("p (k n) -> p k n", k=kk), src).then_inc(landed2[k % RAW2], 16)

            m1 = a["moe_w1"][0].rearrange("e (h k p) n -> e h p k n", h=2, p=P)
            m3 = a["moe_w3"][0].rearrange("e (h k p) n -> e h p k n", h=2, p=P)
            m2 = a["moe_w2"][0].rearrange("e (f k p) n -> e f p k n", k=2, p=P)
            one = lambda x: x.rearrange("o p k n -> p (o k) n")

            def up_tiles(k, i, b, ex, blk):
                for n, m in enumerate((m1, m3)):
                    for half in range(2):
                        cols = bass.ds(blk * 512, 512) if b is not None else slice(blk * 512, blk * 512 + 512)
                        load2(k + 2 * n + half, i, b, 6, one(m[bass.ds(ex, 1), half, :, :, cols]), 4)

            def down_tiles(k, i, b, ex, blk):
                for half in range(2):
                    f = (blk * 2 + half)
                    src = m2[bass.ds(ex, 1), bass.ds(f, 1) if b is not None else slice(f, f + 1)]
                    load2(k + half, i, b, 6, src.rearrange("o f p k n -> p (o f k) n"), 2)

            e.wait_ge(tab_ready, 1)
            count = e.value_load(itab[0:1, 12:13], min_val=NE, max_val=MAX_ITEMS)
            with e.Fori(0, count) as i:
                ex = e.value_load(itab[0:1, bass.ds(i, 1)], min_val=0, max_val=NE - 1)
                up_tiles(0, i, None, ex, 0)
                with e.Fori(0, EB - 1) as b:
                    up_tiles(4, i, b, ex, b + 1)
                    down_tiles(8, i, b, ex, b)
                down_tiles(TPI - 2, i, None, ex, EB - 1)
            for k in range(2):
                e.wait_ge(lo2, count * TPI + (k + 1))
                e.dma_start(raw2[:, k, :].rearrange("p (k n) -> p k n", k=4), one(m1[0:1, k, :, :, 0:512])).then_inc(landed2[k], 16)
            for t in range(2):
                e.wait_ge(out_ready, t + 1)
                e.dma_start(out[0, t * P:(t + 1) * P, :], acc[:, t, :]).then_inc(out_done, 16)
            e.wait_ge(out_done, 32)

        @block.gpsimd
        def _(e):
            e.memset(ident[:], 0.0)
            e.memset(ones[:], 1.0)
            e.memset(fold[:], 0.0)
            e.memset(sel_row[:], 1.0)
            e.memset(eps_col[:], EPS)
            e.memset(before[:], 1.0)
            e.drain()
            e.affine_select(out=ident[:], in_=ident[:], compare_op=ALU.not_equal, fill=1.0, base=0,
                            pattern=[[-1, P]], channel_multiplier=1)
            e.affine_select(out=tri_le[:], in_=ones[:], compare_op=ALU.is_ge, fill=0.0, base=0,
                            pattern=[[1, P]], channel_multiplier=-1)
            e.affine_select(out=tri_ge[:], in_=ones[:], compare_op=ALU.is_ge, fill=0.0, base=0,
                            pattern=[[-1, P]], channel_multiplier=1)
            e.affine_select(out=tri_lt[:], in_=ones[:], compare_op=ALU.is_gt, fill=0.0, base=0,
                            pattern=[[1, P]], channel_multiplier=-1)
            e.affine_select(out=tri_gt[:], in_=ones[:], compare_op=ALU.is_gt, fill=0.0, base=0,
                            pattern=[[-1, P]], channel_multiplier=1)
            for kind in range(2):
                for q in (kind, kind + 2, 4):
                    v_ = fold[:, 16 * kind:16 * kind + 16]
                    e.affine_select(out=v_, in_=v_, compare_op=ALU.not_equal, fill=1.0, base=-16 * q,
                                    pattern=[[-1, 16]], channel_multiplier=1)
                    e.drain()
            for q in (1, 3):
                e.affine_select(out=sel_row[:], in_=sel_row[:], compare_op=ALU.not_equal, fill=0.0, base=-q,
                                pattern=[[0, P]], channel_multiplier=1)
                e.drain()
            e.affine_select(out=before[:], in_=before[:], compare_op=ALU.is_gt, fill=0.0, base=0,
                            pattern=[[1, NE], [-1, NE]], channel_multiplier=0)
            e.iota(slot_id[:], pattern=[[1, P]], base=0, channel_multiplier=0, allow_small_or_imprecise_dtypes=True)
            e.iota(expert_id[:], pattern=[[1, NE]], base=0, channel_multiplier=0, allow_small_or_imprecise_dtypes=True)
            for i in range(4):
                e.iota(inv_cnt[:, i, 0:NTOK], pattern=[[0, 4], [1, GRID_W]], base=0, channel_multiplier=0,
                       allow_small_or_imprecise_dtypes=True)
                e.iota(inv_cnt[:, i, NTOK:], pattern=[[1, NTOK]], base=0, channel_multiplier=0,
                       allow_small_or_imprecise_dtypes=True)
            e.drain().then_inc(consts_ready, 1)
            e.memset(padded[:], 0.0)
            e.memset(wing[:], 0.0)
            e.drain().then_inc(pads_zero, 1)

            def keep_rows(layer, p):
                n = layer * 3 + p
                e.wait_ge(mod_row, 4 * (n + 1))
                e.dma_start(scr[layer, p], mrow[:, n % 2, :]).then_inc(mod_saved, 16)
                e.wait_ge(mod_saved, 16 * (n + 1))
                e.dma_start(rb[0:64, layer, p, :], scr[layer, p].rearrange("q (i d) -> (q i) d", d=P)).then_inc(mod_back, 16)

            keep_rows(0, 0)
            e.wait_ge(pad_ready, 1)
            for g in (2, 3):
                pool_windows(e, g, wing)
                e.drain().then_inc(pool_g, 1)
                if g == 2:
                    keep_rows(0, 1)
            keep_rows(0, 2)
            for p in range(3):
                keep_rows(1, p)
            e.wait_ge(tn_ready, 2 * KD)
            e.wait_ge(ul_ready, 3 * KD)
            e.memset(cp[:], 0.0)
            e.memset(ysum[:], 0.0)
            e.drain().then_inc(pads2, 1)
            e.wait_ge(wdec_ready, 2)
            hv = lambda x: x.rearrange("p (h c) -> p h c", c=64)

            def spread(t, h0):
                return t[:, h0:h0 + HPG].unsqueeze(2).to_broadcast([P, HPG, 64])

            def y_squares(g):
                for c in range(2):
                    e.wait_ge(y_taken, 2 * g + c + 1)
                y2g = y2[:, 4 * g:4 * g + 4, :]
                for i in range(0, 4, 2):
                    e.drain()
                    e.tensor_tensor(ytmp[:].rearrange("p (c n) -> p c n", c=2), y2g[:, i:i + 2, :], y2g[:, i:i + 2, :], ALU.mult)
                    e.drain()
                    for j in range(2):
                        e.tensor_tensor(ysum[:], ysum[:], ytmp[:, j * NTOK:(j + 1) * NTOK], ALU.add)
                        e.drain()

            for g in range(NG):
                q = g % 2
                e.wait_ge(aux_taken, aux_no[("turn", g, 4)] + 1)
                for n, (tile, w) in enumerate(((2, 0), (3, 2), (2, 1), (3, 3), (0, 4), (1, 5))):
                    m = 6 * g + n
                    if n in (2, 3):
                        e.wait_ge(aux_mm, aux_no[("state", g, 0)] + 1)
                    elif n in (4, 5):
                        e.wait_ge(aux_mm, aux_no[("state", g, 1)] + 1)
                    elif g:
                        e.wait_ge(aux_mm, aux_no[("state", g - 1, 3)] + 1)
                    e.tensor_tensor(hv(xdd[m % 2][:]), hv(xs_tok[:, q, tile, :]), spread(wdec[:, w, :], HPG * g),
                                    ALU.mult).then_inc(xdd_ready, 1)
                if g:
                    e.wait_ge(y_mm, 4 * g)
                for d in range(2):
                    for c in range(2):
                        e.tensor_tensor(hv(xd[:, d, c, :]), hv(xs_tok[:, q, c, :]), spread(dt_tok[:, c, :], 32 * d + HPG * g),
                                        ALU.mult).then_inc(xd_ready, 1)
                if g:
                    y_squares(g - 1)
            y_squares(NG - 1)
            e.drain().then_inc(ysum_ready, 1)
            e.wait_ge(y_taken, 2 * NG)
            e.dma_start(mrow5[0:4, 0:2, :], scr[1, 1].rearrange("q (m d) -> q m d", m=2)).then_inc(rows_back, 16)
            e.dma_start(mrow5[0:4, 2:4, :], scr[1, 2].rearrange("q (m d) -> q m d", m=2)).then_inc(rows_back, 16)
            e.dma_start(mrow5[4:5, :, :], a["ada_b"][1:2, 2 * D:6 * D].rearrange("q (m d) -> q m d", m=4)).then_inc(rows_back, 16)
            e.dma_start(nfw[:], a["norm_ffn_w"][1:2, :].to_broadcast([P, D])).then_inc(rows_back, 16)
            e.dma_start(fnw[:], a["final_norm_w"].rearrange("(o d) -> o d", o=1).to_broadcast([P, D])).then_inc(rows_back, 16)
            e.dma_start(rw[:], a["moe_router_w"][0].rearrange("(k p) e -> p k e", p=P)).then_inc(rows_back, 16)

        @block.scalar
        def _(e):
            vec = [(a["norm_mix_w"][0], 0, 8), (a["norm_mix_w"][1], 8, 8), (a["norm_ffn_w"][0], 16, 8),
                   (a["pool_scale"][0], 24, 8), (a["ssd_norm_w"][0], 32, 16), (a["c"][0], 48, 8), (a["c_ctx"], 56, 8)]
            for src, r, n in vec:
                e.dma_start(rows_in[r:r + n, 0, :], src.rearrange("(r d) -> r d", d=P)).then_inc(loaded_vec, 16)
            e.dma_start(rows_in[0:96, 1, :], a["ssd_conv_w"][0].rearrange("t (r d) -> (t r) d", d=P)).then_inc(loaded_vec, 16)
            e.dma_start(rows_in[96:120, 1, :], a["ssd_conv_b"][0].rearrange("(r d) -> r d", d=P)).then_inc(loaded_vec, 16)
            for kind, src in enumerate((a["x"][0], a["ctx"][0])):
                for i in range(2):
                    e.dma_start(xtok[:, 2 * kind + i, :], src[i * P:(i + 1) * P, :]).then_inc(loaded_x, 16)
            for layer in range(2):
                e.dma_start(rb[64:80, layer, :, :], a["ada_b"][layer].rearrange("(p i d) -> i p d", i=16, d=P)).then_inc(loaded_bias, 16)
            e.dma_start(dpar[64:128, 0:1], a["ssd_dt_bias"][0].rearrange("d (h o) -> (d h) o", o=1)).then_inc(loaded_misc, 16)
            e.dma_start(dpar[64:128, 1:2], a["ssd_A_log"][0].rearrange("d (h o) -> (d h) o", o=1)).then_inc(loaded_misc, 16)
            for half in range(2):
                d_ = a["ssd_D"][0].rearrange("(c h) -> h c", h=2)[half:half + 1, :]
                e.dma_start(dcol[64 * half:64 * half + 64, :], d_.to_broadcast([64, 16]), allow_slow_non_contiguous=True).then_inc(loaded_misc, 16)
            e.wait_ge(vec_t, 1)
            e.activation(va[:], bank[7][:, 0:64], ACT.Copy)
            e.activation(vb[:], bank[7][:, 64:184], ACT.Copy).then_inc(vec_cols, 1)
            e.drain()
            e.activation(va[:, 48:64], va[:, 48:64], ACT.Silu)
            e.drain()
            e.wait_ge(cst_ready, 1)
            for kind in range(2):
                e.activation(cst[:, :, kind], va[:, 48 + 8 * kind:56 + 8 * kind], ACT.Copy).then_inc(vec_cols, 1)

            def rows_out(n):
                e.wait_ge(used, 2 * n + 2 if n < 12 else E0 + 2 * (n - 12) + 2)
                p = n // 4
                if p >= 2 and n % 4 == 0:
                    e.wait_ge(mod_saved, 16 * (p - 1))
                e.activation(mrow[:, p % 2, (n % 4) * 512:(n % 4 + 1) * 512], bank[n % 2][0:4, :], ACT.Copy).then_inc(mod_row, 1)

            def fold_cols(layer, p):
                e.wait_ge(fold_mm, layer * 3 + p + 1)
                e.activation(mc[layer][:, p].rearrange("p a b k -> p (a b k)"), bank[5][:, 0:32], ACT.Copy).then_inc(mc_ready, 1)

            def squares(k):
                e.activation(sq[:, :, k, :], ht[:, :, k, :], ACT.Square).then_inc(sq_ready, 1)

            def root(n):
                e.wait_ge(ms_ready, n + 1)
                e.activation(rstd[:], bank[4][:], ACT.Sqrt, bias=eps_col[:], scale=1.0 / D).then_inc(sd_ready, 1)

            split_hi(e, 0)
            for t in range(24):
                split_hi(e, t + 1)
                if t < KD:
                    e.wait_ge(x_t, t + 1)
                    if t == 0:
                        e.wait_ge(vec_t, 1)
                    e.activation(ht[:, :, t, :], two(bank[2 + t % 2][:]), ACT.Copy).then_inc(x_copied, 1)
                    e.drain()
                    squares(t)
                if t == KD:
                    root(0)
                if t % 2 == 1 and t >= 3:
                    rows_out(t // 2 - 1)
                if t == 13:
                    fold_cols(0, 0)
                if t == 21:
                    fold_cols(0, 1)
            rows_out(11)
            for g in range(4):
                if g < 2:
                    e.wait_ge(pool_v, g + 1)
                else:
                    e.wait_ge(pool_g, g - 1)
                for k in (2 * g, 2 * g + 1):
                    split_u_hi(e, k)
            fold_cols(0, 2)
            split_hi(e, FFN0)
            for k in range(KD):
                e.wait_ge(pool_added, 2 * (k + 1))
                squares(k)
            root(1)
            for k in range(KD):
                e.wait_ge(tn_ready, k + 1)
                split_u_hi(e, k)

            def ffn_acts(j, it, pick_silu):
                for c in range(2):
                    if pick_silu:
                        chunk_done(e, ffn_h1, w1_tile(j), j, c, it)
                        if j:
                            e.wait_ge(ffn_g, val(2 * (j - 1) + c + 1, 4, it))
                        e.activation(sg[:, c, :], bank[c][:], ACT.Silu).then_inc(ffn_silu, 1)
                    else:
                        e.wait_ge(ffn_g, val(2 * j + c + 1, 4, it))
                        e.activation(gh[:, j % 2, c, :], gf[:, c, :], ACT.Copy).then_inc(ffn_gh, 1)

            split_hi(e, FFN0 + 1)
            ffn_acts(0, None, True)
            split_hi(e, FFN0 + 2)
            ffn_acts(0, None, False)
            with e.Fori(0, FF_BLOCKS // 2) as it:
                for u in range(2):
                    j, k = 1 + u, FFN0 + 2 + 3 * u
                    split_hi(e, (k + 1, it))
                    split_hi(e, (k + 2, it))
                    ffn_acts(j, it, True)
                    split_hi(e, (k + 3, it))
                    ffn_acts(j, it, False)
            split_hi(e, E0)
            for t in range(24):
                split_hi(e, E0 + t + 1)
                if t == 0:
                    for k in range(KD):
                        e.wait_ge(ffn_added, KD * (FF_BLOCKS - 1) + k + 1)
                        squares(k)
                if t == 4:
                    root(2)
                if t % 2 == 1 and t >= 3:
                    rows_out(12 + t // 2 - 1)
                if t == 14:
                    fold_cols(1, 0)
                if t == 18:
                    for k in range(KD):
                        e.wait_ge(tn_ready, KD + k + 1)
                        split_u_hi(e, k)
                if t == 22:
                    fold_cols(1, 1)
            rows_out(23)
            split_hi(e, in_tile(0, 0))
            fold_cols(1, 2)
            R = slice(64, 128)
            e.wait_ge(loaded_misc, 64)
            e.wait_ge(used, IN0 + 1)
            e.activation(dts[R, 0, :], bank[0][R, :], ACT.Identity, bias=dpar[R, 0:1]).then_inc(in_taken, 1)
            e.activation(dpar[R, 2:3], dpar[R, 1:2], ACT.Exp).then_inc(dt_act, 1)
            e.wait_ge(dt_steps, 1)
            e.activation(dts[R, 1, :], dts[R, 1, :], ACT.Exp, scale=-1.0).then_inc(dt_act, 1)
            e.wait_ge(dt_steps, 2)
            e.activation(dts[R, 3, :], dts[R, 2, :], ACT.Ln).then_inc(dt_act, 1)

            def take_aux(key):
                n = aux_no[key]
                what, g, i = key
                b = bank[2 + n % 2]
                e.wait_ge(aux_mm, n + 1)
                if what == "dt":
                    e.activation(dt_tok[:].rearrange("p t h -> p (t h)"), b[:, 0:256], ACT.Copy)
                    ins = e.activation(a_tok[:].rearrange("p t h -> p (t h)"), b[:, 256:512], ACT.Copy)
                elif what == "decay":
                    e.activation(wdec[:].rearrange("p t h -> p (t h)"), b[:, 0:256], ACT.Exp)
                    ins = e.activation(acs[:].rearrange("p t h -> p (t h)"), b[:, 256:384], ACT.Copy)
                elif what == "turn":
                    o = b_tok[:, g % 2] if i == 0 else xs_tok[:, g % 2, :, (i - 1) * P:i * P]
                    ins = e.activation(o, b[:].rearrange("p (t n) -> p t n", t=4), ACT.Copy)
                elif what == "cb":
                    ins = e.activation(cb[:, 0].rearrange("p c n -> p (c n)"), b[:, 0:256], ACT.Copy)
                elif what == "state":
                    ins = e.activation(states[:, i, :], b[:], ACT.Copy)
                elif what == "resid":
                    ins = e.activation(hl[:, i // 2, (i % 2) * 512:(i % 2 + 1) * 512], b[:], ACT.Copy)
                elif what == "mods":
                    ins = e.activation(mods[:, i // 2, (i % 2) * 512:(i % 2 + 1) * 512], b[:], ACT.Copy)
                elif what == "v":
                    ins = e.activation(vt[:, 4 * (i % 2):4 * (i % 2) + 4, (i // 2) * P:(i // 2 + 1) * P],
                                       b[:].rearrange("p (k n) -> p k n", k=4), ACT.Copy)
                ins.then_inc(aux_taken, 1)

            def take_in(g, j):
                for c in range(2):
                    if c == 0:
                        e.wait_ge(in_mm, 5 * g + j + 1)
                    else:
                        e.wait_ge(used, in_tile(g, j) + 1)
                    b = bank[in_chunk(g, j, c) % 2]
                    if j < 3:
                        v_ = 6 * g + 2 * j + c
                        if v_ >= 2:
                            e.wait_ge(conv_acc, v_ - 1)
                        n = 1 if (j, c) == (0, 1) else 2
                        e.activation(cp[:, v_ % 2, 0:n, 2:258], two(b[:])[:, 0:n, :], ACT.Copy).then_inc(in_taken, 1)
                    else:
                        e.activation(sz[:, g % 2, 2 * (j - 3) + c, :], b[:, 0:NTOK], ACT.Silu).then_inc(in_taken, 1)

            def conv_silu(g, j):
                q = g % 2
                for c in range(2):
                    v_ = 6 * g + 2 * j + c
                    e.wait_ge(conv_acc, v_ + 1)
                    o = (bt[:, q, :], ct[:, q, :])[c] if j == 0 else xst[:, q, 2 * (j - 1) + c, :]
                    ins = e.activation(o, cacc[:, v_ % 2, 0:NTOK], ACT.Silu)
                    if (j, c) != (0, 1):
                        ins = e.activation(ccv[:, c, :], cacc[:, v_ % 2, NTOK:], ACT.Silu)
                    ins.then_inc(conv_out, 1)

            def exps(g, u):
                n = 4 * g + u
                for d in range(2):
                    e.wait_ge(seg_ready, 2 * n + d + 1)
                    e.activation(seg[:, d, :], seg[:, d, :], ACT.Exp)
                    e.activation(csc[:, d, :], bank[4 + d][:], ACT.Exp).then_inc(exp_ready, 1)

            def y_hi(k0, k1):
                for k in range(k0, k1):
                    e.activation(yh[:, k, :], y2[:, k, :], ACT.Identity, scale=va[:, 32 + k:33 + k]).then_inc(yh_ready, 1)

            take_aux(("dt", 0, 0))
            e.wait_ge(pads2, 1)
            for g in range(NG + 1):
                for j in range(5):
                    if g < NG:
                        split_hi(e, in_tile(g, j) + 1)
                    elif j == 0:
                        split_hi(e, OUT0 + 1)
                    pg, pj = (g, j - 1) if j else (g - 1, 4)
                    if pg >= 0:
                        if pg < NG:
                            take_in(pg, pj)
                        if pj == 0:
                            for key in aux:
                                if key[0] in ("cb", "state") and key[1] == pg - 1:
                                    take_aux(key)
                        elif pj in (2, 3, 4) and pg < NG:
                            for i in {2: (0,), 3: (1, 2), 4: (3, 4)}[pj]:
                                take_aux(("turn", pg, i))
                        if pg >= 1 and pj < 4:
                            exps(pg - 1, pj)
                    if g < NG and j in (2, 3, 4):
                        conv_silu(g, j - 2)
                    if (g, j) == (0, 0):
                        take_aux(("decay", 0, 0))
                        e.drain().then_inc(wdec_ready, 1)
                    if g == NG and j in (1, 2, 3):
                        e.wait_ge(y_taken, 2 * j)
                        y_hi(4 * (j - 1), 4 * j)
            e.wait_ge(y_taken, 2 * NG)
            y_hi(12, 16)
            for n in range(4):
                take_aux(("resid", 0, n))
            e.drain().then_inc(hl_ready, 1)
            for t in range(2, 5):
                split_hi(e, OUT0 + t)
            e.wait_ge(rt_mm, 1)
            e.activation(ry[:, 0:2], bank[6][:, 0:2], ACT.Sqrt, bias=eps_col[:], scale=1.0 / DI).then_inc(ry_root, 1)
            for t in range(5, 8):
                split_hi(e, OUT0 + t)
            for n in range(8):
                take_aux(("mods", 0, n))
            e.drain().then_inc(mods_ready, 1)
            e.wait_ge(h_ready, 1)
            for t in range(2):
                e.activation(sq2[:], hl[:, t, :], ACT.Square, accum_out=stat[:, t:t + 1])
                e.drain()
            e.activation(stat[:, 2:4], stat[:, 0:2], ACT.Sqrt, bias=eps_col[:], scale=1.0 / D).then_inc(hsq_ready, 1)
            for n in range(4):
                take_aux(("v", 0, n))
            e.wait_ge(rt_dve, 1)
            for t in range(2):
                e.activation(gate[:, t, :], lg[:, t, :], ACT.Exp, bias=rsc[:, t:t + 1])
            e.drain().then_inc(rt_act, 1)

            def hi_of(k, i, b=None):
                if b is None:
                    e.wait_ge(landed2[k % RAW2], i * (16 * EB) + 16 * (k // RAW2 + 1) if i is not None else 16)
                else:
                    e.wait_ge(landed2[k % RAW2], i * (16 * EB) + b * 16 + 16 * (k // RAW2 + 1))
                e.wait_ge(used2, val2(k + 1, i, b, 6))
                e.activation(whi2[:, k % SPL2, :], raw2[:, k % RAW2, :], ACT.Copy).then_inc(hi2, 1)

            def silu_of(i, blk, b=None):
                e.activation(sge[:], bank[0][:], ACT.Silu).then_inc(silu2, 1)

            def gth_of(i, blk, b=None):
                e.wait_ge(turn_mm, val3(blk + 1, i, b))
                e.activation(gth[:].rearrange("p f n -> p (f n)"), bank[2][:], ACT.Copy).then_inc(gth_ready, 1)

            def xgh_of(n):
                e.wait_ge(gather_mm, n)
                for h in range(2):
                    ins = e.activation(xgh[:, 4 * h:4 * h + 4, :].rearrange("p k n -> p (k n)"), bank[5 + h][:], ACT.Copy)
                ins.then_inc(xgh_ready, 1)

            def block(i, k, blk, b=None):
                hi_of(k + 2, i, b)
                gth_of(i, blk - 1, b)
                hi_of(k + 3, i, b)
                hi_of(k + 4, i, b)
                silu_of(i, blk, b)
                for n in range(5, 8):
                    hi_of(k + n, i, b)

            hi_of(0, None)
            hi_of(1, None)
            xgh_of(1)
            e.wait_ge(tab_ready, 1)
            count = e.value_load(itab[0:1, 12:13], min_val=NE, max_val=MAX_ITEMS)
            with e.Fori(0, count) as i:
                hi_of(2, i)
                hi_of(3, i)
                hi_of(4, i)
                silu_of(i, 0)
                hi_of(5, i)
                e.wait_ge(put_mm, i + 1)
                e.activation(put[:].rearrange("p t n -> p (t n)"), bank[7][:, 0:256], ACT.Copy).then_inc(put_ready, 1)
                block(i, 4, 1)
                with e.Fori(0, EB - 2) as b:
                    block(i, 10, 2, b)
                hi_of(TPI, i)
                gth_of(i, EB - 1)
                xgh_of(i + 2)
                hi_of(TPI + 1, i)
                e.wait_ge(used2, i * TPI + (TPI + SPL2))
                for n in range(2):
                    ins = e.activation(osb[:, n * 512:(n + 1) * 512], bank[3 + n][:], ACT.Copy)
                ins.then_inc(osb_ready, 1)
            e.wait_ge(out_sq, 1)
            for t in range(2):
                e.activation(v[:, t, :], hl[:, t, :], ACT.Square, accum_out=stat[:, 8 + t:9 + t])
            e.drain()
            e.activation(stat[:, 10:12], stat[:, 8:10], ACT.Sqrt, bias=eps_col[:], scale=1.0 / D).then_inc(out_sq, 1)

        @block.vector
        def _(e):
            e.memset(cst[:].bitcast(F32), 0.0).then_inc(cst_ready, 1)
            e.memset(win[:], 0.0)
            e.wait_ge(consts_ready, 1)
            for i, w in enumerate(WINDOWS):
                for L, s in ((GRID_W, slice(0, NTOK)), (NTOK, slice(NTOK, NT2))):
                    e.tensor_scalar(rstd[:, s], inv_cnt[:, i, s], float(-(w // 2)), 0.0, ALU.add, ALU.max)
                e.drain()
                for L, s in ((GRID_W, slice(0, NTOK)), (NTOK, slice(NTOK, NT2))):
                    e.tensor_scalar(inv_cnt[:, i, s], inv_cnt[:, i, s], float(w - w // 2), float(L), ALU.add, ALU.min)
                e.drain()
                e.tensor_tensor(inv_cnt[:, i, :], inv_cnt[:, i, :], rstd[:], ALU.subtract)
                e.drain()
                e.reciprocal(inv_cnt[:, i, :], inv_cnt[:, i, :])
                e.drain()
            e.wait_ge(vec_cols, 3)
            for kind in range(2):
                e.tensor_tensor(cst[:, :, 2 + kind], va[:, 48 + 8 * kind:56 + 8 * kind],
                                cst[:, :, kind].bitcast(F32), ALU.subtract).then_inc(cst_ready, 1)

            def scales(i, layer, src_pair, src_one, w0, plus_one):
                for kind in range(2):
                    e.scalar_tensor_tensor(out=aff[:, i, kind, :], in0=mc[layer][:, src_pair, kind, src_one, :],
                                           scalar=1.0 if plus_one else 0.0, in1=va[:, w0:w0 + KD], op0=ALU.add, op1=ALU.mult)

            def normalise(n):
                e.wait_ge(sd_ready, n + 1)
                e.reciprocal(rstd[:], rstd[:])
                e.drain()
                for k in range(KD):
                    e.tensor_tensor(tn[:, :, k, :], ht[:, :, k, :], two(rstd[:]), ALU.mult)
                e.drain()

            def modulated(i, layer, pair, one, write):
                for k in range(KD):
                    for kind in range(2):
                        ins = write(k, kind, aff[:, i, kind, k:k + 1], mc[layer][:, pair, kind, one, k:k + 1])
                return ins

            def into_padded(k, kind, s, b):
                if kind == 0:
                    c0 = 8 + 4 * (GRID_W + 8)
                    o = padded[:, k, 8:c0].rearrange("p (r w) -> p r w", w=GRID_W + 8)[:, :, 0:GRID_W]
                    i_ = tn[:, 0, k, :].rearrange("p (r w) -> p r w", w=GRID_W)
                else:
                    o, i_ = padded[:, k, 8 + 4 * (GRID_W + 8):PADW - 8], tn[:, 1, k, :]
                return e.tensor_scalar(o, i_, s, b, ALU.mult, ALU.add)

            def in_place(k, kind, s, b):
                ins = e.tensor_scalar(tn[:, kind, k, :], tn[:, kind, k, :], s, b, ALU.mult, ALU.add)
                if kind == 1:
                    ins.then_inc(tn_ready, 1)
                return ins

            split_lo(e, 0)
            for t in range(24):
                split_lo(e, t + 1)
                if t == 9:
                    normalise(0)
                if t == 13:
                    e.wait_ge(mc_ready, 1)
                    scales(0, 0, 0, 1, 0, True)
                    e.drain()
                    e.wait_ge(pads_zero, 1)
                    modulated(0, 0, 0, 0, into_padded).then_inc(pad_ready, 1)
                    e.drain()
                if t in (15, 17):
                    g = (t - 15) // 2
                    pool_windows(e, g, win)
                    e.drain().then_inc(pool_v, 1)
            for k in range(KD):
                if k == 4:
                    e.wait_ge(pool_g, 1)
                if k == 6:
                    e.wait_ge(pool_g, 2)
                split_u_lo(e, k, 0)
            e.wait_ge(mc_ready, 3)
            scales(1, 0, 1, 0, 24, False)
            scales(2, 0, 2, 0, 16, True)
            e.drain()
            for k in range(KD):
                if k < KD - 1:
                    e.wait_ge(pool_mm, k + 1)
                else:
                    e.wait_ge(used, POOL0 + 1)
                for kind in range(2):
                    e.scalar_tensor_tensor(out=ht[:, kind, k, :], in0=bank[k][:, kind * NTOK:(kind + 1) * NTOK],
                                           scalar=aff[:, 1, kind, k:k + 1], in1=ht[:, kind, k, :],
                                           op0=ALU.mult, op1=ALU.add).then_inc(pool_added, 1)
            e.drain()
            split_lo(e, FFN0)
            normalise(1)
            modulated(2, 0, 1, 1, in_place)
            for k in range(KD):
                split_u_lo(e, k, KD)

            def ffn_g_of(j, it):
                for c in range(2):
                    chunk_done(e, ffn_h3, w1_tile(j) + 1, j, c, it)
                    e.wait_ge(ffn_silu, val(2 * j + c + 1, 4, it))
                    if j:
                        e.wait_ge(ffn_gh, val(2 * (j - 1) + c + 1, 4, it))
                    e.tensor_tensor(gf[:, c, :], sg[:, c, :], bank[2 + c][:], ALU.mult).then_inc(ffn_g, 1)

            def ffn_lo(j, it):
                for c in range(2):
                    e.wait_ge(ffn_gh, val(2 * j + c + 1, 4, it))
                    e.tensor_tensor(gl[:, j % 2, c, :], gf[:, c, :], gh[:, j % 2, c, :].bitcast(F32),
                                    ALU.subtract).then_inc(ffn_gl, 1)

            def ffn_add(j, it, ks):
                for k in ks:
                    if k < KD - 1:
                        e.wait_ge(ffn_out, val(7 * j + k + 1, 14, it))
                    else:
                        e.wait_ge(used, val(w2_tile(j) + 1, 6, it))
                    for kind in range(2):
                        ins = e.scalar_tensor_tensor(out=ht[:, kind, k, :], in0=bank[4 + k % 4][:, kind * NTOK:(kind + 1) * NTOK],
                                                     scalar=mc[0][:, 2, kind, 1, k:k + 1], in1=ht[:, kind, k, :],
                                                     op0=ALU.mult, op1=ALU.add)
                    ins.then_inc(ffn_added, 1)

            split_lo(e, FFN0 + 1)
            split_lo(e, FFN0 + 2)
            ffn_g_of(0, None)
            e.drain()
            ffn_lo(0, None)
            with e.Fori(0, FF_BLOCKS // 2) as it:
                for u in range(2):
                    j, k = 1 + u, FFN0 + 2 + 3 * u
                    split_lo(e, (k + 1, it))
                    split_lo(e, (k + 2, it))
                    e.drain()
                    split_lo(e, (k + 3, it))
                    ffn_g_of(j, it)
                    ffn_add(j - 1, it, range(4))
                    e.drain()
                    ffn_lo(j, it)
                    ffn_add(j - 1, it, range(4, 8))
            e.drain()
            split_lo(e, E0)
            ffn_add(FF_BLOCKS - 1, None, range(8))
            for t in range(24):
                split_lo(e, E0 + t + 1)
                if t == 5:
                    e.drain()
                    normalise(2)
                if t == 16:
                    e.wait_ge(mc_ready, 4)
                    scales(3, 1, 0, 1, 8, True)
                    e.drain()
                    modulated(3, 1, 0, 0, in_place)
                if t == 19:
                    for k in range(KD):
                        split_u_lo(e, k, 2 * KD)
            split_lo(e, in_tile(0, 0))
            R = slice(64, 128)
            e.wait_ge(dt_act, 1)
            e.wait_ge(in_taken, 1)
            e.scalar_tensor_tensor(out=dts[R, 1, :], in0=dts[R, 0, :], scalar=-1.0, in1=dts[R, 0, :], op0=ALU.mult, op1=ALU.max).then_inc(dt_steps, 1)
            e.wait_ge(dt_act, 2)
            e.tensor_scalar(dts[R, 2, :], dts[R, 1, :], 1.0, None, ALU.add).then_inc(dt_steps, 1)
            e.wait_ge(dt_act, 3)
            e.tensor_scalar(dts[R, 2, :], dts[R, 2, :], -1.0, None, ALU.add)
            e.drain()
            e.tensor_scalar(dts[R, 4, :], dts[R, 2, :], 0.0, None, ALU.is_equal)
            e.drain()
            e.tensor_tensor(dts[R, 2, :], dts[R, 2, :], dts[R, 4, :], ALU.add)
            e.tensor_tensor(dts[R, 3, :], dts[R, 3, :], dts[R, 4, :], ALU.add)
            e.drain()
            e.reciprocal(dts[R, 2, :], dts[R, 2, :])
            e.drain()
            e.tensor_tensor(dts[R, 3, :], dts[R, 3, :], dts[R, 2, :], ALU.mult)
            e.drain()
            e.tensor_tensor(dts[R, 3, :], dts[R, 3, :], dts[R, 1, :], ALU.mult)
            e.drain()
            e.scalar_tensor_tensor(out=dts[R, 0, :], in0=dts[R, 0, :], scalar=0.0, in1=dts[R, 3, :], op0=ALU.max, op1=ALU.add)
            e.drain()
            e.tensor_scalar(dts[R, 1, :], dts[R, 0, :], dpar[R, 2:3], -1.0, ALU.mult, ALU.mult)
            e.drain().then_inc(a_ready, 1)

            def conv(g, j):
                for c in range(2):
                    v_ = 6 * g + 2 * j + c
                    ch = 16 + 4 * c + g if j == 0 else 4 * g + 2 * (j - 1) + c
                    n = 1 if (j, c) == (0, 1) else 2
                    e.wait_ge(in_taken, in_chunk(g, j, c) + 1)
                    if v_ >= 2:
                        e.wait_ge(conv_out, v_ - 1)
                    src = lambda k: cp[:, v_ % 2, 0:n, k:k + NTOK]
                    o = two(cacc[:, v_ % 2, :])[:, 0:n, :]
                    e.tensor_scalar(o, src(0), vb[:, ch:ch + 1], vb[:, 96 + ch:97 + ch], ALU.mult, ALU.add)
                    for k in range(1, 4):
                        e.drain()
                        ins = e.scalar_tensor_tensor(out=o, in0=src(k), scalar=vb[:, 24 * k + ch:24 * k + ch + 1], in1=o,
                                                     op0=ALU.mult, op1=ALU.add)
                    ins.then_inc(conv_acc, 1)

            def segs(g, u):
                c, q4 = u // 2, u % 2
                n = 4 * g + u
                for d in range(2):
                    e.wait_ge(bc_mm, 2 * n + d + 1)
                    for h in range(4):
                        hh = HPG * g + 4 * q4 + h
                        ins = e.tensor_scalar(seg[:, d, h * P:(h + 1) * P], bank[4 + d][:, h * P:(h + 1) * P],
                                              acs[:, 2 * d + c, hh:hh + 1], 0.0, ALU.subtract, ALU.min)
                    ins.then_inc(seg_ready, 1)

            def mixes(g, u):
                c = u // 2
                n = 4 * g + u
                f4 = lambda x: x.rearrange("p (h n) -> p h n", h=4)
                for d in range(2):
                    e.wait_ge(exp_ready, 2 * n + d + 1)
                    e.tensor_tensor(f4(seg[:, d, :]), f4(seg[:, d, :]), cb[:, d, c, :].unsqueeze(1).to_broadcast([P, 4, P]), ALU.mult)
                    e.tensor_tensor(f4(csc[:, d, :]), f4(csc[:, d, :]),
                                    ct[:, g % 2, c * P:(c + 1) * P].unsqueeze(1).to_broadcast([P, 4, P]), ALU.mult)
                e.drain().then_inc(mix_ready, 1)

            def masks(g):
                e.wait_ge(aux_taken, aux_no[("cb", g, 0)] + 1)
                for c in range(2):
                    e.tensor_tensor(cb[:, 1, c, :], cb[:, 0, c, :], tri_ge[:], ALU.mult)
                e.drain()
                for c in range(2):
                    e.tensor_tensor(cb[:, 0, c, :], cb[:, 0, c, :], tri_le[:], ALU.mult)
                e.wait_ge(aux_taken, aux_no[("state", g, 3)] + 1)
                hv = lambda x: x.rearrange("p (h c) -> p h c", c=64)
                for d in range(2):
                    e.tensor_tensor(hv(csc[:, d, :]), hv(states[:, d, :]),
                                    wdec[:, 6 + d, HPG * g:HPG * g + HPG].unsqueeze(2).to_broadcast([P, HPG, 64]), ALU.mult)
                e.drain()
                for d in range(2):
                    e.tensor_tensor(states[:, 2 + d, :], states[:, 2 + d, :], csc[:, d, :], ALU.add)
                e.drain().then_inc(st_ready, 1)

            def y_out(g, c):
                e.wait_ge(y_mm, 4 * g + 2 * c + 2)
                q = g % 2
                for i in range(4):
                    k = 4 * g + i
                    e.scalar_tensor_tensor(out=y2[:, k, c * P:(c + 1) * P], in0=xst[:, q, i, c * P:(c + 1) * P], scalar=dcol[:, k:k + 1],
                                           in1=bank[6 + c][:, i * P:(i + 1) * P], op0=ALU.mult, op1=ALU.add)
                e.drain()
                o = y2[:, 4 * g:4 * g + 4, c * P:(c + 1) * P]
                e.tensor_tensor(o, o, sz[:, q, :, c * P:(c + 1) * P], ALU.mult).then_inc(y_taken, 1)

            def y_lo(k0, k1):
                for k in range(k0, k1):
                    e.wait_ge(yh_ready, k + 1)
                    e.scalar_tensor_tensor(out=yl[:, k, :], in0=y2[:, k, :], scalar=va[:, 32 + k:33 + k], in1=yh[:, k, :].bitcast(F32),
                                           op0=ALU.mult, op1=ALU.subtract).then_inc(yl_ready, 1)

            e.wait_ge(pads2, 1)
            for g in range(NG + 1):
                for j in range(5):
                    if g < NG:
                        split_lo(e, in_tile(g, j) + 1)
                    elif j == 0:
                        split_lo(e, OUT0 + 1)
                    pg, pj = (g, j - 1) if j else (g - 1, 4)
                    if (g, j) == (0, 0):
                        e.wait_ge(wdec_ready, 1)
                        for n, (tile, d) in enumerate(((2, 0), (2, 1), (3, 0), (3, 1), (0, 0), (1, 1))):
                            e.tensor_tensor(wdec[:, n, :], wdec[:, n, :], dt_tok[:, tile, 32 * d:32 * d + 32], ALU.mult)
                        e.drain().then_inc(wdec_ready, 1)
                    if pg >= 1 and pj == 0:
                        masks(pg - 1)
                    if pg >= 1 and pj < 4:
                        segs(pg - 1, pj)
                    if pg < NG and 0 <= pj < 3 and pg >= 0:
                        conv(pg, pj)
                    if pg >= 1 and pj < 4:
                        mixes(pg - 1, pj)
                    if pg >= 1 and pj in (2, 4):
                        y_out(pg - 1, pj // 2 - 1)
                    if g == NG and j in (1, 2, 3):
                        y_lo(4 * (j - 1), 4 * j)
            e.drain()
            y_out(NG - 1, 1)
            y_lo(12, 16)
            for t in range(2, 8):
                if t == 5:
                    e.wait_ge(ry_root, 1)
                    e.reciprocal(ry[:, 2:4], ry[:, 0:2])
                split_lo(e, OUT0 + t)
            e.drain().then_inc(lo2, 3)
            e.wait_ge(mods_ready, 1)
            e.wait_ge(hl_ready, 1)
            e.wait_ge(rows_back, 6 * 16)
            e.scalar_tensor_tensor(out=mods[:, 2, :], in0=mods[:, 2, :], scalar=1.0, in1=nfw[:], op0=ALU.add, op1=ALU.mult)
            for n in range(2):
                e.wait_ge(used, OUT0 + 4 * n + 4)
                for t in range(2):
                    s = slice(n * 512, (n + 1) * 512)
                    e.scalar_tensor_tensor(out=v[:, t, s], in0=bank[4 * n + t][:], scalar=ry[:, 2 + t:3 + t], in1=mods[:, 0, s],
                                           op0=ALU.mult, op1=ALU.mult)
                    e.drain()
                    e.tensor_tensor(hl[:, t, s], hl[:, t, s], v[:, t, s], ALU.add)
            e.drain().then_inc(h_ready, 1)
            e.wait_ge(hsq_ready, 1)
            e.reciprocal(stat[:, 4:6], stat[:, 2:4])
            e.drain()
            for t in range(2):
                e.scalar_tensor_tensor(out=v[:, t, :], in0=hl[:, t, :], scalar=stat[:, 4 + t:5 + t], in1=mods[:, 2, :],
                                       op0=ALU.mult, op1=ALU.mult)
                e.drain()
                e.tensor_tensor(v[:, t, :], v[:, t, :], mods[:, 1, :], ALU.add)
            e.drain().then_inc(v_ready, 1)
            e.memset(acc[:], 0.0)
            e.wait_ge(lg_mm, 1)
            e.tensor_copy(lg[:].rearrange("p t x -> p (t x)"), bank[6][:, 16:32])
            e.drain()
            for t in range(2):
                own = lg[:, t, :].unsqueeze(2).to_broadcast([P, NE, NE])
                other = lg[:, t, :].unsqueeze(1).to_broadcast([P, NE, NE])
                e.tensor_tensor(cmp[:, t], other, own, ALU.is_gt)
                e.tensor_tensor(eqs[:, t], other, own, ALU.is_equal)
                e.drain()
                e.tensor_tensor(eqs[:, t], eqs[:, t], before[:], ALU.mult)
                e.drain()
                e.tensor_tensor(cmp[:, t], cmp[:, t], eqs[:, t], ALU.add)
                e.drain()
                e.tensor_reduce(sel[:, t, :], cmp[:, t], AX_X, ALU.add)
                e.tensor_reduce(rsc[:, 2 + t:3 + t], lg[:, t, :], AX_X, ALU.max)
                e.drain()
                e.tensor_scalar(sel[:, t, :], sel[:, t, :], 1.5, None, ALU.is_lt)
                e.tensor_scalar(rsc[:, t:t + 1], rsc[:, 2 + t:3 + t], -1.0, None, ALU.mult)
            e.drain().then_inc(rt_dve, 1)
            e.wait_ge(rt_act, 1)
            for t in range(2):
                e.tensor_tensor(gate[:, t, :], gate[:, t, :], sel[:, t, :], ALU.mult)
                e.drain()
                e.tensor_reduce(rsc[:, 4 + t:5 + t], gate[:, t, :], AX_X, ALU.add)
                e.drain()
                e.reciprocal(rsc[:, 6 + t:7 + t], rsc[:, 4 + t:5 + t])
                e.drain()
                e.tensor_scalar(gate[:, t, :], gate[:, t, :], rsc[:, 6 + t:7 + t], None, ALU.mult)
            e.wait_ge(rt_mm, 2)
            for t in range(2):
                e.scalar_tensor_tensor(out=pos[:, t, :], in0=bank[6][:, 32 + 8 * t:40 + 8 * t], scalar=1.0, in1=sel[:, t, :],
                                       op0=ALU.add, op1=ALU.mult)
            e.tensor_copy(cnt[:], bank[6][:, 48:56])
            e.drain()
            e.tensor_scalar(over[:], cnt[:], float(P), None, ALU.is_gt)
            e.memset(pos_item[:], -1.0)
            e.memset(gate_item[:], 0.0)
            e.memset(ftab[:], 0.0)
            e.drain()
            e.tensor_tensor(cmp[:, 0], over[:].unsqueeze(1).to_broadcast([P, NE, NE]), before[:], ALU.mult)
            e.tensor_reduce(rsc[:, 8:9], over[:], AX_X, ALU.add)
            e.drain()
            e.tensor_reduce(rsc[:, 12:13], over[:], AX_X, ALU.add)
            e.tensor_reduce(cnt[:], cmp[:, 0], AX_X, ALU.add)
            e.drain()
            for m in range(3):
                e.scalar_tensor_tensor(out=more[:, m, :], in0=cnt[:], scalar=float(m), in1=over[:], op0=ALU.is_equal, op1=ALU.mult)
            e.drain()
            bc3 = lambda x: x.unsqueeze(1).to_broadcast([P, 3, NE])
            e.tensor_tensor(tmp3[:], more[:], bc3(expert_id[:]), ALU.mult)
            e.drain()
            e.tensor_copy(ftab[:, 0:NE], expert_id[:])
            e.tensor_reduce(ftab[:, NE:NE + 3], tmp3[:], AX_X, ALU.add)
            e.tensor_scalar(ftab[:, 12:13], rsc[:, 8:9], float(NE), None, ALU.add)
            e.drain()
            e.tensor_copy(itab[:], ftab[0:1, :])
            e.drain().then_inc(tab_ready, 1)
            for t in range(2):
                e.tensor_scalar(pos_item[:, t, 0:NE], pos[:, t, :], -1.0, None, ALU.add)
                e.tensor_copy(gate_item[:, t, 0:NE], gate[:, t, :])
                e.scalar_tensor_tensor(out=tmp3[:], in0=bc3(pos[:, t, :]), scalar=-float(P), in1=more[:], op0=ALU.add, op1=ALU.mult)
                e.drain()
                e.tensor_reduce(pos_item[:, t, NE:NE + 3], tmp3[:], AX_X, ALU.add)
                e.drain()
                e.tensor_scalar(pos_item[:, t, NE:NE + 3], pos_item[:, t, NE:NE + 3], -1.0, None, ALU.add)
                e.tensor_tensor(tmp3[:], bc3(gate[:, t, :]), more[:], ALU.mult)
                e.drain()
                e.tensor_reduce(gate_item[:, t, NE:NE + 3], tmp3[:], AX_X, ALU.add)
                e.drain()

            def pick_of(col):
                for t in range(2):
                    e.tensor_scalar(pick[:, t, :], slot_id[:], pos_item[:, t, col], None, ALU.is_equal)
                    e.tensor_scalar(pickg[:, t, :], slot_id[:], pos_item[:, t, col], gate_item[:, t, col], ALU.is_equal, ALU.mult)

            pick_of(slice(0, 1))
            e.drain().then_inc(pick_ready, 1)
            e.wait_ge(used, NTILES)
            e.drain().then_inc(lo2, 3)
            e.drain().then_inc(acc_added, 1)

            def lo_of(k, i, b=None):
                e.wait_ge(hi2, val2(k + 1, i, b, 6))
                e.tensor_tensor(wlo2[:, k % SPL2, :], raw2[:, k % RAW2, :], whi2[:, k % SPL2, :].bitcast(F32),
                                ALU.subtract).then_inc(lo2, 1)

            def gm_of(i, blk, b=None):
                e.wait_ge(silu2, val3(blk + 1, i, b))
                e.tensor_tensor(gme[:], sge[:], bank[1][:], ALU.mult).then_inc(gm_ready, 1)

            def gtl_of(i, blk, b=None):
                e.wait_ge(gth_ready, val3(blk + 1, i, b))
                e.tensor_tensor(gtl[:].rearrange("p f n -> p (f n)"), bank[2][:], gth[:].bitcast(F32).rearrange("p f n -> p (f n)"),
                                ALU.subtract).then_inc(gtl_ready, 1)

            def xgl_of(n):
                e.wait_ge(xgh_ready, n)
                for h in range(2):
                    ins = e.tensor_tensor(xgl[:, 4 * h:4 * h + 4, :].rearrange("p k n -> p (k n)"), bank[5 + h][:],
                                          xgh[:, 4 * h:4 * h + 4, :].bitcast(F32).rearrange("p k n -> p (k n)"), ALU.subtract)
                ins.then_inc(xgl_ready, 1)

            def block(i, k, blk, b=None):
                lo_of(k + 2, i, b)
                gtl_of(i, blk - 1, b)
                for n in range(3, 7):
                    lo_of(k + n, i, b)
                gm_of(i, blk, b)
                lo_of(k + 7, i, b)

            lo_of(0, None)
            lo_of(1, None)
            xgl_of(1)
            count = e.value_load(itab[0:1, 12:13], min_val=NE, max_val=MAX_ITEMS)
            with e.Fori(0, count) as i:
                for k in (2, 3, 4, 5):
                    lo_of(k, i)
                e.wait_ge(used2, i * TPI + (4 + SPL2))
                gm_of(i, 0)
                block(i, 4, 1)
                e.wait_ge(put_ready, i + 1)
                pick_of(bass.ds(i + 1, 1))
                e.drain().then_inc(pick_ready, 1)
                with e.Fori(0, EB - 2) as b:
                    block(i, 10, 2, b)
                lo_of(TPI, i)
                gtl_of(i, EB - 1)
                xgl_of(i + 2)
                lo_of(TPI + 1, i)
                for n, bk in enumerate((7, 2, 3, 4)):
                    t, h = n // 2, n % 2
                    e.wait_ge(scat_mm, i * 4 + (n + 1))
                    o = acc[:, t, h * 512:(h + 1) * 512]
                    e.tensor_tensor(o, o, bank[bk][:], ALU.add).then_inc(acc_added, 1)
                e.drain()
            for t in range(2):
                e.tensor_tensor(acc[:, t, :], acc[:, t, :], mods[:, 3, :], ALU.mult)
                e.drain()
                e.tensor_tensor(hl[:, t, :], hl[:, t, :], acc[:, t, :], ALU.add)
            e.drain().then_inc(out_sq, 1)
            e.wait_ge(out_sq, 2)
            e.reciprocal(stat[:, 12:14], stat[:, 10:12])
            e.drain()
            for t in range(2):
                e.scalar_tensor_tensor(out=acc[:, t, :], in0=hl[:, t, :], scalar=stat[:, 12 + t:13 + t], in1=fnw[:],
                                       op0=ALU.mult, op1=ALU.mult).then_inc(out_ready, 1)

        @block.tensor
        def _(e):
            def passes(o, wsl, usl, first, last):
                ins = None
                for n, (i, j) in enumerate(((0, 0), (0, 1), (1, 0))):
                    ins = e.matmul(o, wsl[i], usl[j], start=first and n == 0, stop=last and n == 2)
                return ins

            def wpart(s, view):
                return view(whi[:, s, :]), view(wlo[:, s, :])

            e.wait_ge(loaded_vec, 9 * 16)
            e.wait_ge(consts_ready, 1)
            e.transpose(bank[7][:, 0:64], rows_in[0:64, 0, :], ident[0:64, 0:64])
            e.transpose(bank[7][:, 64:184], rows_in[0:120, 1, :], ident[0:120, 0:120]).then_inc(vec_t, 1)
            e.wait_ge(loaded_x, 64)
            e.wait_ge(cst_ready, 3)

            def mod_tile(base, n0, t):
                s = w_ready(e, base + t)
                n, kh = n0 + t // 2, t % 2
                if kh == 0 and n >= 2:
                    e.wait_ge(mod_row, n - 1)
                for k in range(4):
                    for i, part in enumerate((whi, wlo)):
                        ins = e.matmul(bank[n % 2][:], cst[:, 4 * kh + k, :], part[:, s, k * 512:(k + 1) * 512],
                                       start=kh == 0 and k == 0 and i == 0, stop=kh == 1 and k == 3 and i == 1)
                ins.then_inc(used, 1)

            def fold_pair(layer, p):
                n = layer * 3 + p
                e.wait_ge(mod_back, 16 * (n + 1))
                e.wait_ge(loaded_bias, 32)
                if n:
                    e.wait_ge(mc_ready, n)
                e.matmul(bank[5][:, 0:32], rb[:, layer, p, :], fold[:], start=True, stop=True).then_inc(fold_mm, 1)

            def mean_square(n):
                e.wait_ge(sq_ready, KD * (n + 1))
                for k in range(KD):
                    ins = e.matmul(bank[4][:], ones[:], sq[:, :, k, :], start=k == 0, stop=k == KD - 1)
                ins.then_inc(ms_ready, 1)

            for t in range(24):
                mod_tile(A0, 0, t)
                if t < KD:
                    if t >= 2:
                        e.wait_ge(x_copied, t - 1)
                    for i in range(4):
                        ins = e.transpose(bank[2 + t % 2][:, i * P:(i + 1) * P], xtok[:, i, t * P:(t + 1) * P], ident[:])
                    ins.then_inc(x_t, 1)
                if t == KD:
                    mean_square(0)
                if t == 12:
                    fold_pair(0, 0)
                if t == 20:
                    fold_pair(0, 1)
            fold_pair(0, 2)
            e.wait_ge(mod_row, 12)
            e.wait_ge(mc_ready, 3)
            s = w_ready(e, POOL0)
            for g in range(4):
                e.wait_ge(ul_ready, 2 * g + 2)
                for o in range(2):
                    for i in range(2):
                        ins = passes(bank[2 * g + o][:], wpart(s, lambda w: w[:, (2 * g + i) * 256 + o * P:(2 * g + i) * 256 + (o + 1) * P]),
                                     (uh[:, 2 * g + i, :], ul[:, 2 * g + i, :]), i == 0, i == 1)
                    ins.then_inc(used if (g, o) == (3, 1) else pool_mm, 1)
            mean_square(1)
            e.wait_ge(ul_ready, 2 * KD)

            def hidden(t, b0, j, it, free):
                s = w_ready(e, t)
                for c in range(2):
                    if j:
                        e.wait_ge(free, val(2 * (j - 1) + c + 1, 4, it))
                    for k in range(KD):
                        ins = passes(bank[b0 + c][:], wpart(s, lambda w: w[:, k * 256 + c * P:k * 256 + (c + 1) * P]),
                                     (uh[:, k, :], ul[:, k, :]), k == 0, k == KD - 1)
                    ins.then_inc(used if c else (ffn_h3 if b0 else ffn_h1), 1)

            def down(t, j, it):
                s = w_ready(e, t)
                e.wait_ge(ffn_gl, val(2 * j + 2, 4, it))
                for k in range(KD):
                    if 8 * j + k >= 4:
                        e.wait_ge(ffn_added, val(8 * j + k - 3, 16, it))
                    for i in range(2):
                        ins = passes(bank[4 + k % 4][:], wpart(s, lambda w: w[:, i * D + k * P:i * D + (k + 1) * P]),
                                     (gh[:, j % 2, i, :], gl[:, j % 2, i, :]), i == 0, i == 1)
                    ins.then_inc(used if k == KD - 1 else ffn_out, 1)

            hidden(FFN0, 0, 0, None, ffn_silu)
            hidden(FFN0 + 1, 2, 0, None, ffn_g)
            with e.Fori(0, FF_BLOCKS // 2) as it:
                for u in range(2):
                    j, k = 1 + u, FFN0 + 2 + 3 * u
                    hidden((k, it), 0, j, it, ffn_silu)
                    hidden((k + 1, it), 2, j, it, ffn_g)
                    down((k + 2, it), j - 1, it)
            down(E0 - 1, FF_BLOCKS - 1, None)
            for t in range(24):
                mod_tile(E0, 12, t)
                if t == 4:
                    mean_square(2)
                if t == 13:
                    fold_pair(1, 0)
                if t == 21:
                    fold_pair(1, 1)
            fold_pair(1, 2)
            e.wait_ge(ul_ready, 3 * KD)

            def project(t, c0, q, n, done):
                s = w_ready(e, t)
                if q >= 2:
                    e.wait_ge(in_taken, q - 1)
                for k in range(KD):
                    ins = passes(bank[q % 2][:, 0:n], wpart(s, lambda w: w[:, k * 256 + c0:k * 256 + c0 + P]),
                                 (uh[:, k, 0:n], ul[:, k, 0:n]), k == 0, k == KD - 1)
                ins.then_inc(done, 1)

            def aux_bank(key):
                n = aux_no[key]
                if n >= 2:
                    e.wait_ge(aux_taken, n - 1)
                return bank[2 + n % 2]

            e.wait_ge(mod_row, 24)
            project(IN0, P, 0, NT2, used)
            e.wait_ge(a_ready, 1)
            b = aux_bank(("dt", 0, 0))
            for i in range(2):
                for t in range(4):
                    ins = e.transpose(b[:, i * 256 + t * 64:i * 256 + (t + 1) * 64], dts[64:128, i, t * P:(t + 1) * P], ident[64:128, 64:128])
            ins.then_inc(aux_mm, 1)
            b = aux_bank(("decay", 0, 0))
            e.wait_ge(aux_taken, 1)
            F, B = slice(0, 32), slice(32, 64)
            sums = [[(tri_gt, 2, F), (ones, 3, F)], [(tri_lt, 2, B)], [(tri_gt, 3, F)], [(tri_lt, 3, B), (ones, 2, B)],
                    [(tri_gt, 0, F)], [(tri_lt, 1, B)], [(ones, 0, F)], [(ones, 1, B)],
                    [(tri_le, 0, F)], [(tri_le, 1, F)], [(tri_ge, 0, B)], [(tri_ge, 1, B)]]
            for n, terms in enumerate(sums):
                for i, (w, t, s) in enumerate(terms):
                    ins = e.matmul(b[:, n * 32:(n + 1) * 32], w[:], a_tok[:, t, s], start=i == 0, stop=i == len(terms) - 1)
            ins.then_inc(aux_mm, 1)

            def turn(g, i):
                v_ = 6 * g + (0 if i == 0 else i + 1)
                b = aux_bank(("turn", g, i))
                e.wait_ge(conv_out, v_ + 1)
                lat = bt[:, g % 2, :] if i == 0 else xst[:, g % 2, i - 1, :]
                con = ccv[:, v_ % 2, :]
                for t in range(4):
                    src = lat[:, t * P:(t + 1) * P] if t < 2 else con[:, (t - 2) * P:(t - 1) * P]
                    ins = e.transpose(b[:, t * P:(t + 1) * P], src, ident[:])
                ins.then_inc(aux_mm, 1)

            def group_states(g):
                q = g % 2
                b = aux_bank(("cb", g, 0))
                for c in range(2):
                    s = slice(c * P, (c + 1) * P)
                    ins = e.matmul(b[:, s], bt[:, q, s], ct[:, q, s], start=True, stop=True)
                ins.then_inc(aux_mm, 1)
                for i, terms in enumerate((((2, 0), (3, 1)), ((2, 2), (3, 3)), ((0, 4),), ((1, 5),))):
                    b = aux_bank(("state", g, i))
                    for n, (t, m) in enumerate(terms):
                        e.wait_ge(xdd_ready, 6 * g + m + 1)
                        ins = e.matmul(b[:], b_tok[:, q, t, :], xdd[m % 2][:], start=n == 0, stop=n == len(terms) - 1)
                    ins.then_inc(aux_mm, 1)

            def cumulative(g, u):
                c, q4 = u // 2, u % 2
                for d, tri in enumerate((tri_le, tri_ge)):
                    for h in range(4):
                        hh = 32 * d + HPG * g + 4 * q4 + h
                        ins = e.matmul(bank[4 + d][:, h * P:(h + 1) * P], a_tok[:, c, hh:hh + 1].to_broadcast([P, P]), tri[:],
                                       start=True, stop=True)
                    ins.then_inc(bc_mm, 1)

            def heads(g, u):
                c, q4 = u // 2, u % 2
                n = 4 * g + u
                if q4 == 0 and g:
                    e.wait_ge(y_taken, 2 * (g - 1) + c + 1)
                e.wait_ge(xd_ready, 4 * (g + 1))
                e.wait_ge(st_ready, g + 1)
                e.wait_ge(mix_ready, n + 1)
                for h in range(4):
                    hg = 4 * q4 + h
                    o = bank[6 + c][64 * (h % 2):64 * (h % 2) + 64, (hg // 2) * P:(hg // 2 + 1) * P]
                    hs, ms = slice(hg * 64, hg * 64 + 64), slice(h * P, (h + 1) * P)
                    st = (0 if c == 0 else 2, 3 if c == 0 else 1)
                    for d in range(2):
                        e.matmul(o, xd[:, d, c, hs], seg[:, d, ms], start=d == 0, stop=False)
                    for d in range(2):
                        ins = e.matmul(o, states[:, st[d], hs], csc[:, d, ms], start=False, stop=d == 1)
                ins.then_inc(y_mm, 1)

            for g in range(NG + 1):
                for j in range(5):
                    if g < NG:
                        for c in range(2):
                            z_or_c = j >= 3 or (j, c) == (0, 1)
                            project(in_tile(g, j), c * P, in_chunk(g, j, c), NTOK if z_or_c else NT2, used if c else in_mm)
                    if g and j == 0:
                        group_states(g - 1)
                    if g and j:
                        heads(g - 1, j - 1)
                    if g and j < 4:
                        cumulative(g - 1, j)
                    if g < NG and j >= 2:
                        for i in {2: (0,), 3: (1, 2), 4: (3, 4)}[j]:
                            turn(g, i)
            for n in range(4):
                b = aux_bank(("resid", 0, n))
                t, half = n // 2, n % 2
                for k in range(4):
                    ins = e.transpose(b[:, k * P:(k + 1) * P], ht[:, 0, 4 * half + k, t * P:(t + 1) * P], ident[:])
                ins.then_inc(aux_mm, 1)
            for n in range(2):
                for kq in range(4):
                    s = w_ready(e, OUT0 + 4 * n + kq)
                    e.wait_ge(yl_ready, 4 * (kq + 1))
                    for t in range(2):
                        for k in range(4):
                            ts = slice(t * P, (t + 1) * P)
                            c = 4 * kq + k
                            ins = passes(bank[4 * n + t][:], (yh[:, c, ts], yl[:, c, ts]),
                                         wpart(s, lambda w: w[:, k * 512:(k + 1) * 512]), kq == 0 and k == 0, kq == 3 and k == 3)
                    ins.then_inc(used, 1)
                    if (n, kq) == (0, 3):
                        e.wait_ge(ysum_ready, 1)
                        for t in range(2):
                            ins = e.matmul(bank[6][:, t:t + 1], ysum[:, t * P:(t + 1) * P], ones[:, 0:1], start=True, stop=True)
                        ins.then_inc(rt_mm, 1)
            e.wait_ge(rows_back, 6 * 16)
            for i in range(8):
                b = aux_bank(("mods", 0, i))
                e.matmul(b[:], sel_row[:], mrow5[:, i // 2, (i % 2) * 512:(i % 2 + 1) * 512], start=True, stop=True).then_inc(aux_mm, 1)
            e.wait_ge(v_ready, 1)
            for n in range(4):
                b = aux_bank(("v", 0, n))
                t, half = n // 2, n % 2
                for k in range(4):
                    ins = e.transpose(b[:, k * P:(k + 1) * P], v[:, t, (4 * half + k) * P:(4 * half + k + 1) * P], ident[:])
                ins.then_inc(aux_mm, 1)
            e.wait_ge(aux_taken, len(aux))
            for t in range(2):
                for k in range(KD):
                    ins = e.matmul(bank[6][:, 16 + 8 * t:24 + 8 * t], vt[:, k, t * P:(t + 1) * P], rw[:, k, :], start=k == 0, stop=k == KD - 1)
            ins.then_inc(lg_mm, 1)
            e.wait_ge(rt_dve, 1)
            e.matmul(bank[6][:, 32:40], tri_lt[:], sel[:, 0, :], start=True, stop=True)
            e.matmul(bank[6][:, 40:48], tri_lt[:], sel[:, 1, :], start=True, stop=False)
            e.matmul(bank[6][:, 40:48], ones[:], sel[:, 0, :], start=False, stop=True)
            e.matmul(bank[6][:, 48:56], ones[:], sel[:, 0, :], start=True, stop=False)
            e.matmul(bank[6][:, 48:56], ones[:], sel[:, 1, :], start=False, stop=True).then_inc(rt_mm, 1)
            e.drain().then_inc(used2, SPL2)

            def gather(n):
                e.wait_ge(pick_ready, n)
                for k in range(KD):
                    for t in range(2):
                        ins = e.matmul(bank[5 + k // 4][:, (k % 4) * P:(k % 4 + 1) * P], v[:, t, k * P:(k + 1) * P], pick[:, t, :],
                                       start=t == 0, stop=t == 1)
                ins.then_inc(gather_mm, 1)

            def tile2(k, i, b=None):
                e.wait_ge(lo2, val2(RAW2 + k + 1, i, b, 6))
                return k % SPL2

            def up(i, k, bk, b=None):
                for half in range(2):
                    s = tile2(k + half, i, b)
                    for kk in range(4):
                        c = 4 * half + kk
                        w = slice(kk * 512, (kk + 1) * 512)
                        ins = passes(bank[bk][:], (xgh[:, c, :], xgl[:, c, :]), (whi2[:, s, w], wlo2[:, s, w]), c == 0, c == KD - 1)
                    ins.then_inc(used2, 1)

            def down2(i, k, blk, first, last, b=None):
                e.wait_ge(gtl_ready, val3(blk + 1, i, b))
                for half in range(2):
                    s = tile2(k + half, i, b)
                    for f in range(2):
                        ff = 2 * half + f
                        for n in range(2):
                            w = slice(f * D + n * 512, f * D + (n + 1) * 512)
                            ins = passes(bank[3 + n][:], (gth[:, ff, :], gtl[:, ff, :]), (whi2[:, s, w], wlo2[:, s, w]),
                                         first and ff == 0, last and ff == 3)
                    ins.then_inc(used2, 1)

            def turn2(i, blk, b=None):
                e.wait_ge(gm_ready, val3(blk + 1, i, b))
                for f in range(4):
                    ins = e.transpose(bank[2][:, f * P:(f + 1) * P], gme[:, f * P:(f + 1) * P], ident[:])
                ins.then_inc(turn_mm, 1)

            gather(1)
            e.wait_ge(tab_ready, 1)
            count = e.value_load(itab[0:1, 12:13], min_val=NE, max_val=MAX_ITEMS)
            with e.Fori(0, count) as i:
                e.wait_ge(xgl_ready, i + 1)
                up(i, 0, 0)
                up(i, 2, 1)
                e.wait_ge(acc_added, i * 4 + 1)
                for t in range(2):
                    ins = e.transpose(bank[7][:, t * P:(t + 1) * P], pickg[:, t, :], ident[:])
                ins.then_inc(put_mm, 1)
                turn2(i, 0)
                up(i, 4, 0)
                up(i, 6, 1)
                down2(i, 8, 0, True, False)
                turn2(i, 1)
                with e.Fori(0, EB - 2) as b:
                    up(i, 10, 0, b)
                    up(i, 12, 1, b)
                    down2(i, 14, 1, False, False, b)
                    turn2(i, 2, b)
                gather(i + 2)
                down2(i, TPI - 2, EB - 1, False, True)
                e.wait_ge(put_ready, i + 1)
                e.wait_ge(osb_ready, i + 1)
                for n, bk in enumerate((7, 2, 3, 4)):
                    t, h = n // 2, n % 2
                    e.matmul(bank[bk][:], put[:, t, :], osb[:, h * 512:(h + 1) * 512], start=True, stop=True).then_inc(scat_mm, 1)


_INS = ['x', 'c', 'ctx', 'c_ctx', 'ada_w', 'ada_b', 'norm_mix_w', 'norm_ffn_w',
        'pool_w', 'pool_scale', 'ssd_in_w', 'ssd_conv_w', 'ssd_conv_b', 'ssd_A_log', 'ssd_dt_bias', 'ssd_D',
        'ssd_norm_w', 'ssd_out_w', 'ffn_w1', 'ffn_w3', 'ffn_w2', 'moe_router_w', 'moe_w1', 'moe_w3',
        'moe_w2', 'final_norm_w']
_OUTS = [((1, 256, 1024), 'float32')]


def kernel(**inputs):
    import numpy as _np
    import concourse.bacc as _bacc
    from concourse import mybir as _mybir
    from concourse.bass_utils import run_bass_kernel_spmd as _run

    nc = _bacc.Bacc("TRN2", target_bir_lowering=False, num_devices=1)
    arrays, args = {}, {}
    for name in _INS:
        a = _np.ascontiguousarray(inputs[name])
        arrays[f"in_{name}_dram"] = a
        args[name] = nc.dram_tensor(f"in_{name}_dram", a.shape, _mybir.dt.from_np(a.dtype), kind="ExternalInput").ap()
    shape, dtype = _OUTS[0]
    out = nc.dram_tensor("out_0_dram", shape, _mybir.dt.from_np(_np.dtype(dtype)), kind="ExternalOutput").ap()
    hybrid_backbone(nc, args, out)
    r = _run(nc, [arrays], core_ids=[0])
    return r.results[0]["out_0_dram"]
```

```python
from contextlib import ExitStack

import numpy as np

import concourse.bass as bass
from concourse import mybir

F32 = mybir.dt.float32
F32R = mybir.dt.float32r
I32 = mybir.dt.int32
ALU = mybir.AluOpType
ACT = mybir.ActivationFunctionType
AX_X = mybir.AxisListType.X

P = 128
D = 1024
KD = D // P
NTOK = 256
NT2 = 2 * NTOK
GRID_W = 64
EPS = 1e-6
NMOD = 6
WINDOWS = (2, 4, 8, 16)
DI = 2048
NG = 4
NH = 32
HPG = NH // NG
BC = 512
DSTATE = 128
DFF = 2816
NE = 8
DFE = 3584
TILE = 2048

FF_BLOCKS = DFF // 256
MODT = 48
POOL0 = 27
FFN0 = MODT + 1
IN0 = FFN0 + 3 * FF_BLOCKS
OUT0 = IN0 + 1 + 5 * NG
NTILES = OUT0 + 8
RAW1, SPL1 = 3, 2

EB = DFE // 512
TPI = 6 * EB
RAW2, SPL2 = 6, 3
MAX_ITEMS = NE + 3

PLAIN = tuple(t for t in range(8, 39) if t != POOL0)
POOLED_AT = (19, 20, 23, 25)
MS_BANK = (4, 4, 2)
POOL_BANKS = (2, 3, 6, 7)
NORM1_AT = POOL0 + 6

PADW = 8 + 4 * (GRID_W + 8) + NTOK + 8


def hybrid_backbone(nc, a, out):
    ctx = ExitStack()
    with ctx:
        def sem(name):
            return ctx.enter_context(nc.semaphore(name))

        def sb(name, shape, dt=F32):
            return ctx.enter_context(nc.sbuf_tensor(name, shape, dt))

        bank = [ctx.enter_context(nc.psum_tensor(f"bank{i}", [P, 512], F32)) for i in range(8)]

        ident = sb("ident", [P, P])
        ones = sb("ones", [P, P])
        tri_le = sb("tri_le", [P, P])
        tri_ge = sb("tri_ge", [P, P])
        tri_lt = sb("tri_lt", [P, P])
        tri_gt = sb("tri_gt", [P, P])
        fold = sb("fold", [80, 32])
        slot_id = sb("slot_id", [P, P])
        before = sb("before", [P, NE, NE])
        expert_id = sb("expert_id", [P, NE])
        eps_col = sb("eps_col", [P, 1])
        va = sb("va", [P, 64])
        vb = sb("vb", [P, 120])
        mc = [sb(f"mc{i}", [P, 3, 2, 2, KD]) for i in range(2)]
        aff = sb("aff", [P, 4, 2, KD])
        dcol = sb("dcol", [P, 16])
        sel_row = sb("sel_row", [5, P])

        top = [(nc.sbuf_base + 31) // 32 * 32]
        origin = top[0]

        def at(name, off_kb, shape, dt=F32):
            size = int(np.prod(shape[1:])) * 4
            off = origin + int(off_kb * 1024)
            assert off + size <= nc.sbuf_usable_end, (name, off + size - nc.sbuf_usable_end)
            top[0] = max(top[0], off + size)
            return nc.alloc_sbuf_tensor_at(name, shape, dt, offset=off)

        raw = at("raw", 0, [P, RAW1, TILE])
        whi = at("whi", 24, [P, SPL1, TILE], F32R)
        wlo = at("wlo", 40, [P, SPL1, TILE], F32R)
        uh = at("uh", 56, [P, KD, NT2], F32R)
        ul = at("ul", 72, [P, KD, NT2], F32R)
        ht = at("ht", 88, [P, 2, KD, NTOK])
        sq = at("sq", 104, [P, 2, KD, NTOK])
        xtok = at("xtok", 120, [P, 4, D])
        tn = at("tn", 120, [P, 2, KD, NTOK])
        padded = at("padded", 136, [P, KD, PADW])
        win = at("win", 153.5, [P, 2, 2, PADW])
        wing = at("wing", 162.5, [P, 2, 2, PADW])
        inv_cnt = at("inv_cnt", 80, [P, 4, NT2])
        sg = at("sg", 136, [P, 2, NT2])
        gf = at("gf", 140, [P, 2, NT2])
        gh = at("gh", 144, [P, 2, 2, NT2], F32R)
        gl = at("gl", 152, [P, 2, 2, NT2], F32R)
        mrow = at("mrow", 171.5, [4, 2, 2048])
        rb = at("rb", 187.5, [80, 2, 3, P])
        rstd = at("rstd", 190.5, [P, NT2])
        csf = at("csf", 171.25, [P, KD, 4])
        cst = at("cst", 192.5, [P, KD, P], F32R)
        rows_in = at("rows_in", 104, [P, 2, P])

        y2 = at("y2", 104, [P, 16, NTOK])
        xs_tok = at("xs_tok", 120, [P, 2, 4, 512])
        b_tok = at("b_tok", 136, [P, 2, 4, P])
        bt = at("bt", 140, [P, 2, NTOK])
        ct = at("ct", 142, [P, 2, NTOK])
        xst = at("xst", 144, [P, 2, 4, NTOK])
        sz = at("sz", 152, [P, 2, 4, NTOK])
        xd = at("xd", 160, [P, 2, 2, 512])
        xdd = [at("xdd0", 168, [P, 512]), at("xdd1", 199.25, [P, 512])]
        seg = at("seg", 170, [P, 2, 512])
        ytmp = at("ytmp", 174, [P, 512])
        ysum = at("ysum", 198, [P, NTOK])
        csc = at("csc", 178, [P, 2, 512])
        cp = at("cp", 182, [P, 2, 2, 260])
        cacc = at("cacc", 186.25, [P, 2, 512])
        ccv = at("ccv", 190.25, [P, 2, NTOK])
        cb = at("cb", 192.25, [P, 2, 2, P])
        states = at("states", 96, [P, 4, 512])
        dt_tok = at("dt_tok", 194.25, [P, 4, 64])
        a_tok = at("a_tok", 195.25, [P, 4, 64])
        wdec = at("wdec", 196.25, [P, 8, NH])
        acs = at("acs", 197.25, [P, 4, NH])
        ry = at("ry", 197.875, [P, 8])
        dts = at("dts", 160, [P, 5, NT2])
        dpar = at("dpar", 197.8125, [P, 4])

        raw2 = at("raw2", 0, [P, RAW2, TILE])
        yh = uh[:].rearrange("p k (c n) -> p (k c) n", c=2)
        yl = ul[:].rearrange("p k (c n) -> p (k c) n", c=2)
        whi2 = at("whi2", 48, [P, SPL2, TILE], F32R)
        wlo2 = at("wlo2", 72, [P, SPL2, TILE], F32R)
        xgh = at("xgh", 96, [P, KD, P], F32R)
        xgl = at("xgl", 100, [P, KD, P], F32R)
        gth = at("gth", 104, [P, 4, P], F32R)
        gtl = at("gtl", 106, [P, 4, P], F32R)
        sge = at("sge", 108, [P, 512])
        gme = at("gme", 110, [P, 512])
        osb = at("osb", 112, [P, D])
        pick = at("pick", 116, [P, 2, P])
        pickg = at("pickg", 117, [P, 2, P])
        put = at("put", 118, [P, 2, P])
        hl = at("hl", 120, [P, 2, D])
        mods = at("mods", 128, [P, 4, D])
        nfw = at("nfw", 144, [P, D])
        fnw = at("fnw", 148, [P, D])
        v = at("v", 152, [P, 2, D])
        vt = at("vt", 160, [P, KD, NTOK])
        acc = at("acc", 168, [P, 2, D])
        mrow5 = at("mrow5", 176, [5, 4, D])
        rw = at("rw", 192, [P, KD, NE])
        lg = at("lg", 192.5, [P, 2, NE])
        cmp = at("cmp", 193, [P, 2, NE, NE])
        eqs = at("eqs", 193.5, [P, 2, NE, NE])
        sel = at("sel", 194, [P, 2, NE])
        gate = at("gate", 194.125, [P, 2, NE])
        pos = at("pos", 194.25, [P, 2, NE])
        rsc = at("rsc", 194.375, [P, 16])
        cnt = at("cnt", 194.5, [P, NE])
        over = at("over", 194.625, [P, NE])
        more = at("more", 194.75, [P, 3, NE])
        tmp3 = at("tmp3", 195, [P, 3, NE])
        pos_item = at("pos_item", 195.25, [P, 2, 12])
        gate_item = at("gate_item", 195.375, [P, 2, 12])
        ftab = at("ftab", 195.5, [P, 16])
        itab = at("itab", 195.75, [1, 16], I32)
        stat = at("stat", 196, [P, 16])
        sq2 = at("sq2", 160, [P, D])

        scr = nc.dram_tensor("mod_scratch", [2, 3, 4, 2048], F32, kind="Internal").ap()

        landed = [sem(f"landed{i}") for i in range(RAW1)]
        hi_done, lo_done, used = sem("hi_done"), sem("lo_done"), sem("used")
        consts_ready = sem("consts_ready")
        loaded_x, loaded_vec, loaded_bias, loaded_misc = sem("loaded_x"), sem("loaded_vec"), sem("loaded_bias"), sem("loaded_misc")
        vec_t, vec_cols, cst_ready = sem("vec_t"), sem("vec_cols"), sem("cst_ready")
        x_t, x_copied = sem("x_t"), sem("x_copied")
        sq_ready, ms_ready, sd_ready, tn_ready = sem("sq_ready"), sem("ms_ready"), sem("sd_ready"), sem("tn_ready")
        mod_row, mod_saved, mod_back = sem("mod_row"), sem("mod_saved"), sem("mod_back")
        fold_mm, mc_ready = sem("fold_mm"), sem("mc_ready")
        pads_zero, pad_ready, pool_g, pool_v = sem("pads_zero"), sem("pad_ready"), sem("pool_g"), sem("pool_v")
        uh_ready, ul_ready = sem("uh_ready"), sem("ul_ready")
        pool_mm, pool_added = sem("pool_mm"), sem("pool_added")
        ffn_h1, ffn_silu, ffn_h3, ffn_g = sem("ffn_h1"), sem("ffn_silu"), sem("ffn_h3"), sem("ffn_g")
        ffn_gh, ffn_gl, ffn_out, ffn_added = sem("ffn_gh"), sem("ffn_gl"), sem("ffn_out"), sem("ffn_added")
        in_mm, in_taken, landed_c, conv_acc, conv_out = sem("in_mm"), sem("in_taken"), sem("landed_c"), sem("conv_acc"), sem("conv_out")
        dt_steps, dt_act, a_ready = sem("dt_steps"), sem("dt_act"), sem("a_ready")
        aux_mm, aux_taken, wdec_ready = sem("aux_mm"), sem("aux_taken"), sem("wdec_ready")
        z_ready, cb_ready, st_ready = sem("z_ready"), sem("cb_ready"), sem("st_ready")
        xd_ready, xdd_ready = sem("xd_ready"), sem("xdd_ready")
        bc_mm, seg_ready, exp_ready, mix_ready = sem("bc_mm"), sem("seg_ready"), sem("exp_ready"), sem("mix_ready")
        y_mm, y_taken, ysum_ready, pads2 = sem("y_mm"), sem("y_taken"), sem("ysum_ready"), sem("pads2")
        yw_ready, yh_ready, yl_ready, ry_root, ry_ready = sem("yw_ready"), sem("yh_ready"), sem("yl_ready"), sem("ry_root"), sem("ry_ready")
        rows_back, hl_ready, mods_ready = sem("rows_back"), sem("hl_ready"), sem("mods_ready")
        h_ready, hsq_ready, v_ready, lg_mm, rt_dve, rt_act, rt_mm, tab_ready = (sem(n) for n in (
            "h_ready", "hsq_ready", "v_ready", "lg_mm", "rt_dve", "rt_act", "rt_mm", "tab_ready"))
        landed2 = [sem(f"expert_landed{i}") for i in range(RAW2)]
        hi2, lo2, used2 = sem("expert_hi"), sem("expert_lo"), sem("expert_used")
        pick_ready, put_mm, put_ready = sem("pick_ready"), sem("put_mm"), sem("put_ready")
        gather_mm, xgh_ready, xgl_ready = sem("gather_mm"), sem("xgh_ready"), sem("xgl_ready")
        silu2, gm_ready, turn_mm, gth_ready, gtl_ready = (sem(n) for n in ("silu2", "gm_ready", "turn_mm", "gth_ready", "gtl_ready"))
        osb_ready, scat_mm, acc_added, out_sq, out_ready, out_done = (sem(n) for n in (
            "osb_ready", "scat_mm", "acc_added", "out_sq", "out_ready", "out_done"))

        block = ctx.enter_context(nc.Block())

        c_tiles = [IN0 + 1 + 5 * g for g in range(NG)]

        def tile_ref(t):
            return t if isinstance(t, tuple) else (t, None)

        def val(const, coef, reg):
            return const if reg is None else reg * coef + const

        def val2(const, i, b, coef):
            x = const if i is None else i * TPI + const
            return x if b is None else b * coef + x

        def val3(const, i, b):
            x = const if i is None else i * EB + const
            return x if b is None else x + b

        def splits(k):
            return k - sum(t < k for t in PLAIN)

        split_tiles = [t for t in range(FFN0 + 3) if t not in PLAIN]

        def split_hi(e, t):
            k, reg = tile_ref(t)
            if k in PLAIN:
                return
            e.wait_ge(landed[k % RAW1], val(16 * (k // RAW1 + 1), 32, reg))
            if reg is None and k in c_tiles:
                e.wait_ge(landed_c, 16 * (c_tiles.index(k) + 1))
            if k >= SPL1:
                last = split_tiles[splits(k) - SPL1] if k < FFN0 + 2 else k - SPL1
                e.wait_ge(used, val(last + 1, 6, reg))
            e.activation(whi[:, splits(k) % SPL1, :], raw[:, k % RAW1, :], ACT.Copy).then_inc(hi_done, 1)

        def split_lo(e, t):
            k, reg = tile_ref(t)
            if k in PLAIN:
                return
            i = splits(k)
            e.wait_ge(hi_done, val(i + 1, 6, reg))
            e.tensor_tensor(wlo[:, i % SPL1, :], raw[:, k % RAW1, :], whi[:, i % SPL1, :].bitcast(F32),
                            ALU.subtract).then_inc(lo_done, 1)

        def w_ready(e, t):
            k, reg = tile_ref(t)
            e.wait_ge(lo_done, val(splits(k) + 1, 6, reg))
            return splits(k) % SPL1

        def slot_free(e, k, reg=None):
            if k - RAW1 in PLAIN:
                e.wait_ge(used, k - RAW1 + 1)
            elif k >= RAW1:
                e.wait_ge(lo_done, val(splits(k - RAW1) + 1, 6, reg))

        def mod_at(m):
            return m if m < POOL0 else m + 1

        def mod_no(s):
            return s if s < POOL0 else None if s == POOL0 else s - 1

        def mod_src(m):
            layer, t = m // 24, m % 24
            n, kh = t // 2, t % 2
            return a["ada_w"][layer, kh * 512:(kh + 1) * 512, n * 512:(n + 1) * 512].rearrange("(k p) n -> p k n", p=P)

        def cols_src(w, c0):
            return w[:, c0:c0 + 256].rearrange("(k p) n -> p k n", p=P)

        def pool_windows(e, g, w):
            src, n = padded[:, 2 * g:2 * g + 2, :], PADW
            e.tensor_tensor(w[:, 0, :, 1:n], src[:, :, 0:n - 1], src[:, :, 1:n], ALU.add)
            e.drain()
            cur, sh = 0, 1
            for _ in range(g):
                e.tensor_tensor(w[:, 1 - cur, :, sh:n - sh], w[:, cur, :, 0:n - 2 * sh], w[:, cur, :, 2 * sh:n], ALU.add)
                e.drain()
                cur, sh = 1 - cur, 2 * sh
            c0 = 8 + 4 * (GRID_W + 8)
            lat = lambda x: x[:, 8:c0].rearrange("p (r w) -> p r w", w=GRID_W + 8)[:, :, 0:GRID_W]
            rows = lambda x: x.rearrange("p (r w) -> p r w", w=GRID_W)
            for k in range(2):
                e.tensor_tensor(rows(tn[:, 0, 2 * g + k, :]), lat(w[:, cur, k, :]), rows(inv_cnt[:, g, 0:NTOK]), ALU.mult)
                e.tensor_tensor(tn[:, 1, 2 * g + k, :], w[:, cur, k, c0:c0 + NTOK], inv_cnt[:, g, NTOK:], ALU.mult)
            e.drain()
            for k in range(2):
                e.tensor_tensor(rows(tn[:, 0, 2 * g + k, :]), rows(tn[:, 0, 2 * g + k, :]), lat(padded[:, 2 * g + k, :]), ALU.subtract)
                e.tensor_tensor(tn[:, 1, 2 * g + k, :], tn[:, 1, 2 * g + k, :], padded[:, 2 * g + k, c0:c0 + NTOK], ALU.subtract)

        def two(x):
            return x.rearrange("p (s n) -> p s n", s=2)

        def split_u_hi(e, k):
            e.activation(two(uh[:, k, :]), tn[:, :, k, :], ACT.Copy).then_inc(uh_ready, 1)

        def split_u_lo(e, k, base):
            e.wait_ge(uh_ready, base + k + 1)
            e.tensor_tensor(two(ul[:, k, :]), tn[:, :, k, :], two(uh[:, k, :].bitcast(F32)), ALU.subtract).then_inc(ul_ready, 1)

        def w1_tile(j):
            return FFN0 + 2 + 3 * (j - 1) if j else FFN0

        def w2_tile(j):
            return IN0 - 1 if j == FF_BLOCKS - 1 else FFN0 + 3 * j + 4

        def chunk_done(e, s, tile, j, c, it):
            if c == 0:
                e.wait_ge(s, val(j + 1, 2, it))
            else:
                e.wait_ge(used, val(tile + 1, 6, it))

        aux = [("dt", 0, 0), ("decay", 0, 0)]
        for g in range(NG + 1):
            if g:
                aux += [("cb", g - 1, 0)] + [("state", g - 1, i) for i in range(4)]
            if g < NG:
                aux += [("turn", g, i) for i in range(5)]
        aux += [("resid", 0, i) for i in range(4)] + [("mods", 0, i) for i in range(8)] + [("v", 0, i) for i in range(4)]
        aux_no = {key: n for n, key in enumerate(aux)}

        def in_tile(g, j):
            return IN0 + 1 + 5 * g + j

        def in_chunk(g, j, c):
            return 1 + 10 * g + 2 * j + c

        @block.sync
        def _(e):
            def load(t, src, shape):
                k, reg = tile_ref(t)
                slot_free(e, k, reg)
                dst = raw[:, k % RAW1, :].rearrange("p (k n) -> p k n", k=shape)
                e.dma_start(dst, src).then_inc(landed[k % RAW1], 16)

            for s in range(FFN0):
                if s == POOL0:
                    load(s, a["pool_w"][0].rearrange("g (i p) o -> p (g i) o", p=P), 8)
                else:
                    load(s, mod_src(mod_no(s)), 4)
            w1, w3, w2 = a["ffn_w1"][0], a["ffn_w3"][0], a["ffn_w2"][0]
            load(FFN0, cols_src(w1, 0), 8)
            load(FFN0 + 1, cols_src(w3, 0), 8)
            with e.Fori(0, FF_BLOCKS // 2) as it:
                for u in range(2):
                    k = FFN0 + 2 + 3 * u
                    c = it * 512 + (1 + u) * 256
                    load((k, it), w1[:, bass.ds(c, 256)].rearrange("(k p) n -> p k n", p=P), 8)
                    load((k + 1, it), w3[:, bass.ds(c, 256)].rearrange("(k p) n -> p k n", p=P), 8)
                    load((k + 2, it), w2[bass.ds(it * 512 + u * 256, 256), :].rearrange("(k p) n -> p k n", p=P), 2)
            load(IN0 - 1, w2[DFF - 256:DFF, :].rearrange("(k p) n -> p k n", p=P), 2)
            inw = a["ssd_in_w"][0]
            load(IN0, cols_src(inw, inw.shape[1] - 256), 8)
            for g in range(NG):
                k = in_tile(g, 0)
                slot_free(e, k)
                dst = raw[:, k % RAW1, :].rearrange("p (k b n) -> p b k n", k=KD, b=2)
                for b_, done in ((0, landed[k % RAW1]), (1, landed_c)):
                    c0 = 2 * DI + b_ * BC + g * P
                    e.dma_start(dst[:, b_], inw[:, c0:c0 + P].rearrange("(k p) n -> p k n", p=P)).then_inc(done, 16)
                for j in (0, 1):
                    load(in_tile(g, 1 + j), cols_src(inw, DI + 512 * g + 256 * j), 8)
                for j in (0, 1):
                    load(in_tile(g, 3 + j), cols_src(inw, 512 * g + 256 * j), 8)
            for n in range(2):
                for kq in range(4):
                    load(OUT0 + 4 * n + kq, a["ssd_out_w"][0][kq * 512:(kq + 1) * 512, n * 512:(n + 1) * 512].rearrange("(k p) n -> p k n", p=P), 4)
            def load2(k, i, b, coef, src, kk):
                e.wait_ge(lo2, val2(k + 1, i, b, coef))
                e.dma_start(raw2[:, k % RAW2, :].rearrange("p (k n) -> p k n", k=kk), src).then_inc(landed2[k % RAW2], 16)

            m1 = a["moe_w1"][0].rearrange("e (h k p) n -> e h p k n", h=2, p=P)
            m3 = a["moe_w3"][0].rearrange("e (h k p) n -> e h p k n", h=2, p=P)
            m2 = a["moe_w2"][0].rearrange("e (f k p) n -> e f p k n", k=2, p=P)
            one = lambda x: x.rearrange("o p k n -> p (o k) n")

            def up_tiles(k, i, b, ex, blk):
                for n, m in enumerate((m1, m3)):
                    for half in range(2):
                        cols = bass.ds(blk * 512, 512) if b is not None else slice(blk * 512, blk * 512 + 512)
                        load2(k + 2 * n + half, i, b, 6, one(m[bass.ds(ex, 1), half, :, :, cols]), 4)

            def down_tiles(k, i, b, ex, blk):
                for half in range(2):
                    f = (blk * 2 + half)
                    src = m2[bass.ds(ex, 1), bass.ds(f, 1) if b is not None else slice(f, f + 1)]
                    load2(k + half, i, b, 6, src.rearrange("o f p k n -> p (o f k) n"), 2)

            e.wait_ge(tab_ready, 1)
            count = e.value_load(itab[0:1, 12:13], min_val=NE, max_val=MAX_ITEMS)
            with e.Fori(0, count) as i:
                ex = e.value_load(itab[0:1, bass.ds(i, 1)], min_val=0, max_val=NE - 1)
                up_tiles(0, i, None, ex, 0)
                with e.Fori(0, EB - 1) as b:
                    up_tiles(4, i, b, ex, b + 1)
                    down_tiles(8, i, b, ex, b)
                down_tiles(TPI - 2, i, None, ex, EB - 1)
            for k in range(2):
                e.wait_ge(lo2, count * TPI + (k + 1))
                e.dma_start(raw2[:, k, :].rearrange("p (k n) -> p k n", k=4), one(m1[0:1, k, :, :, 0:512])).then_inc(landed2[k], 16)
            for t in range(2):
                e.wait_ge(out_ready, t + 1)
                e.dma_start(out[0, t * P:(t + 1) * P, :], acc[:, t, :]).then_inc(out_done, 16)
            e.wait_ge(out_done, 32)

        @block.gpsimd
        def _(e):
            e.memset(ident[:], 0.0)
            e.drain()
            e.affine_select(out=ident[:], in_=ident[:], compare_op=ALU.not_equal, fill=1.0, base=0,
                            pattern=[[-1, P]], channel_multiplier=1)
            e.drain().then_inc(consts_ready, 1)
            e.memset(ones[:], 1.0)
            e.memset(fold[:], 0.0)
            e.memset(sel_row[:], 1.0)
            e.memset(eps_col[:], EPS)
            e.memset(before[:], 1.0)
            e.drain()
            e.affine_select(out=tri_le[:], in_=ones[:], compare_op=ALU.is_ge, fill=0.0, base=0,
                            pattern=[[1, P]], channel_multiplier=-1)
            e.affine_select(out=tri_ge[:], in_=ones[:], compare_op=ALU.is_ge, fill=0.0, base=0,
                            pattern=[[-1, P]], channel_multiplier=1)
            e.affine_select(out=tri_lt[:], in_=ones[:], compare_op=ALU.is_gt, fill=0.0, base=0,
                            pattern=[[1, P]], channel_multiplier=-1)
            e.affine_select(out=tri_gt[:], in_=ones[:], compare_op=ALU.is_gt, fill=0.0, base=0,
                            pattern=[[-1, P]], channel_multiplier=1)
            for kind in range(2):
                for q in (kind, kind + 2, 4):
                    v_ = fold[:, 16 * kind:16 * kind + 16]
                    e.affine_select(out=v_, in_=v_, compare_op=ALU.not_equal, fill=1.0, base=-16 * q,
                                    pattern=[[-1, 16]], channel_multiplier=1)
                    e.drain()
            for q in (1, 3):
                e.affine_select(out=sel_row[:], in_=sel_row[:], compare_op=ALU.not_equal, fill=0.0, base=-q,
                                pattern=[[0, P]], channel_multiplier=1)
                e.drain()
            e.affine_select(out=before[:], in_=before[:], compare_op=ALU.is_gt, fill=0.0, base=0,
                            pattern=[[1, NE], [-1, NE]], channel_multiplier=0)
            e.iota(slot_id[:], pattern=[[1, P]], base=0, channel_multiplier=0, allow_small_or_imprecise_dtypes=True)
            e.iota(expert_id[:], pattern=[[1, NE]], base=0, channel_multiplier=0, allow_small_or_imprecise_dtypes=True)
            e.drain().then_inc(consts_ready, 1)
            e.memset(padded[:], 0.0)
            e.memset(wing[:], 0.0)
            for i, w in enumerate(WINDOWS):
                e.memset(inv_cnt[:, i, :], 1.0 / w)
            e.drain()
            for i, w in enumerate(WINDOWS):
                lo, hi = w // 2, w - 1 - w // 2
                for s, L in ((slice(0, NTOK), GRID_W), (slice(NTOK, NT2), NTOK)):
                    rows = inv_cnt[:, i, s].rearrange("p (r w) -> p r w", w=L)
                    for x in range(lo):
                        e.memset(rows[:, :, x:x + 1], 1.0 / (x + hi + 1))
                    for x in range(hi):
                        e.memset(rows[:, :, L - 1 - x:L - x], 1.0 / (x + lo + 1))
            e.drain().then_inc(pads_zero, 1)

            def keep_rows(layer, p):
                n = layer * 3 + p
                e.wait_ge(mod_row, 4 * (n + 1))
                e.dma_start(scr[layer, p], mrow[:, n % 2, :]).then_inc(mod_saved, 16)
                if n > 3:
                    return
                e.wait_ge(mod_saved, 16 * (n + 1))
                e.dma_start(rb[0:64, layer, p, :], scr[layer, p].rearrange("q (i d) -> (q i) d", d=P)).then_inc(mod_back, 16)

            keep_rows(0, 0)
            e.wait_ge(pad_ready, 1)
            for g in (2, 3):
                pool_windows(e, g, wing)
                e.drain().then_inc(pool_g, 1)
                if g == 2:
                    keep_rows(0, 1)
            keep_rows(0, 2)
            for p in range(3):
                keep_rows(1, p)
            e.wait_ge(tn_ready, 2 * KD)
            e.wait_ge(ul_ready, 3 * KD)
            e.wait_ge(mod_saved, 6 * 16)
            e.memset(cp[:], 0.0)
            e.memset(ysum[:], 0.0)
            e.drain().then_inc(pads2, 1)
            e.wait_ge(wdec_ready, 2)
            hv = lambda x: x.rearrange("p (h c) -> p h c", c=64)

            def spread(t, h0):
                return t[:, h0:h0 + HPG].unsqueeze(2).to_broadcast([P, HPG, 64])

            def y_squares(g):
                for c in range(2):
                    e.wait_ge(y_taken, 2 * g + c + 1)
                y2g = y2[:, 4 * g:4 * g + 4, :]
                for i in range(0, 4, 2):
                    e.drain()
                    e.tensor_tensor(ytmp[:].rearrange("p (c n) -> p c n", c=2), y2g[:, i:i + 2, :], y2g[:, i:i + 2, :], ALU.mult)
                    e.drain()
                    for j in range(2):
                        e.tensor_tensor(ysum[:], ysum[:], ytmp[:, j * NTOK:(j + 1) * NTOK], ALU.add)
                        e.drain()

            for g in range(NG):
                q = g % 2
                e.wait_ge(aux_taken, aux_no[("turn", g, 4)] + 1)
                for n, (tile, w) in enumerate(((2, 0), (3, 2), (2, 1), (3, 3), (0, 4), (1, 5))):
                    m = 6 * g + n
                    if n in (2, 3):
                        e.wait_ge(aux_mm, aux_no[("state", g, 0)] + 1)
                    elif n in (4, 5):
                        e.wait_ge(aux_mm, aux_no[("state", g, 1)] + 1)
                    elif g:
                        e.wait_ge(aux_mm, aux_no[("state", g - 1, 3)] + 1)
                    e.tensor_tensor(hv(xdd[m % 2][:]), hv(xs_tok[:, q, tile, :]), spread(wdec[:, w, :], HPG * g),
                                    ALU.mult).then_inc(xdd_ready, 1)
                if g:
                    e.wait_ge(y_mm, 4 * g)
                for d in range(2):
                    for c in range(2):
                        e.tensor_tensor(hv(xd[:, d, c, :]), hv(xs_tok[:, q, c, :]), spread(dt_tok[:, c, :], 32 * d + HPG * g),
                                        ALU.mult).then_inc(xd_ready, 1)
                if g:
                    y_squares(g - 1)
            y_squares(NG - 1)
            e.drain().then_inc(ysum_ready, 1)
            e.wait_ge(y_taken, 2 * NG)
            e.dma_start(mrow5[0:4, 0:2, :], scr[1, 1].rearrange("q (m d) -> q m d", m=2)).then_inc(rows_back, 16)
            e.dma_start(mrow5[0:4, 2:4, :], scr[1, 2].rearrange("q (m d) -> q m d", m=2)).then_inc(rows_back, 16)
            e.dma_start(mrow5[4:5, :, :], a["ada_b"][1:2, 2 * D:6 * D].rearrange("q (m d) -> q m d", m=4)).then_inc(rows_back, 16)
            e.dma_start(nfw[:], a["norm_ffn_w"][1:2, :].to_broadcast([P, D])).then_inc(rows_back, 16)
            e.dma_start(fnw[:], a["final_norm_w"].rearrange("(o d) -> o d", o=1).to_broadcast([P, D])).then_inc(rows_back, 16)
            e.dma_start(rw[:], a["moe_router_w"][0].rearrange("(k p) e -> p k e", p=P)).then_inc(rows_back, 16)

        @block.scalar
        def _(e):
            vec = [(a["norm_mix_w"][0], 0, 8), (a["norm_mix_w"][1], 8, 8), (a["norm_ffn_w"][0], 16, 8),
                   (a["pool_scale"][0], 24, 8), (a["ssd_norm_w"][0], 32, 16), (a["c"][0], 48, 8), (a["c_ctx"], 56, 8)]
            for src, r, n in vec:
                e.dma_start(rows_in[r:r + n, 0, :], src.rearrange("(r d) -> r d", d=P)).then_inc(loaded_vec, 16)
            e.dma_start(rows_in[0:96, 1, :], a["ssd_conv_w"][0].rearrange("t (r d) -> (t r) d", d=P)).then_inc(loaded_vec, 16)
            e.dma_start(rows_in[96:120, 1, :], a["ssd_conv_b"][0].rearrange("(r d) -> r d", d=P)).then_inc(loaded_vec, 16)
            for kind, src in enumerate((a["x"][0], a["ctx"][0])):
                for i in range(2):
                    e.dma_start(xtok[:, 2 * kind + i, :], src[i * P:(i + 1) * P, :]).then_inc(loaded_x, 16)
            for layer in range(2):
                e.dma_start(rb[64:80, layer, :, :], a["ada_b"][layer].rearrange("(p i d) -> i p d", i=16, d=P)).then_inc(loaded_bias, 16)
            e.dma_start(dpar[64:128, 0:1], a["ssd_dt_bias"][0].rearrange("d (h o) -> (d h) o", o=1)).then_inc(loaded_misc, 16)
            e.dma_start(dpar[64:128, 1:2], a["ssd_A_log"][0].rearrange("d (h o) -> (d h) o", o=1)).then_inc(loaded_misc, 16)
            for half in range(2):
                d_ = a["ssd_D"][0].rearrange("(c h) -> h c", h=2)[half:half + 1, :]
                e.dma_start(dcol[64 * half:64 * half + 64, :], d_.to_broadcast([64, 16]), allow_slow_non_contiguous=True).then_inc(loaded_misc, 16)
            e.wait_ge(vec_t, 1)
            e.activation(va[:], bank[7][:, 0:64], ACT.Copy)
            e.activation(vb[:], bank[7][:, 64:184], ACT.Copy).then_inc(vec_cols, 1)
            e.drain()
            e.activation(va[:, 48:64], va[:, 48:64], ACT.Silu)
            e.drain()
            e.wait_ge(cst_ready, 1)
            for kind in range(2):
                e.activation(csf[:, :, kind], va[:, 48 + 8 * kind:56 + 8 * kind], ACT.Copy)
                e.activation(cst[:, :, kind], va[:, 48 + 8 * kind:56 + 8 * kind], ACT.Copy).then_inc(vec_cols, 1)

            def rows_out(n):
                e.wait_ge(used, mod_at(2 * n + 1) + 1)
                p = n // 4
                if p >= 2 and n % 4 == 0:
                    e.wait_ge(mod_saved, 16 * (p - 1))
                e.activation(mrow[:, p % 2, (n % 4) * 512:(n % 4 + 1) * 512], bank[n % 2][0:4, :], ACT.Copy).then_inc(mod_row, 1)

            def fold_cols(n):
                e.wait_ge(fold_mm, n + 1)
                e.activation(mc[n // 3][:, n % 3].rearrange("p a b k -> p (a b k)"), bank[5][:, 0:32], ACT.Copy).then_inc(mc_ready, 1)

            def squares(k):
                e.activation(sq[:, :, k, :], ht[:, :, k, :], ACT.Square).then_inc(sq_ready, 1)

            def root(n):
                e.wait_ge(ms_ready, n + 1)
                e.activation(rstd[:], bank[MS_BANK[n]][:], ACT.Sqrt, bias=eps_col[:], scale=1.0 / D).then_inc(sd_ready, 1)

            def shifted_hi(n, k):
                pair, one, layer = ((1, 1, 0), (0, 0, 1))[n - 1]
                e.wait_ge(tn_ready, KD * (n - 1) + k + 1)
                for kind in range(2):
                    ins = e.activation(uh[:, k, kind * NTOK:(kind + 1) * NTOK], tn[:, kind, k, :], ACT.Identity,
                                       bias=mc[layer][:, pair, kind, one, k:k + 1])
                ins.then_inc(uh_ready, 1)

            split_hi(e, 0)
            for s in range(FFN0):
                split_hi(e, s + 1)
                if s < KD:
                    e.wait_ge(x_t, s + 1)
                    if s == 0:
                        e.wait_ge(vec_t, 1)
                    e.activation(ht[:, :, s, :], two(bank[2 + s % 2][:]), ACT.Copy).then_inc(x_copied, 1)
                    e.drain()
                    squares(s)
                if s == KD:
                    root(0)
                m = mod_no(s)
                if m is not None and m % 2 == 1 and m >= 3:
                    rows_out(m // 2 - 1)
                if s in (13, 21, 29, 39):
                    fold_cols((13, 21, 29, 39).index(s))
                if s in POOLED_AT:
                    g = POOLED_AT.index(s)
                    if g < 2:
                        e.wait_ge(pool_v, g + 1)
                    else:
                        e.wait_ge(pool_g, g - 1)
                    for k in (2 * g, 2 * g + 1):
                        split_u_hi(e, k)
                if s in (POOL0 + 1, POOL0 + 2):
                    for k in range(4 * (s - POOL0 - 1), 4 * (s - POOL0)):
                        e.wait_ge(pool_added, 2 * (k + 1))
                        squares(k)
                if s == POOL0 + 3:
                    root(1)
                if s in (NORM1_AT, NORM1_AT + 1):
                    for k in range(4 * (s - NORM1_AT), 4 * (s - NORM1_AT) + 4):
                        shifted_hi(1, k)
            rows_out(23)

            def ffn_acts(j, it, pick_silu):
                for c in range(2):
                    if pick_silu:
                        chunk_done(e, ffn_h1, w1_tile(j), j, c, it)
                        if j:
                            e.wait_ge(ffn_g, val(2 * (j - 1) + c + 1, 4, it))
                        e.activation(sg[:, c, :], bank[c][:], ACT.Silu).then_inc(ffn_silu, 1)
                    else:
                        e.wait_ge(ffn_g, val(2 * j + c + 1, 4, it))
                        e.activation(gh[:, j % 2, c, :], gf[:, c, :], ACT.Copy).then_inc(ffn_gh, 1)

            split_hi(e, FFN0 + 1)
            ffn_acts(0, None, True)
            split_hi(e, FFN0 + 2)
            ffn_acts(0, None, False)
            with e.Fori(0, FF_BLOCKS // 2) as it:
                for u in range(2):
                    j, k = 1 + u, FFN0 + 2 + 3 * u
                    split_hi(e, (k + 1, it))
                    split_hi(e, (k + 2, it))
                    ffn_acts(j, it, True)
                    split_hi(e, (k + 3, it))
                    ffn_acts(j, it, False)
            split_hi(e, IN0)
            for k in range(KD):
                e.wait_ge(ffn_added, KD * (FF_BLOCKS - 1) + k + 1)
                squares(k)
            root(2)
            for k in range(KD):
                shifted_hi(2, k)
            split_hi(e, in_tile(0, 0))
            R = slice(64, 128)
            e.wait_ge(loaded_misc, 64)
            e.wait_ge(used, IN0 + 1)
            e.activation(dts[R, 0, :], bank[0][R, :], ACT.Identity, bias=dpar[R, 0:1]).then_inc(in_taken, 1)
            e.activation(dpar[R, 2:3], dpar[R, 1:2], ACT.Exp).then_inc(dt_act, 1)
            split_hi(e, in_tile(0, 1))
            e.wait_ge(dt_steps, 1)
            e.activation(dts[R, 1, :], dts[R, 1, :], ACT.Exp, scale=-1.0).then_inc(dt_act, 1)
            e.wait_ge(dt_steps, 2)
            e.activation(dts[R, 3, :], dts[R, 2, :], ACT.Ln).then_inc(dt_act, 1)

            def take_aux(key):
                n = aux_no[key]
                what, g, i = key
                b = bank[2 + n % 2]
                e.wait_ge(aux_mm, n + 1)
                if what == "dt":
                    e.activation(dt_tok[:].rearrange("p t h -> p (t h)"), b[:, 0:256], ACT.Copy)
                    ins = e.activation(a_tok[:].rearrange("p t h -> p (t h)"), b[:, 256:512], ACT.Copy)
                elif what == "decay":
                    e.activation(wdec[:].rearrange("p t h -> p (t h)"), b[:, 0:256], ACT.Exp)
                    ins = e.activation(acs[:].rearrange("p t h -> p (t h)"), b[:, 256:384], ACT.Copy)
                elif what == "turn":
                    o = b_tok[:, g % 2] if i == 0 else xs_tok[:, g % 2, :, (i - 1) * P:i * P]
                    ins = e.activation(o, b[:].rearrange("p (t n) -> p t n", t=4), ACT.Copy)
                elif what == "cb":
                    ins = e.activation(cb[:, 0].rearrange("p c n -> p (c n)"), b[:, 0:256], ACT.Copy)
                elif what == "state":
                    ins = e.activation(states[:, i, :], b[:], ACT.Copy)
                elif what == "resid":
                    ins = e.activation(hl[:, i // 2, (i % 2) * 512:(i % 2 + 1) * 512], b[:], ACT.Copy)
                elif what == "mods":
                    ins = e.activation(mods[:, i // 2, (i % 2) * 512:(i % 2 + 1) * 512], b[:], ACT.Copy)
                elif what == "v":
                    ins = e.activation(vt[:, 4 * (i % 2):4 * (i % 2) + 4, (i // 2) * P:(i // 2 + 1) * P],
                                       b[:].rearrange("p (k n) -> p k n", k=4), ACT.Copy)
                ins.then_inc(aux_taken, 1)

            def take_in(g, j):
                for c in range(2):
                    if c == 0:
                        e.wait_ge(in_mm, 5 * g + j + 1)
                    else:
                        e.wait_ge(used, in_tile(g, j) + 1)
                    b = bank[in_chunk(g, j, c) % 2]
                    if j < 3:
                        v_ = 6 * g + 2 * j + c
                        if v_ >= 2:
                            e.wait_ge(conv_acc, v_ - 1)
                        n = 1 if (j, c) == (0, 1) else 2
                        e.activation(cp[:, v_ % 2, 0:n, 2:258], two(b[:])[:, 0:n, :], ACT.Copy).then_inc(in_taken, 1)
                    else:
                        e.activation(sz[:, g % 2, 2 * (j - 3) + c, :], b[:, 0:NTOK], ACT.Silu).then_inc(in_taken, 1)

            def conv_silu(g, j):
                q = g % 2
                for c in range(2):
                    v_ = 6 * g + 2 * j + c
                    e.wait_ge(conv_acc, v_ + 1)
                    o = (bt[:, q, :], ct[:, q, :])[c] if j == 0 else xst[:, q, 2 * (j - 1) + c, :]
                    ins = e.activation(o, cacc[:, v_ % 2, 0:NTOK], ACT.Silu)
                    if (j, c) != (0, 1):
                        ins = e.activation(ccv[:, c, :], cacc[:, v_ % 2, NTOK:], ACT.Silu)
                    ins.then_inc(conv_out, 1)

            def exps(g, u):
                n = 4 * g + u
                for d in range(2):
                    e.wait_ge(seg_ready, 2 * n + d + 1)
                    e.activation(seg[:, d, :], seg[:, d, :], ACT.Exp)
                    e.activation(csc[:, d, :], bank[4 + d][:], ACT.Exp).then_inc(exp_ready, 1)

            def y_hi(k0, k1):
                for k in range(k0, k1):
                    e.activation(yh[:, k, :], y2[:, k, :], ACT.Identity, scale=va[:, 32 + k:33 + k]).then_inc(yh_ready, 1)

            e.wait_ge(pads2, 1)
            for g in range(NG + 1):
                for j in range(5):
                    if (g, j) == (0, 0):
                        continue
                    if g < NG:
                        split_hi(e, in_tile(g, j) + 1)
                    elif j == 0:
                        split_hi(e, OUT0 + 1)
                    pg, pj = (g, j - 1) if j else (g - 1, 4)
                    if pg >= 0:
                        if pg < NG:
                            take_in(pg, pj)
                        if pj == 0:
                            for key in aux:
                                if key[0] in ("cb", "state") and key[1] == pg - 1:
                                    take_aux(key)
                        elif pj in (2, 3, 4) and pg < NG:
                            for i in {2: (0,), 3: (1, 2), 4: (3, 4)}[pj]:
                                take_aux(("turn", pg, i))
                        if pg >= 1 and pj < 4:
                            exps(pg - 1, pj)
                    if g < NG and j in (2, 3, 4):
                        conv_silu(g, j - 2)
                    if (g, j) == (0, 1):
                        take_aux(("dt", 0, 0))
                    if (g, j) == (0, 2):
                        take_aux(("decay", 0, 0))
                        e.drain().then_inc(wdec_ready, 1)
                    if g == NG and j in (1, 2, 3):
                        e.wait_ge(y_taken, 2 * j)
                        y_hi(4 * (j - 1), 4 * j)
                    if g == NG and j >= 2:
                        split_hi(e, OUT0 + j)
            e.wait_ge(y_taken, 2 * NG)
            y_hi(12, 16)
            for n in range(4):
                take_aux(("resid", 0, n))
            e.drain().then_inc(hl_ready, 1)
            split_hi(e, OUT0 + 5)
            e.wait_ge(rt_mm, 1)
            e.activation(ry[:, 0:2], bank[6][:, 0:2], ACT.Sqrt, bias=eps_col[:], scale=1.0 / DI).then_inc(ry_root, 1)
            for t in range(6, 8):
                split_hi(e, OUT0 + t)
            for n in range(8):
                take_aux(("mods", 0, n))
            e.drain().then_inc(mods_ready, 1)
            e.wait_ge(h_ready, 1)
            for t in range(2):
                e.activation(sq2[:], hl[:, t, :], ACT.Square, accum_out=stat[:, t:t + 1])
                e.drain()
            e.activation(stat[:, 2:4], stat[:, 0:2], ACT.Sqrt, bias=eps_col[:], scale=1.0 / D).then_inc(hsq_ready, 1)
            for n in range(4):
                take_aux(("v", 0, n))
            e.wait_ge(rt_dve, 1)
            for t in range(2):
                e.activation(gate[:, t, :], lg[:, t, :], ACT.Exp, bias=rsc[:, t:t + 1])
            e.drain().then_inc(rt_act, 1)

            def hi_of(k, i, b=None):
                if b is None:
                    e.wait_ge(landed2[k % RAW2], i * (16 * EB) + 16 * (k // RAW2 + 1) if i is not None else 16)
                else:
                    e.wait_ge(landed2[k % RAW2], i * (16 * EB) + b * 16 + 16 * (k // RAW2 + 1))
                e.wait_ge(used2, val2(k + 1, i, b, 6))
                e.activation(whi2[:, k % SPL2, :], raw2[:, k % RAW2, :], ACT.Copy).then_inc(hi2, 1)

            def silu_of(i, blk, b=None):
                e.activation(sge[:], bank[0][:], ACT.Silu).then_inc(silu2, 1)

            def gth_of(i, blk, b=None):
                e.wait_ge(turn_mm, val3(blk + 1, i, b))
                e.activation(gth[:].rearrange("p f n -> p (f n)"), bank[2][:], ACT.Copy).then_inc(gth_ready, 1)

            def xgh_of(n):
                e.wait_ge(gather_mm, n)
                for h in range(2):
                    ins = e.activation(xgh[:, 4 * h:4 * h + 4, :].rearrange("p k n -> p (k n)"), bank[5 + h][:], ACT.Copy)
                ins.then_inc(xgh_ready, 1)

            def block(i, k, blk, b=None):
                hi_of(k + 2, i, b)
                gth_of(i, blk - 1, b)
                hi_of(k + 3, i, b)
                hi_of(k + 4, i, b)
                silu_of(i, blk, b)
                for n in range(5, 8):
                    hi_of(k + n, i, b)

            hi_of(0, None)
            hi_of(1, None)
            xgh_of(1)
            e.wait_ge(tab_ready, 1)
            count = e.value_load(itab[0:1, 12:13], min_val=NE, max_val=MAX_ITEMS)
            with e.Fori(0, count) as i:
                hi_of(2, i)
                hi_of(3, i)
                hi_of(4, i)
                silu_of(i, 0)
                hi_of(5, i)
                e.wait_ge(put_mm, i + 1)
                e.activation(put[:].rearrange("p t n -> p (t n)"), bank[7][:, 0:256], ACT.Copy).then_inc(put_ready, 1)
                block(i, 4, 1)
                with e.Fori(0, EB - 2) as b:
                    block(i, 10, 2, b)
                hi_of(TPI, i)
                gth_of(i, EB - 1)
                xgh_of(i + 2)
                hi_of(TPI + 1, i)
                e.wait_ge(used2, i * TPI + (TPI + SPL2))
                for n in range(2):
                    ins = e.activation(osb[:, n * 512:(n + 1) * 512], bank[3 + n][:], ACT.Copy)
                ins.then_inc(osb_ready, 1)
            e.wait_ge(out_sq, 1)
            for t in range(2):
                e.activation(v[:, t, :], hl[:, t, :], ACT.Square, accum_out=stat[:, 8 + t:9 + t])
            e.drain()
            e.activation(stat[:, 10:12], stat[:, 8:10], ACT.Sqrt, bias=eps_col[:], scale=1.0 / D).then_inc(out_sq, 1)

        @block.vector
        def _(e):
            e.memset(csf[:], 0.0)
            e.memset(cst[:].bitcast(F32), 0.0).then_inc(cst_ready, 1)
            e.memset(win[:], 0.0)
            e.wait_ge(vec_cols, 3)
            for kind in range(2):
                e.tensor_tensor(cst[:, :, 2 + kind], va[:, 48 + 8 * kind:56 + 8 * kind],
                                cst[:, :, kind].bitcast(F32), ALU.subtract).then_inc(cst_ready, 1)

            def scales(i, layer, src_pair, src_one, w0, plus_one):
                for kind in range(2):
                    e.scalar_tensor_tensor(out=aff[:, i, kind, :], in0=mc[layer][:, src_pair, kind, src_one, :],
                                           scalar=1.0 if plus_one else 0.0, in1=va[:, w0:w0 + KD], op0=ALU.add, op1=ALU.mult)

            def inverse_root(n):
                e.wait_ge(sd_ready, n + 1)
                e.reciprocal(rstd[:], rstd[:])
                e.drain()

            def normalise(n):
                inverse_root(n)
                for k in range(KD):
                    e.tensor_tensor(tn[:, :, k, :], ht[:, :, k, :], two(rstd[:]), ALU.mult)
                e.drain()

            def modulated(i, layer, pair, one, write, chunks=range(KD)):
                for k in chunks:
                    for kind in range(2):
                        ins = write(k, kind, aff[:, i, kind, k:k + 1], mc[layer][:, pair, kind, one, k:k + 1])
                return ins

            def into_padded(k, kind, s, b):
                if kind == 0:
                    c0 = 8 + 4 * (GRID_W + 8)
                    o = padded[:, k, 8:c0].rearrange("p (r w) -> p r w", w=GRID_W + 8)[:, :, 0:GRID_W]
                    i_ = tn[:, 0, k, :].rearrange("p (r w) -> p r w", w=GRID_W)
                else:
                    o, i_ = padded[:, k, 8 + 4 * (GRID_W + 8):PADW - 8], tn[:, 1, k, :]
                return e.tensor_scalar(o, i_, s, b, ALU.mult, ALU.add)

            def scaled(n, k):
                for kind in range(2):
                    ins = e.scalar_tensor_tensor(out=tn[:, kind, k, :], in0=ht[:, kind, k, :], scalar=aff[:, n + 1, kind, k:k + 1],
                                                 in1=rstd[:, kind * NTOK:(kind + 1) * NTOK], op0=ALU.mult, op1=ALU.mult)
                ins.then_inc(tn_ready, 1)

            def shifted_lo(n, k):
                pair, one, layer = ((1, 1, 0), (0, 0, 1))[n - 1]
                e.wait_ge(uh_ready, KD * n + k + 1)
                for kind in range(2):
                    h = slice(kind * NTOK, (kind + 1) * NTOK)
                    ins = e.scalar_tensor_tensor(out=ul[:, k, h], in0=tn[:, kind, k, :], scalar=mc[layer][:, pair, kind, one, k:k + 1],
                                                 in1=uh[:, k, h].bitcast(F32), op0=ALU.add, op1=ALU.subtract)
                ins.then_inc(ul_ready, 1)

            split_lo(e, 0)
            for s in range(FFN0):
                split_lo(e, s + 1)
                if s == 9:
                    normalise(0)
                if s == 13:
                    e.wait_ge(mc_ready, 1)
                    scales(0, 0, 0, 1, 0, True)
                    e.drain()
                    e.wait_ge(pads_zero, 1)
                    modulated(0, 0, 0, 0, into_padded).then_inc(pad_ready, 1)
                    e.drain()
                if s in (15, 17):
                    pool_windows(e, (s - 15) // 2, win)
                    e.drain().then_inc(pool_v, 1)
                if s in POOLED_AT:
                    g = POOLED_AT.index(s)
                    if g == 2:
                        e.wait_ge(pool_g, 2)
                    for k in (2 * g, 2 * g + 1):
                        split_u_lo(e, k, 0)
                if s == 22:
                    e.wait_ge(mc_ready, 2)
                    scales(1, 0, 1, 0, 24, False)
                if s in (POOL0, POOL0 + 1):
                    for k in range(4 * (s - POOL0), 4 * (s - POOL0) + 4):
                        if k < KD - 1:
                            e.wait_ge(pool_mm, k + 1)
                        else:
                            e.wait_ge(used, POOL0 + 1)
                        for kind in range(2):
                            e.scalar_tensor_tensor(out=ht[:, kind, k, :], in0=bank[POOL_BANKS[k % 4]][:, kind * NTOK:(kind + 1) * NTOK],
                                                   scalar=aff[:, 1, kind, k:k + 1], in1=ht[:, kind, k, :],
                                                   op0=ALU.mult, op1=ALU.add).then_inc(pool_added, 1)
                if s == 30:
                    e.wait_ge(mc_ready, 3)
                    scales(2, 0, 2, 0, 16, True)
                if s == POOL0 + 4:
                    e.drain()
                    inverse_root(1)
                if s in (NORM1_AT - 1, NORM1_AT):
                    for k in range(4 * (s - NORM1_AT + 1), 4 * (s - NORM1_AT + 2)):
                        scaled(1, k)
                if s in (NORM1_AT + 1, NORM1_AT + 2):
                    for k in range(4 * (s - NORM1_AT - 1), 4 * (s - NORM1_AT)):
                        shifted_lo(1, k)
                if s == 40:
                    e.wait_ge(mc_ready, 4)
                    scales(3, 1, 0, 1, 8, True)
            e.drain()

            def ffn_g_of(j, it):
                for c in range(2):
                    chunk_done(e, ffn_h3, w1_tile(j) + 1, j, c, it)
                    e.wait_ge(ffn_silu, val(2 * j + c + 1, 4, it))
                    if j:
                        e.wait_ge(ffn_gh, val(2 * (j - 1) + c + 1, 4, it))
                    e.tensor_tensor(gf[:, c, :], sg[:, c, :], bank[2 + c][:], ALU.mult).then_inc(ffn_g, 1)

            def ffn_lo(j, it):
                for c in range(2):
                    e.wait_ge(ffn_gh, val(2 * j + c + 1, 4, it))
                    e.tensor_tensor(gl[:, j % 2, c, :], gf[:, c, :], gh[:, j % 2, c, :].bitcast(F32),
                                    ALU.subtract).then_inc(ffn_gl, 1)

            def ffn_add(j, it, ks):
                for k in ks:
                    if k < KD - 1:
                        e.wait_ge(ffn_out, val(7 * j + k + 1, 14, it))
                    else:
                        e.wait_ge(used, val(w2_tile(j) + 1, 6, it))
                    for kind in range(2):
                        ins = e.scalar_tensor_tensor(out=ht[:, kind, k, :], in0=bank[4 + k % 4][:, kind * NTOK:(kind + 1) * NTOK],
                                                     scalar=mc[0][:, 2, kind, 1, k:k + 1], in1=ht[:, kind, k, :],
                                                     op0=ALU.mult, op1=ALU.add)
                    ins.then_inc(ffn_added, 1)

            split_lo(e, FFN0 + 1)
            split_lo(e, FFN0 + 2)
            ffn_g_of(0, None)
            e.drain()
            ffn_lo(0, None)
            with e.Fori(0, FF_BLOCKS // 2) as it:
                for u in range(2):
                    j, k = 1 + u, FFN0 + 2 + 3 * u
                    split_lo(e, (k + 1, it))
                    split_lo(e, (k + 2, it))
                    e.drain()
                    split_lo(e, (k + 3, it))
                    ffn_g_of(j, it)
                    ffn_add(j - 1, it, range(4))
                    e.drain()
                    ffn_lo(j, it)
                    ffn_add(j - 1, it, range(4, 8))
            e.drain()
            ffn_add(FF_BLOCKS - 1, None, range(8))
            e.drain()
            split_lo(e, IN0)
            inverse_root(2)
            for k in range(KD + 2):
                if k < KD:
                    scaled(2, k)
                if k >= 2:
                    shifted_lo(2, k - 2)
            split_lo(e, in_tile(0, 0))
            R = slice(64, 128)
            e.wait_ge(dt_act, 1)
            e.wait_ge(in_taken, 1)
            e.scalar_tensor_tensor(out=dts[R, 1, :], in0=dts[R, 0, :], scalar=-1.0, in1=dts[R, 0, :], op0=ALU.mult, op1=ALU.max).then_inc(dt_steps, 1)
            split_lo(e, in_tile(0, 1))
            e.wait_ge(dt_act, 2)
            e.tensor_scalar(dts[R, 2, :], dts[R, 1, :], 1.0, None, ALU.add).then_inc(dt_steps, 1)
            e.wait_ge(dt_act, 3)
            e.tensor_scalar(dts[R, 2, :], dts[R, 2, :], -1.0, None, ALU.add)
            e.drain()
            e.tensor_scalar(dts[R, 4, :], dts[R, 2, :], 0.0, None, ALU.is_equal)
            e.drain()
            e.tensor_tensor(dts[R, 2, :], dts[R, 2, :], dts[R, 4, :], ALU.add)
            e.tensor_tensor(dts[R, 3, :], dts[R, 3, :], dts[R, 4, :], ALU.add)
            e.drain()
            e.reciprocal(dts[R, 2, :], dts[R, 2, :])
            e.drain()
            e.tensor_tensor(dts[R, 3, :], dts[R, 3, :], dts[R, 2, :], ALU.mult)
            e.drain()
            e.tensor_tensor(dts[R, 3, :], dts[R, 3, :], dts[R, 1, :], ALU.mult)
            e.drain()
            e.scalar_tensor_tensor(out=dts[R, 0, :], in0=dts[R, 0, :], scalar=0.0, in1=dts[R, 3, :], op0=ALU.max, op1=ALU.add)
            e.drain()
            e.tensor_scalar(dts[R, 1, :], dts[R, 0, :], dpar[R, 2:3], -1.0, ALU.mult, ALU.mult)
            e.drain().then_inc(a_ready, 1)

            def conv(g, j):
                for c in range(2):
                    v_ = 6 * g + 2 * j + c
                    ch = 16 + 4 * c + g if j == 0 else 4 * g + 2 * (j - 1) + c
                    n = 1 if (j, c) == (0, 1) else 2
                    e.wait_ge(in_taken, in_chunk(g, j, c) + 1)
                    if v_ >= 2:
                        e.wait_ge(conv_out, v_ - 1)
                    src = lambda k: cp[:, v_ % 2, 0:n, k:k + NTOK]
                    o = two(cacc[:, v_ % 2, :])[:, 0:n, :]
                    e.tensor_scalar(o, src(0), vb[:, ch:ch + 1], vb[:, 96 + ch:97 + ch], ALU.mult, ALU.add)
                    for k in range(1, 4):
                        e.drain()
                        ins = e.scalar_tensor_tensor(out=o, in0=src(k), scalar=vb[:, 24 * k + ch:24 * k + ch + 1], in1=o,
                                                     op0=ALU.mult, op1=ALU.add)
                    ins.then_inc(conv_acc, 1)

            def segs(g, u):
                c, q4 = u // 2, u % 2
                n = 4 * g + u
                for d in range(2):
                    e.wait_ge(bc_mm, 2 * n + d + 1)
                    for h in range(4):
                        hh = HPG * g + 4 * q4 + h
                        ins = e.tensor_scalar(seg[:, d, h * P:(h + 1) * P], bank[4 + d][:, h * P:(h + 1) * P],
                                              acs[:, 2 * d + c, hh:hh + 1], 0.0, ALU.subtract, ALU.min)
                    ins.then_inc(seg_ready, 1)

            def mixes(g, u):
                c = u // 2
                n = 4 * g + u
                f4 = lambda x: x.rearrange("p (h n) -> p h n", h=4)
                for d in range(2):
                    e.wait_ge(exp_ready, 2 * n + d + 1)
                    e.tensor_tensor(f4(seg[:, d, :]), f4(seg[:, d, :]), cb[:, d, c, :].unsqueeze(1).to_broadcast([P, 4, P]), ALU.mult)
                    e.tensor_tensor(f4(csc[:, d, :]), f4(csc[:, d, :]),
                                    ct[:, g % 2, c * P:(c + 1) * P].unsqueeze(1).to_broadcast([P, 4, P]), ALU.mult)
                e.drain().then_inc(mix_ready, 1)

            def masks(g):
                e.wait_ge(aux_taken, aux_no[("cb", g, 0)] + 1)
                for c in range(2):
                    e.tensor_tensor(cb[:, 1, c, :], cb[:, 0, c, :], tri_ge[:], ALU.mult)
                e.drain()
                for c in range(2):
                    e.tensor_tensor(cb[:, 0, c, :], cb[:, 0, c, :], tri_le[:], ALU.mult)
                e.wait_ge(aux_taken, aux_no[("state", g, 3)] + 1)
                hv = lambda x: x.rearrange("p (h c) -> p h c", c=64)
                for d in range(2):
                    e.tensor_tensor(hv(csc[:, d, :]), hv(states[:, d, :]),
                                    wdec[:, 6 + d, HPG * g:HPG * g + HPG].unsqueeze(2).to_broadcast([P, HPG, 64]), ALU.mult)
                e.drain()
                for d in range(2):
                    e.tensor_tensor(states[:, 2 + d, :], states[:, 2 + d, :], csc[:, d, :], ALU.add)
                e.drain().then_inc(st_ready, 1)

            def y_out(g, c):
                e.wait_ge(y_mm, 4 * g + 2 * c + 2)
                q = g % 2
                for i in range(4):
                    k = 4 * g + i
                    e.scalar_tensor_tensor(out=y2[:, k, c * P:(c + 1) * P], in0=xst[:, q, i, c * P:(c + 1) * P], scalar=dcol[:, k:k + 1],
                                           in1=bank[6 + c][:, i * P:(i + 1) * P], op0=ALU.mult, op1=ALU.add)
                e.drain()
                o = y2[:, 4 * g:4 * g + 4, c * P:(c + 1) * P]
                e.tensor_tensor(o, o, sz[:, q, :, c * P:(c + 1) * P], ALU.mult).then_inc(y_taken, 1)

            def y_lo(k0, k1):
                for k in range(k0, k1):
                    e.wait_ge(yh_ready, k + 1)
                    e.scalar_tensor_tensor(out=yl[:, k, :], in0=y2[:, k, :], scalar=va[:, 32 + k:33 + k], in1=yh[:, k, :].bitcast(F32),
                                           op0=ALU.mult, op1=ALU.subtract).then_inc(yl_ready, 1)

            e.wait_ge(pads2, 1)
            for g in range(NG + 1):
                for j in range(5):
                    if (g, j) == (0, 0):
                        continue
                    if g < NG:
                        split_lo(e, in_tile(g, j) + 1)
                    elif j == 0:
                        split_lo(e, OUT0 + 1)
                    pg, pj = (g, j - 1) if j else (g - 1, 4)
                    if pg >= 1 and pj == 0:
                        masks(pg - 1)
                    if pg >= 1 and pj < 4:
                        segs(pg - 1, pj)
                    if pg < NG and 0 <= pj < 3 and pg >= 0:
                        conv(pg, pj)
                    if (g, j) == (0, 2):
                        e.wait_ge(wdec_ready, 1)
                        for n, (tile, d) in enumerate(((2, 0), (2, 1), (3, 0), (3, 1), (0, 0), (1, 1))):
                            e.tensor_tensor(wdec[:, n, :], wdec[:, n, :], dt_tok[:, tile, 32 * d:32 * d + 32], ALU.mult)
                        e.drain().then_inc(wdec_ready, 1)
                    if pg >= 1 and pj < 4:
                        mixes(pg - 1, pj)
                    if pg >= 1 and pj in (2, 4):
                        y_out(pg - 1, pj // 2 - 1)
                    if g == NG and j in (1, 2, 3):
                        y_lo(4 * (j - 1), 4 * j)
                    if g == NG and j >= 2:
                        split_lo(e, OUT0 + j)
            e.drain()
            y_out(NG - 1, 1)
            y_lo(12, 16)
            for t in range(5, 8):
                if t == 6:
                    e.wait_ge(ry_root, 1)
                    e.reciprocal(ry[:, 2:4], ry[:, 0:2])
                split_lo(e, OUT0 + t)
            e.drain().then_inc(lo2, 3)
            e.wait_ge(mods_ready, 1)
            e.wait_ge(hl_ready, 1)
            e.wait_ge(rows_back, 6 * 16)
            e.scalar_tensor_tensor(out=mods[:, 2, :], in0=mods[:, 2, :], scalar=1.0, in1=nfw[:], op0=ALU.add, op1=ALU.mult)
            for n in range(2):
                e.wait_ge(used, OUT0 + 4 * n + 4)
                for t in range(2):
                    s = slice(n * 512, (n + 1) * 512)
                    e.scalar_tensor_tensor(out=v[:, t, s], in0=bank[4 * n + t][:], scalar=ry[:, 2 + t:3 + t], in1=mods[:, 0, s],
                                           op0=ALU.mult, op1=ALU.mult)
                    e.drain()
                    e.tensor_tensor(hl[:, t, s], hl[:, t, s], v[:, t, s], ALU.add)
            e.drain().then_inc(h_ready, 1)
            e.wait_ge(hsq_ready, 1)
            e.reciprocal(stat[:, 4:6], stat[:, 2:4])
            e.drain()
            for t in range(2):
                e.scalar_tensor_tensor(out=v[:, t, :], in0=hl[:, t, :], scalar=stat[:, 4 + t:5 + t], in1=mods[:, 2, :],
                                       op0=ALU.mult, op1=ALU.mult)
                e.drain()
                e.tensor_tensor(v[:, t, :], v[:, t, :], mods[:, 1, :], ALU.add)
            e.drain().then_inc(v_ready, 1)
            e.memset(acc[:], 0.0)
            e.wait_ge(lg_mm, 1)
            e.tensor_copy(lg[:].rearrange("p t x -> p (t x)"), bank[6][:, 16:32])
            e.drain()
            for t in range(2):
                own = lg[:, t, :].unsqueeze(2).to_broadcast([P, NE, NE])
                other = lg[:, t, :].unsqueeze(1).to_broadcast([P, NE, NE])
                e.tensor_tensor(cmp[:, t], other, own, ALU.is_gt)
                e.tensor_tensor(eqs[:, t], other, own, ALU.is_equal)
                e.drain()
                e.tensor_tensor(eqs[:, t], eqs[:, t], before[:], ALU.mult)
                e.drain()
                e.tensor_tensor(cmp[:, t], cmp[:, t], eqs[:, t], ALU.add)
                e.drain()
                e.tensor_reduce(sel[:, t, :], cmp[:, t], AX_X, ALU.add)
                e.tensor_reduce(rsc[:, 2 + t:3 + t], lg[:, t, :], AX_X, ALU.max)
                e.drain()
                e.tensor_scalar(sel[:, t, :], sel[:, t, :], 1.5, None, ALU.is_lt)
                e.tensor_scalar(rsc[:, t:t + 1], rsc[:, 2 + t:3 + t], -1.0, None, ALU.mult)
            e.drain().then_inc(rt_dve, 1)
            e.wait_ge(rt_act, 1)
            for t in range(2):
                e.tensor_tensor(gate[:, t, :], gate[:, t, :], sel[:, t, :], ALU.mult)
                e.drain()
                e.tensor_reduce(rsc[:, 4 + t:5 + t], gate[:, t, :], AX_X, ALU.add)
                e.drain()
                e.reciprocal(rsc[:, 6 + t:7 + t], rsc[:, 4 + t:5 + t])
                e.drain()
                e.tensor_scalar(gate[:, t, :], gate[:, t, :], rsc[:, 6 + t:7 + t], None, ALU.mult)
            e.wait_ge(rt_mm, 2)
            for t in range(2):
                e.scalar_tensor_tensor(out=pos[:, t, :], in0=bank[6][:, 32 + 8 * t:40 + 8 * t], scalar=1.0, in1=sel[:, t, :],
                                       op0=ALU.add, op1=ALU.mult)
            e.tensor_copy(cnt[:], bank[6][:, 48:56])
            e.drain()
            e.tensor_scalar(over[:], cnt[:], float(P), None, ALU.is_gt)
            e.memset(pos_item[:], -1.0)
            e.memset(gate_item[:], 0.0)
            e.memset(ftab[:], 0.0)
            e.drain()
            e.tensor_tensor(cmp[:, 0], over[:].unsqueeze(1).to_broadcast([P, NE, NE]), before[:], ALU.mult)
            e.tensor_reduce(rsc[:, 8:9], over[:], AX_X, ALU.add)
            e.drain()
            e.tensor_reduce(rsc[:, 12:13], over[:], AX_X, ALU.add)
            e.tensor_reduce(cnt[:], cmp[:, 0], AX_X, ALU.add)
            e.drain()
            for m in range(3):
                e.scalar_tensor_tensor(out=more[:, m, :], in0=cnt[:], scalar=float(m), in1=over[:], op0=ALU.is_equal, op1=ALU.mult)
            e.drain()
            bc3 = lambda x: x.unsqueeze(1).to_broadcast([P, 3, NE])
            e.tensor_tensor(tmp3[:], more[:], bc3(expert_id[:]), ALU.mult)
            e.drain()
            e.tensor_copy(ftab[:, 0:NE], expert_id[:])
            e.tensor_reduce(ftab[:, NE:NE + 3], tmp3[:], AX_X, ALU.add)
            e.tensor_scalar(ftab[:, 12:13], rsc[:, 8:9], float(NE), None, ALU.add)
            e.drain()
            e.tensor_copy(itab[:], ftab[0:1, :])
            e.drain().then_inc(tab_ready, 1)
            for t in range(2):
                e.tensor_scalar(pos_item[:, t, 0:NE], pos[:, t, :], -1.0, None, ALU.add)
                e.tensor_copy(gate_item[:, t, 0:NE], gate[:, t, :])
                e.scalar_tensor_tensor(out=tmp3[:], in0=bc3(pos[:, t, :]), scalar=-float(P), in1=more[:], op0=ALU.add, op1=ALU.mult)
                e.drain()
                e.tensor_reduce(pos_item[:, t, NE:NE + 3], tmp3[:], AX_X, ALU.add)
                e.drain()
                e.tensor_scalar(pos_item[:, t, NE:NE + 3], pos_item[:, t, NE:NE + 3], -1.0, None, ALU.add)
                e.tensor_tensor(tmp3[:], bc3(gate[:, t, :]), more[:], ALU.mult)
                e.drain()
                e.tensor_reduce(gate_item[:, t, NE:NE + 3], tmp3[:], AX_X, ALU.add)
                e.drain()

            def pick_of(col):
                for t in range(2):
                    e.tensor_scalar(pick[:, t, :], slot_id[:], pos_item[:, t, col], None, ALU.is_equal)
                    e.tensor_scalar(pickg[:, t, :], slot_id[:], pos_item[:, t, col], gate_item[:, t, col], ALU.is_equal, ALU.mult)

            pick_of(slice(0, 1))
            e.drain().then_inc(pick_ready, 1)
            e.wait_ge(used, NTILES)
            e.drain().then_inc(lo2, 3)
            e.drain().then_inc(acc_added, 1)

            def lo_of(k, i, b=None):
                e.wait_ge(hi2, val2(k + 1, i, b, 6))
                e.tensor_tensor(wlo2[:, k % SPL2, :], raw2[:, k % RAW2, :], whi2[:, k % SPL2, :].bitcast(F32),
                                ALU.subtract).then_inc(lo2, 1)

            def gm_of(i, blk, b=None):
                e.wait_ge(silu2, val3(blk + 1, i, b))
                e.tensor_tensor(gme[:], sge[:], bank[1][:], ALU.mult).then_inc(gm_ready, 1)

            def gtl_of(i, blk, b=None):
                e.wait_ge(gth_ready, val3(blk + 1, i, b))
                e.tensor_tensor(gtl[:].rearrange("p f n -> p (f n)"), bank[2][:], gth[:].bitcast(F32).rearrange("p f n -> p (f n)"),
                                ALU.subtract).then_inc(gtl_ready, 1)

            def xgl_of(n):
                e.wait_ge(xgh_ready, n)
                for h in range(2):
                    ins = e.tensor_tensor(xgl[:, 4 * h:4 * h + 4, :].rearrange("p k n -> p (k n)"), bank[5 + h][:],
                                          xgh[:, 4 * h:4 * h + 4, :].bitcast(F32).rearrange("p k n -> p (k n)"), ALU.subtract)
                ins.then_inc(xgl_ready, 1)

            def block(i, k, blk, b=None):
                lo_of(k + 2, i, b)
                gtl_of(i, blk - 1, b)
                for n in range(3, 7):
                    lo_of(k + n, i, b)
                gm_of(i, blk, b)
                lo_of(k + 7, i, b)

            lo_of(0, None)
            lo_of(1, None)
            xgl_of(1)
            count = e.value_load(itab[0:1, 12:13], min_val=NE, max_val=MAX_ITEMS)
            with e.Fori(0, count) as i:
                for k in (2, 3, 4, 5):
                    lo_of(k, i)
                e.wait_ge(used2, i * TPI + (4 + SPL2))
                gm_of(i, 0)
                block(i, 4, 1)
                e.wait_ge(put_ready, i + 1)
                pick_of(bass.ds(i + 1, 1))
                e.drain().then_inc(pick_ready, 1)
                with e.Fori(0, EB - 2) as b:
                    block(i, 10, 2, b)
                lo_of(TPI, i)
                gtl_of(i, EB - 1)
                xgl_of(i + 2)
                lo_of(TPI + 1, i)
                for n, bk in enumerate((7, 2, 3, 4)):
                    t, h = n // 2, n % 2
                    e.wait_ge(scat_mm, i * 4 + (n + 1))
                    o = acc[:, t, h * 512:(h + 1) * 512]
                    e.tensor_tensor(o, o, bank[bk][:], ALU.add).then_inc(acc_added, 1)
                e.drain()
            for t in range(2):
                e.tensor_tensor(acc[:, t, :], acc[:, t, :], mods[:, 3, :], ALU.mult)
                e.drain()
                e.tensor_tensor(hl[:, t, :], hl[:, t, :], acc[:, t, :], ALU.add)
            e.drain().then_inc(out_sq, 1)
            e.wait_ge(out_sq, 2)
            e.reciprocal(stat[:, 12:14], stat[:, 10:12])
            e.drain()
            for t in range(2):
                e.scalar_tensor_tensor(out=acc[:, t, :], in0=hl[:, t, :], scalar=stat[:, 12 + t:13 + t], in1=fnw[:],
                                       op0=ALU.mult, op1=ALU.mult).then_inc(out_ready, 1)

        @block.tensor
        def _(e):
            def passes(o, wsl, usl, first, last):
                ins = None
                for n, (i, j) in enumerate(((0, 0), (0, 1), (1, 0))):
                    ins = e.matmul(o, wsl[i], usl[j], start=first and n == 0, stop=last and n == 2)
                return ins

            def wpart(s, view):
                return view(whi[:, s, :]), view(wlo[:, s, :])

            e.wait_ge(loaded_vec, 9 * 16)
            e.wait_ge(consts_ready, 1)
            e.transpose(bank[7][:, 0:64], rows_in[0:64, 0, :], ident[0:64, 0:64])
            e.transpose(bank[7][:, 64:184], rows_in[0:120, 1, :], ident[0:120, 0:120]).then_inc(vec_t, 1)
            e.wait_ge(cst_ready, 3)

            def mod_tile(m):
                s, plain = mod_at(m), mod_at(m) in PLAIN
                n, kh = m // 2, m % 2
                if plain:
                    e.wait_ge(landed[s % RAW1], 16 * (s // RAW1 + 1))
                else:
                    s = w_ready(e, s)
                if kh == 0 and n >= 2:
                    e.wait_ge(mod_row, n - 1)
                for k in range(4):
                    if plain:
                        ins = e.matmul(bank[n % 2][0:4, :], csf[:, 4 * kh + k, :], raw[:, s % RAW1, k * 512:(k + 1) * 512],
                                       start=kh == 0 and k == 0, stop=kh == 1 and k == 3)
                        continue
                    for i, part in enumerate((whi, wlo)):
                        ins = e.matmul(bank[n % 2][:], cst[:, 4 * kh + k, :], part[:, s, k * 512:(k + 1) * 512],
                                       start=kh == 0 and k == 0 and i == 0, stop=kh == 1 and k == 3 and i == 1)
                ins.then_inc(used, 1)

            def fold_pair(n):
                e.wait_ge(mod_back, 16 * (n + 1))
                e.wait_ge(loaded_bias, 32)
                if n:
                    e.wait_ge(mc_ready, n)
                e.matmul(bank[5][:, 0:32], rb[:, n // 3, n % 3, :], fold[:], start=True, stop=True).then_inc(fold_mm, 1)

            def mean_square(n):
                for k in range(KD):
                    e.wait_ge(sq_ready, KD * n + k + 1)
                    ins = e.matmul(bank[MS_BANK[n]][:], ones[:], sq[:, :, k, :], start=k == 0, stop=k == KD - 1)
                ins.then_inc(ms_ready, 1)

            for s in range(FFN0):
                if s == POOL0:
                    t = w_ready(e, POOL0)
                    e.wait_ge(x_copied, KD)
                    for g in range(4):
                        e.wait_ge(ul_ready, 2 * g + 2)
                        for o in range(2):
                            if g >= 2:
                                e.wait_ge(pool_added, 2 * (2 * g + o - 3))
                            for i in range(2):
                                ins = passes(bank[POOL_BANKS[(2 * g + o) % 4]][:],
                                             wpart(t, lambda w: w[:, (2 * g + i) * 256 + o * P:(2 * g + i) * 256 + (o + 1) * P]),
                                             (uh[:, 2 * g + i, :], ul[:, 2 * g + i, :]), i == 0, i == 1)
                            ins.then_inc(used if (g, o) == (3, 1) else pool_mm, 1)
                else:
                    mod_tile(mod_no(s))
                if s < KD:
                    if s == 0:
                        e.wait_ge(loaded_x, 64)
                    if s >= 2:
                        e.wait_ge(x_copied, s - 1)
                    for i in range(4):
                        ins = e.transpose(bank[2 + s % 2][:, i * P:(i + 1) * P], xtok[:, i, s * P:(s + 1) * P], ident[:])
                    ins.then_inc(x_t, 1)
                if s == KD:
                    e.wait_ge(consts_ready, 2)
                    mean_square(0)
                if s in (12, 20, 28, 38):
                    fold_pair((12, 20, 28, 38).index(s))
                if s == POOL0 + 3:
                    mean_square(1)
            e.wait_ge(mod_row, 24)
            e.wait_ge(mc_ready, 4)
            e.wait_ge(ul_ready, 2 * KD)

            def hidden(t, b0, j, it, free):
                s = w_ready(e, t)
                for c in range(2):
                    if j:
                        e.wait_ge(free, val(2 * (j - 1) + c + 1, 4, it))
                    for k in range(KD):
                        ins = passes(bank[b0 + c][:], wpart(s, lambda w: w[:, k * 256 + c * P:k * 256 + (c + 1) * P]),
                                     (uh[:, k, :], ul[:, k, :]), k == 0, k == KD - 1)
                    ins.then_inc(used if c else (ffn_h3 if b0 else ffn_h1), 1)

            def down(t, j, it):
                s = w_ready(e, t)
                e.wait_ge(ffn_gl, val(2 * j + 2, 4, it))
                for k in range(KD):
                    if 8 * j + k >= 4:
                        e.wait_ge(ffn_added, val(8 * j + k - 3, 16, it))
                    for i in range(2):
                        ins = passes(bank[4 + k % 4][:], wpart(s, lambda w: w[:, i * D + k * P:i * D + (k + 1) * P]),
                                     (gh[:, j % 2, i, :], gl[:, j % 2, i, :]), i == 0, i == 1)
                    ins.then_inc(used if k == KD - 1 else ffn_out, 1)

            hidden(FFN0, 0, 0, None, ffn_silu)
            hidden(FFN0 + 1, 2, 0, None, ffn_g)
            with e.Fori(0, FF_BLOCKS // 2) as it:
                for u in range(2):
                    j, k = 1 + u, FFN0 + 2 + 3 * u
                    hidden((k, it), 0, j, it, ffn_silu)
                    hidden((k + 1, it), 2, j, it, ffn_g)
                    down((k + 2, it), j - 1, it)
            down(IN0 - 1, FF_BLOCKS - 1, None)
            e.wait_ge(ffn_g, 2 * FF_BLOCKS)
            mean_square(2)
            def project(t, c0, q, n, done):
                s = w_ready(e, t)
                if q >= 2:
                    e.wait_ge(in_taken, q - 1)
                for k in range(KD):
                    if q == 0:
                        e.wait_ge(ul_ready, 2 * KD + k + 1)
                    ins = passes(bank[q % 2][:, 0:n], wpart(s, lambda w: w[:, k * 256 + c0:k * 256 + c0 + P]),
                                 (uh[:, k, 0:n], ul[:, k, 0:n]), k == 0, k == KD - 1)
                ins.then_inc(done, 1)

            def aux_bank(key):
                n = aux_no[key]
                if n >= 2:
                    e.wait_ge(aux_taken, n - 1)
                return bank[2 + n % 2]

            project(IN0, P, 0, NT2, used)
            def dt_by_tokens():
                e.wait_ge(a_ready, 1)
                b = aux_bank(("dt", 0, 0))
                for i in range(2):
                    for t in range(4):
                        ins = e.transpose(b[:, i * 256 + t * 64:i * 256 + (t + 1) * 64], dts[64:128, i, t * P:(t + 1) * P], ident[64:128, 64:128])
                ins.then_inc(aux_mm, 1)

            def decay_sums():
                b = aux_bank(("decay", 0, 0))
                e.wait_ge(aux_taken, 1)
                F, B = slice(0, 32), slice(32, 64)
                sums = [[(tri_gt, 2, F), (ones, 3, F)], [(tri_lt, 2, B)], [(tri_gt, 3, F)], [(tri_lt, 3, B), (ones, 2, B)],
                        [(tri_gt, 0, F)], [(tri_lt, 1, B)], [(ones, 0, F)], [(ones, 1, B)],
                        [(tri_le, 0, F)], [(tri_le, 1, F)], [(tri_ge, 0, B)], [(tri_ge, 1, B)]]
                for n, terms in enumerate(sums):
                    for i, (w, t, s) in enumerate(terms):
                        ins = e.matmul(b[:, n * 32:(n + 1) * 32], w[:], a_tok[:, t, s], start=i == 0, stop=i == len(terms) - 1)
                ins.then_inc(aux_mm, 1)

            def turn(g, i):
                v_ = 6 * g + (0 if i == 0 else i + 1)
                b = aux_bank(("turn", g, i))
                e.wait_ge(conv_out, v_ + 1)
                lat = bt[:, g % 2, :] if i == 0 else xst[:, g % 2, i - 1, :]
                con = ccv[:, v_ % 2, :]
                for t in range(4):
                    src = lat[:, t * P:(t + 1) * P] if t < 2 else con[:, (t - 2) * P:(t - 1) * P]
                    ins = e.transpose(b[:, t * P:(t + 1) * P], src, ident[:])
                ins.then_inc(aux_mm, 1)

            def group_states(g):
                q = g % 2
                b = aux_bank(("cb", g, 0))
                for c in range(2):
                    s = slice(c * P, (c + 1) * P)
                    ins = e.matmul(b[:, s], bt[:, q, s], ct[:, q, s], start=True, stop=True)
                ins.then_inc(aux_mm, 1)
                for i, terms in enumerate((((2, 0), (3, 1)), ((2, 2), (3, 3)), ((0, 4),), ((1, 5),))):
                    b = aux_bank(("state", g, i))
                    for n, (t, m) in enumerate(terms):
                        e.wait_ge(xdd_ready, 6 * g + m + 1)
                        ins = e.matmul(b[:], b_tok[:, q, t, :], xdd[m % 2][:], start=n == 0, stop=n == len(terms) - 1)
                    ins.then_inc(aux_mm, 1)

            def cumulative(g, u):
                c, q4 = u // 2, u % 2
                for d, tri in enumerate((tri_le, tri_ge)):
                    for h in range(4):
                        hh = 32 * d + HPG * g + 4 * q4 + h
                        ins = e.matmul(bank[4 + d][:, h * P:(h + 1) * P], a_tok[:, c, hh:hh + 1].to_broadcast([P, P]), tri[:],
                                       start=True, stop=True)
                    ins.then_inc(bc_mm, 1)

            def heads(g, u):
                c, q4 = u // 2, u % 2
                n = 4 * g + u
                if q4 == 0 and g:
                    e.wait_ge(y_taken, 2 * (g - 1) + c + 1)
                e.wait_ge(xd_ready, 4 * (g + 1))
                e.wait_ge(st_ready, g + 1)
                e.wait_ge(mix_ready, n + 1)
                for h in range(4):
                    hg = 4 * q4 + h
                    o = bank[6 + c][64 * (h % 2):64 * (h % 2) + 64, (hg // 2) * P:(hg // 2 + 1) * P]
                    hs, ms = slice(hg * 64, hg * 64 + 64), slice(h * P, (h + 1) * P)
                    st = (0 if c == 0 else 2, 3 if c == 0 else 1)
                    for d in range(2):
                        e.matmul(o, xd[:, d, c, hs], seg[:, d, ms], start=d == 0, stop=False)
                    for d in range(2):
                        ins = e.matmul(o, states[:, st[d], hs], csc[:, d, ms], start=False, stop=d == 1)
                ins.then_inc(y_mm, 1)

            def out_tile(n, kq):
                s = w_ready(e, OUT0 + 4 * n + kq)
                e.wait_ge(yl_ready, 4 * (kq + 1))
                if (n, kq) == (0, 0):
                    e.wait_ge(in_taken, 1 + 10 * NG)
                for t in range(2):
                    for k in range(4):
                        ts = slice(t * P, (t + 1) * P)
                        c = 4 * kq + k
                        ins = passes(bank[4 * n + t][:], (yh[:, c, ts], yl[:, c, ts]),
                                     wpart(s, lambda w: w[:, k * 512:(k + 1) * 512]), kq == 0 and k == 0, kq == 3 and k == 3)
                ins.then_inc(used, 1)

            for g in range(NG + 1):
                for j in range(5):
                    if g < NG:
                        for c in range(2):
                            z_or_c = j >= 3 or (j, c) == (0, 1)
                            project(in_tile(g, j), c * P, in_chunk(g, j, c), NTOK if z_or_c else NT2, used if c else in_mm)
                    if (g, j) == (0, 0):
                        dt_by_tokens()
                    if (g, j) == (0, 1):
                        decay_sums()
                    if g and j == 0:
                        group_states(g - 1)
                    if g and j:
                        heads(g - 1, j - 1)
                    if g and j < 4:
                        cumulative(g - 1, j)
                    if g < NG and j >= 2:
                        for i in {2: (0,), 3: (1, 2), 4: (3, 4)}[j]:
                            turn(g, i)
                    if g == NG and 1 <= j <= 3:
                        out_tile(0, j - 1)
            for n in range(4):
                b = aux_bank(("resid", 0, n))
                t, half = n // 2, n % 2
                for k in range(4):
                    ins = e.transpose(b[:, k * P:(k + 1) * P], ht[:, 0, 4 * half + k, t * P:(t + 1) * P], ident[:])
                ins.then_inc(aux_mm, 1)
            for n, kq in [(0, 3)] + [(1, kq) for kq in range(4)]:
                out_tile(n, kq)
                if (n, kq) == (0, 3):
                    e.wait_ge(ysum_ready, 1)
                    for t in range(2):
                        ins = e.matmul(bank[6][:, t:t + 1], ysum[:, t * P:(t + 1) * P], ones[:, 0:1], start=True, stop=True)
                    ins.then_inc(rt_mm, 1)
            e.wait_ge(rows_back, 6 * 16)
            for i in range(8):
                b = aux_bank(("mods", 0, i))
                e.matmul(b[:], sel_row[:], mrow5[:, i // 2, (i % 2) * 512:(i % 2 + 1) * 512], start=True, stop=True).then_inc(aux_mm, 1)
            e.wait_ge(v_ready, 1)
            for n in range(4):
                b = aux_bank(("v", 0, n))
                t, half = n // 2, n % 2
                for k in range(4):
                    ins = e.transpose(b[:, k * P:(k + 1) * P], v[:, t, (4 * half + k) * P:(4 * half + k + 1) * P], ident[:])
                ins.then_inc(aux_mm, 1)
            e.wait_ge(aux_taken, len(aux))
            for t in range(2):
                for k in range(KD):
                    ins = e.matmul(bank[6][:, 16 + 8 * t:24 + 8 * t], vt[:, k, t * P:(t + 1) * P], rw[:, k, :], start=k == 0, stop=k == KD - 1)
            ins.then_inc(lg_mm, 1)
            e.wait_ge(rt_dve, 1)
            e.matmul(bank[6][:, 32:40], tri_lt[:], sel[:, 0, :], start=True, stop=True)
            e.matmul(bank[6][:, 40:48], tri_lt[:], sel[:, 1, :], start=True, stop=False)
            e.matmul(bank[6][:, 40:48], ones[:], sel[:, 0, :], start=False, stop=True)
            e.matmul(bank[6][:, 48:56], ones[:], sel[:, 0, :], start=True, stop=False)
            e.matmul(bank[6][:, 48:56], ones[:], sel[:, 1, :], start=False, stop=True).then_inc(rt_mm, 1)
            e.drain().then_inc(used2, SPL2)

            def gather(n):
                e.wait_ge(pick_ready, n)
                for k in range(KD):
                    for t in range(2):
                        ins = e.matmul(bank[5 + k // 4][:, (k % 4) * P:(k % 4 + 1) * P], v[:, t, k * P:(k + 1) * P], pick[:, t, :],
                                       start=t == 0, stop=t == 1)
                ins.then_inc(gather_mm, 1)

            def tile2(k, i, b=None):
                e.wait_ge(lo2, val2(RAW2 + k + 1, i, b, 6))
                return k % SPL2

            def up(i, k, bk, b=None):
                for half in range(2):
                    s = tile2(k + half, i, b)
                    for kk in range(4):
                        c = 4 * half + kk
                        w = slice(kk * 512, (kk + 1) * 512)
                        ins = passes(bank[bk][:], (xgh[:, c, :], xgl[:, c, :]), (whi2[:, s, w], wlo2[:, s, w]), c == 0, c == KD - 1)
                    ins.then_inc(used2, 1)

            def down2(i, k, blk, first, last, b=None):
                e.wait_ge(gtl_ready, val3(blk + 1, i, b))
                for half in range(2):
                    s = tile2(k + half, i, b)
                    for f in range(2):
                        ff = 2 * half + f
                        for n in range(2):
                            w = slice(f * D + n * 512, f * D + (n + 1) * 512)
                            ins = passes(bank[3 + n][:], (gth[:, ff, :], gtl[:, ff, :]), (whi2[:, s, w], wlo2[:, s, w]),
                                         first and ff == 0, last and ff == 3)
                    ins.then_inc(used2, 1)

            def turn2(i, blk, b=None):
                e.wait_ge(gm_ready, val3(blk + 1, i, b))
                for f in range(4):
                    ins = e.transpose(bank[2][:, f * P:(f + 1) * P], gme[:, f * P:(f + 1) * P], ident[:])
                ins.then_inc(turn_mm, 1)

            gather(1)
            e.wait_ge(tab_ready, 1)
            count = e.value_load(itab[0:1, 12:13], min_val=NE, max_val=MAX_ITEMS)
            with e.Fori(0, count) as i:
                e.wait_ge(xgl_ready, i + 1)
                up(i, 0, 0)
                up(i, 2, 1)
                e.wait_ge(acc_added, i * 4 + 1)
                for t in range(2):
                    ins = e.transpose(bank[7][:, t * P:(t + 1) * P], pickg[:, t, :], ident[:])
                ins.then_inc(put_mm, 1)
                turn2(i, 0)
                up(i, 4, 0)
                up(i, 6, 1)
                down2(i, 8, 0, True, False)
                turn2(i, 1)
                with e.Fori(0, EB - 2) as b:
                    up(i, 10, 0, b)
                    up(i, 12, 1, b)
                    down2(i, 14, 1, False, False, b)
                    turn2(i, 2, b)
                gather(i + 2)
                down2(i, TPI - 2, EB - 1, False, True)
                e.wait_ge(put_ready, i + 1)
                e.wait_ge(osb_ready, i + 1)
                for n, bk in enumerate((7, 2, 3, 4)):
                    t, h = n // 2, n % 2
                    e.matmul(bank[bk][:], put[:, t, :], osb[:, h * 512:(h + 1) * 512], start=True, stop=True).then_inc(scat_mm, 1)


_INS = ['x', 'c', 'ctx', 'c_ctx', 'ada_w', 'ada_b', 'norm_mix_w', 'norm_ffn_w',
        'pool_w', 'pool_scale', 'ssd_in_w', 'ssd_conv_w', 'ssd_conv_b', 'ssd_A_log', 'ssd_dt_bias', 'ssd_D',
        'ssd_norm_w', 'ssd_out_w', 'ffn_w1', 'ffn_w3', 'ffn_w2', 'moe_router_w', 'moe_w1', 'moe_w3',
        'moe_w2', 'final_norm_w']
_OUTS = [((1, 256, 1024), 'float32')]


def kernel(**inputs):
    import numpy as _np
    import concourse.bacc as _bacc
    from concourse import mybir as _mybir
    from concourse.bass_utils import run_bass_kernel_spmd as _run

    nc = _bacc.Bacc("TRN2", target_bir_lowering=False, num_devices=1)
    arrays, args = {}, {}
    for name in _INS:
        a = _np.ascontiguousarray(inputs[name])
        arrays[f"in_{name}_dram"] = a
        args[name] = nc.dram_tensor(f"in_{name}_dram", a.shape, _mybir.dt.from_np(a.dtype), kind="ExternalInput").ap()
    shape, dtype = _OUTS[0]
    out = nc.dram_tensor("out_0_dram", shape, _mybir.dt.from_np(_np.dtype(dtype)), kind="ExternalOutput").ap()
    hybrid_backbone(nc, args, out)
    r = _run(nc, [arrays], core_ids=[0])
    return r.results[0]["out_0_dram"]
```

```python
from contextlib import ExitStack

import numpy as np

import concourse.bass as bass
from concourse import mybir

F32 = mybir.dt.float32
F32R = mybir.dt.float32r
I32 = mybir.dt.int32
ALU = mybir.AluOpType
ACT = mybir.ActivationFunctionType
AX_X = mybir.AxisListType.X

P = 128
D = 1024
KD = D // P
NTOK = 256
NT2 = 2 * NTOK
GRID_W = 64
EPS = 1e-6
NMOD = 6
WINDOWS = (2, 4, 8, 16)
DI = 2048
NG = 4
NH = 32
HPG = NH // NG
BC = 512
DSTATE = 128
DFF = 2816
NE = 8
DFE = 3584
TILE = 2048

FF_BLOCKS = DFF // 256
MODT = 48
POOL0 = 27
FFN0 = MODT + 1
IN0 = FFN0 + 3 * FF_BLOCKS
OUT0 = IN0 + 1 + 5 * NG
NTILES = OUT0 + 8
RAW1, SPL1 = 3, 2
RAW0 = 4

EB = DFE // 512
TPI = 6 * EB
RAW2, SPL2 = 6, 3
MAX_ITEMS = NE + 3

PLAIN = tuple(m + (m >= POOL0) for n in (0, 2, 4, 5, 6, 7, 8, 9, 11, 13, 15, 17, 19, 21) for m in (2 * n, 2 * n + 1))
POOLED_AT = (19, 20, 23, 25)
MS_BANK = (4, 4, 2)
SCATTER_BANKS = (2, 5, 6, 7)
POOL_BANKS = (2, 3, 6, 7)
NORM1_AT = POOL0 + 6

PADW = 8 + 4 * (GRID_W + 8) + NTOK + 8


def hybrid_backbone(nc, a, out):
    ctx = ExitStack()
    with ctx:
        def sem(name):
            return ctx.enter_context(nc.semaphore(name))

        def sb(name, shape, dt=F32):
            return ctx.enter_context(nc.sbuf_tensor(name, shape, dt))

        bank = [ctx.enter_context(nc.psum_tensor(f"bank{i}", [P, 512], F32)) for i in range(8)]

        ident = sb("ident", [P, P])
        ones = sb("ones", [P, P])
        tri_le = sb("tri_le", [P, P])
        tri_ge = sb("tri_ge", [P, P])
        tri_lt = sb("tri_lt", [P, P])
        tri_gt = sb("tri_gt", [P, P])
        fold = sb("fold", [80, 32])
        slot_id = sb("slot_id", [P, P])
        before = sb("before", [P, NE, NE])
        expert_id = sb("expert_id", [P, NE])
        eps_col = sb("eps_col", [P, 1])
        va = sb("va", [P, 64])
        vb = sb("vb", [P, 120])
        mc = [sb(f"mc{i}", [P, 3, 2, 2, KD]) for i in range(2)]
        aff = sb("aff", [P, 4, 2, KD])
        dcol = sb("dcol", [P, 16])
        sel_row = sb("sel_row", [5, P])

        top = [(nc.sbuf_base + 31) // 32 * 32]
        origin = top[0]

        def at(name, off_kb, shape, dt=F32):
            size = int(np.prod(shape[1:])) * 4
            off = origin + int(off_kb * 1024)
            assert off + size <= nc.sbuf_usable_end, (name, off + size - nc.sbuf_usable_end)
            top[0] = max(top[0], off + size)
            return nc.alloc_sbuf_tensor_at(name, shape, dt, offset=off)

        raw = at("raw", 0, [P, RAW1, TILE])
        whi = at("whi", 24, [P, SPL1, TILE], F32R)
        wlo = at("wlo", 40, [P, SPL1, TILE], F32R)
        uh = at("uh", 56, [P, KD, NT2], F32R)
        ul = at("ul", 72, [P, KD, NT2], F32R)
        ht = at("ht", 88, [P, 2, KD, NTOK])
        sq = at("sq", 104, [P, 2, KD, NTOK])
        xtok = at("xtok", 120, [P, 4, D])
        tn = at("tn", 120, [P, 2, KD, NTOK])
        padded = at("padded", 136, [P, KD, PADW])
        win = at("win", 153.5, [P, 2, 2, PADW])
        wing = at("wing", 162.5, [P, 2, 2, PADW])
        inv_cnt = at("inv_cnt", 80, [P, 4, NT2])
        sg = at("sg", 136, [P, 2, NT2])
        gf = at("gf", 140, [P, 2, NT2])
        gh = at("gh", 144, [P, 2, 2, NT2], F32R)
        gl = at("gl", 152, [P, 2, 2, NT2], F32R)
        raw_more = at("raw_more", 179.5, [P, TILE])
        mrow = at("mrow", 171.5, [4, 2048])
        rb = at("rb", 187.5, [80, 2, 3, P])
        rstd = at("rstd", 190.5, [P, NT2])
        csf = at("csf", 171.25, [P, KD, 4])
        cst = at("cst", 192.5, [P, KD, P], F32R)
        rows_in = at("rows_in", 199.5, [P, 3, P])

        y2 = at("y2", 104, [P, 16, NTOK])
        xs_tok = at("xs_tok", 120, [P, 2, 4, 512])
        b_tok = at("b_tok", 136, [P, 2, 4, P])
        bt = at("bt", 140, [P, 2, NTOK])
        ct = at("ct", 142, [P, 2, NTOK])
        xst = at("xst", 144, [P, 2, 4, NTOK])
        sz = at("sz", 152, [P, 2, 4, NTOK])
        xd = at("xd", 160, [P, 2, 2, 512])
        xdd = [at("xdd0", 168, [P, 512]), at("xdd1", 199.25, [P, 512])]
        seg = at("seg", 170, [P, 2, 512])
        ytmp = at("ytmp", 174, [P, 512])
        ysum = at("ysum", 198, [P, NTOK])
        csc = at("csc", 178, [P, 2, 512])
        seg_alt = at("seg_alt", 182, [P, 2, 512])
        csc_alt = at("csc_alt", 186, [P, 2, 512])
        cp = at("cp", 182, [P, 2, 2, 260])
        cacc = at("cacc", 186.25, [P, 2, 512])
        ccv = at("ccv", 190.25, [P, 2, NTOK])
        cb = at("cb", 192.25, [P, 2, 2, P])
        states = at("states", 96, [P, 4, 512])
        dt_tok = at("dt_tok", 194.25, [P, 4, 64])
        a_tok = at("a_tok", 195.25, [P, 4, 64])
        wdec = at("wdec", 196.25, [P, 8, NH])
        acs = at("acs", 197.25, [P, 4, NH])
        ry = at("ry", 197.875, [P, 8])
        dts = at("dts", 160, [P, 5, NT2])
        dpar = at("dpar", 197.8125, [P, 4])

        raw2 = at("raw2", 0, [P, RAW2, TILE])
        yh = uh[:].rearrange("p k (c n) -> p (k c) n", c=2)
        yl = ul[:].rearrange("p k (c n) -> p (k c) n", c=2)
        whi2 = at("whi2", 48, [P, SPL2, TILE], F32R)
        wlo2 = at("wlo2", 72, [P, SPL2, TILE], F32R)
        xgh = at("xgh", 96, [P, KD, P], F32R)
        xgl = at("xgl", 100, [P, KD, P], F32R)
        gth = at("gth", 104, [P, 4, P], F32R)
        gtl = at("gtl", 106, [P, 4, P], F32R)
        sge = at("sge", 108, [P, 512])
        gme = at("gme", 110, [P, 512])
        osh = at("osh", 112, [P, D], F32R)
        osl = at("osl", 128, [P, D], F32R)
        pick = at("pick", 116, [P, 2, P])
        put = at("put", 118, [P, 2, P], F32R)
        hl = at("hl", 120, [P, 2, D])
        mods = at("mods", 128, [P, 4, D])
        nfw = at("nfw", 144, [P, D])
        fnw = at("fnw", 148, [P, D])
        v = at("v", 152, [P, 2, D])
        vt = at("vt", 160, [P, KD, NTOK])
        acc = at("acc", 168, [P, 2, D])
        mrow5 = at("mrow5", 176, [5, 4, D])
        rw = at("rw", 192, [P, KD, NE])
        lg = at("lg", 192.5, [P, 2, NE])
        cmp = at("cmp", 193, [P, 2, NE, NE])
        eqs = at("eqs", 193.5, [P, 2, NE, NE])
        sel = at("sel", 194, [P, 2, NE])
        gate = at("gate", 194.125, [P, 2, NE])
        pos = at("pos", 194.25, [P, 2, NE])
        rsc = at("rsc", 194.375, [P, 16])
        cnt = at("cnt", 194.5, [P, NE])
        over = at("over", 194.625, [P, NE])
        more = at("more", 194.75, [P, 3, NE])
        tmp3 = at("tmp3", 195, [P, 3, NE])
        pos_item = at("pos_item", 195.25, [P, 2, 12])
        gate_item = at("gate_item", 196.25, [P, 2, 1 + 12])
        ftab = at("ftab", 195.5, [P, 16])
        itab = at("itab", 195.75, [1, 16], I32)
        stat = at("stat", 196, [P, 16])
        sq2 = at("sq2", 160, [P, D])

        scr = nc.dram_tensor("mod_scratch", [2, 3, 4, 2048], F32, kind="Internal").ap()

        landed = [sem(f"landed{i}") for i in range(RAW0)]
        hi_done, lo_done, used = sem("hi_done"), sem("lo_done"), sem("used")
        consts_ready = sem("consts_ready")
        loaded_c, loaded_x, loaded_vec, loaded_bias, loaded_misc = sem("loaded_c"), sem("loaded_x"), sem("loaded_vec"), sem("loaded_bias"), sem("loaded_misc")
        vec_t, vec_cols, cst_ready = sem("vec_t"), sem("vec_cols"), sem("cst_ready")
        x_t, x_copied = sem("x_t"), sem("x_copied")
        sq_ready, ms_ready, sd_ready, tn_ready = sem("sq_ready"), sem("ms_ready"), sem("sd_ready"), sem("tn_ready")
        mod_row, mod_saved, mod_back = sem("mod_row"), sem("mod_saved"), sem("mod_back")
        fold_mm, mc_ready = sem("fold_mm"), sem("mc_ready")
        pads_zero, pad_ready, pool_g, pool_v = sem("pads_zero"), sem("pad_ready"), sem("pool_g"), sem("pool_v")
        uh_ready, ul_ready = sem("uh_ready"), sem("ul_ready")
        pool_mm, pool_added = sem("pool_mm"), sem("pool_added")
        ffn_h1, ffn_silu, ffn_h3, ffn_g = sem("ffn_h1"), sem("ffn_silu"), sem("ffn_h3"), sem("ffn_g")
        ffn_gh, ffn_gl, ffn_out, ffn_added = sem("ffn_gh"), sem("ffn_gl"), sem("ffn_out"), sem("ffn_added")
        in_mm, in_taken, conv_acc, conv_out = sem("in_mm"), sem("in_taken"), sem("conv_acc"), sem("conv_out")
        dt_steps, dt_act, a_ready = sem("dt_steps"), sem("dt_act"), sem("a_ready")
        aux_mm, aux_taken, wdec_ready = sem("aux_mm"), sem("aux_taken"), sem("wdec_ready")
        z_ready, cb_ready, st_ready = sem("z_ready"), sem("cb_ready"), sem("st_ready")
        xd_ready, xdd_ready = sem("xd_ready"), sem("xdd_ready")
        bc_mm, seg_ready, exp_ready, mix_ready = sem("bc_mm"), sem("seg_ready"), sem("exp_ready"), sem("mix_ready")
        y_mm, y_taken, ysum_ready, pads2 = sem("y_mm"), sem("y_taken"), sem("ysum_ready"), sem("pads2")
        yw_ready, yh_ready, yl_ready, ry_root, ry_ready = sem("yw_ready"), sem("yh_ready"), sem("yl_ready"), sem("ry_root"), sem("ry_ready")
        rows_back, hl_ready, mods_ready = sem("rows_back"), sem("hl_ready"), sem("mods_ready")
        h_ready, hsq_ready, v_ready, lg_mm, rt_dve, rt_act, rt_mm, tab_ready = (sem(n) for n in (
            "h_ready", "hsq_ready", "v_ready", "lg_mm", "rt_dve", "rt_act", "rt_mm", "tab_ready"))
        landed2 = [sem(f"expert_landed{i}") for i in range(RAW2)]
        hi2, lo2, used2 = sem("expert_hi"), sem("expert_lo"), sem("expert_used")
        pick_ready, put_mm, put_ready = sem("pick_ready"), sem("put_mm"), sem("put_ready")
        gather_mm, xgh_ready, xgl_ready = sem("gather_mm"), sem("xgh_ready"), sem("xgl_ready")
        silu2, gm_ready, turn_mm, gth_ready, gtl_ready = (sem(n) for n in ("silu2", "gm_ready", "turn_mm", "gth_ready", "gtl_ready"))
        osh_ready, osl_ready, scat_mm, acc_added, out_sq, out_ready, out_done = (sem(n) for n in (
            "osh_ready", "osl_ready", "scat_mm", "acc_added", "out_sq", "out_ready", "out_done"))

        block = ctx.enter_context(nc.Block())

        pair_tiles = range(IN0 + 1, OUT0)

        def tile_ref(t):
            return t if isinstance(t, tuple) else (t, None)

        def val(const, coef, reg):
            return const if reg is None else reg * coef + const

        def val2(const, i, b, coef):
            x = const if i is None else i * TPI + const
            return x if b is None else b * coef + x

        def val3(const, i, b):
            x = const if i is None else i * EB + const
            return x if b is None else x + b

        def splits(k):
            return k - sum(t < k for t in PLAIN)

        split_tiles = [t for t in range(FFN0 + 3) if t not in PLAIN]

        def slot(k):
            return k % (RAW0 if k < FFN0 else RAW1)

        def landing(k):
            return raw[:, slot(k), :] if slot(k) < RAW1 else raw_more[:]

        def dmas_into_slot(k):
            return sum(2 if t in pair_tiles else 1 for t in range(k + 1) if slot(t) == slot(k))

        def split_hi(e, t):
            k, reg = tile_ref(t)
            if k in PLAIN:
                return
            e.wait_ge(landed[slot(k)], val(16 * dmas_into_slot(k), 32, reg))
            if splits(k) >= SPL1:
                last = split_tiles[splits(k) - SPL1] if k < FFN0 + 2 else k - SPL1
                e.wait_ge(used, val(last + 1, 6, reg))
            e.activation(whi[:, splits(k) % SPL1, :], landing(k), ACT.Copy).then_inc(hi_done, 1)

        def split_lo(e, t):
            k, reg = tile_ref(t)
            if k in PLAIN:
                return
            i = splits(k)
            e.wait_ge(hi_done, val(i + 1, 6, reg))
            e.tensor_tensor(wlo[:, i % SPL1, :], landing(k), whi[:, i % SPL1, :].bitcast(F32),
                            ALU.subtract).then_inc(lo_done, 1)

        def w_ready(e, t):
            k, reg = tile_ref(t)
            e.wait_ge(lo_done, val(splits(k) + 1, 6, reg))
            return splits(k) % SPL1

        def slot_free(e, k, reg=None):
            before = [t for t in range(k) if slot(t) == slot(k)][-1:]
            if before and before[0] in PLAIN:
                e.wait_ge(used, before[0] + 1)
            elif before:
                e.wait_ge(lo_done, val(splits(before[0]) + 1, 6, reg))

        def mod_at(m):
            return m if m < POOL0 else m + 1

        def mod_no(s):
            return s if s < POOL0 else None if s == POOL0 else s - 1

        def mod_src(m):
            layer, t = m // 24, m % 24
            n, kh = t // 2, t % 2
            return a["ada_w"][layer, kh * 512:(kh + 1) * 512, n * 512:(n + 1) * 512].rearrange("(k p) n -> p k n", p=P)

        def cols_src(w, c0):
            return w[:, c0:c0 + 256].rearrange("(k p) n -> p k n", p=P)

        def pool_windows(e, g, w):
            src, n = padded[:, 2 * g:2 * g + 2, :], PADW
            e.tensor_tensor(w[:, 0, :, 1:n], src[:, :, 0:n - 1], src[:, :, 1:n], ALU.add)
            e.drain()
            cur, sh = 0, 1
            for _ in range(g):
                e.tensor_tensor(w[:, 1 - cur, :, sh:n - sh], w[:, cur, :, 0:n - 2 * sh], w[:, cur, :, 2 * sh:n], ALU.add)
                e.drain()
                cur, sh = 1 - cur, 2 * sh
            c0 = 8 + 4 * (GRID_W + 8)
            lat = lambda x: x[:, 8:c0].rearrange("p (r w) -> p r w", w=GRID_W + 8)[:, :, 0:GRID_W]
            rows = lambda x: x.rearrange("p (r w) -> p r w", w=GRID_W)
            for k in range(2):
                e.tensor_tensor(rows(tn[:, 0, 2 * g + k, :]), lat(w[:, cur, k, :]), rows(inv_cnt[:, g, 0:NTOK]), ALU.mult)
                e.tensor_tensor(tn[:, 1, 2 * g + k, :], w[:, cur, k, c0:c0 + NTOK], inv_cnt[:, g, NTOK:], ALU.mult)
            e.drain()
            for k in range(2):
                e.tensor_tensor(rows(tn[:, 0, 2 * g + k, :]), rows(tn[:, 0, 2 * g + k, :]), lat(padded[:, 2 * g + k, :]), ALU.subtract)
                e.tensor_tensor(tn[:, 1, 2 * g + k, :], tn[:, 1, 2 * g + k, :], padded[:, 2 * g + k, c0:c0 + NTOK], ALU.subtract)

        def two(x):
            return x.rearrange("p (s n) -> p s n", s=2)

        def split_u_hi(e, k):
            e.activation(two(uh[:, k, :]), tn[:, :, k, :], ACT.Copy).then_inc(uh_ready, 1)

        def split_u_lo(e, k, base):
            e.wait_ge(uh_ready, base + k + 1)
            e.tensor_tensor(two(ul[:, k, :]), tn[:, :, k, :], two(uh[:, k, :].bitcast(F32)), ALU.subtract).then_inc(ul_ready, 1)

        def w1_tile(j):
            return FFN0 + 2 + 3 * (j - 1) if j else FFN0

        def w2_tile(j):
            return IN0 - 1 if j == FF_BLOCKS - 1 else FFN0 + 3 * j + 4

        def chunk_done(e, s, tile, j, c, it):
            if c == 0:
                e.wait_ge(s, val(j + 1, 2, it))
            else:
                e.wait_ge(used, val(tile + 1, 6, it))

        aux = [("dt", 0, 0), ("turn", 0, 1), ("decay", 0, 0), ("turn", 0, 2), ("turn", 0, 3), ("turn", 0, 4)]
        for g in range(1, NG + 1):
            aux += [("turn", g - 1, 0), ("cb", g - 1, 0)] + [("state", g - 1, i) for i in range(4)]
            if g < NG:
                aux += [("turn", g, i) for i in range(1, 5)]
        aux += [("resid", 0, i) for i in range(4)] + [("mods", 0, i) for i in range(8)] + [("v", 0, i) for i in range(4)]
        aux_no = {key: n for n, key in enumerate(aux)}

        def in_tile(g, j):
            return IN0 + 1 + 5 * g + j

        def in_chunk(g, j, c):
            return 1 + 10 * g + 2 * j + c

        def unit_bufs(n):
            return (seg_alt, csc_alt) if n >= 4 * (NG - 1) and n % 2 else (seg, csc)

        @block.sync
        def _(e):
            def load(t, src, shape):
                k, reg = tile_ref(t)
                slot_free(e, k, reg)
                dst = landing(k).rearrange("p (k n) -> p k n", k=shape)
                e.dma_start(dst, src).then_inc(landed[slot(k)], 16)

            for kind, src in enumerate((a["c"][0], a["c_ctx"])):
                e.dma_start(rows_in[8 * kind:8 * kind + 8, 2, :], src.rearrange("(r d) -> r d", d=P)).then_inc(loaded_c, 16)
            for s in range(FFN0):
                if s == RAW0:
                    vec = [(a["norm_mix_w"][0], 0, 8), (a["norm_mix_w"][1], 8, 8), (a["norm_ffn_w"][0], 16, 8),
                           (a["pool_scale"][0], 24, 8), (a["ssd_norm_w"][0], 32, 16)]
                    for src, r, n in vec:
                        e.dma_start(rows_in[r:r + n, 0, :], src.rearrange("(r d) -> r d", d=P)).then_inc(loaded_vec, 16)
                    e.dma_start(rows_in[0:96, 1, :], a["ssd_conv_w"][0].rearrange("t (r d) -> (t r) d", d=P)).then_inc(loaded_vec, 16)
                    e.dma_start(rows_in[96:120, 1, :], a["ssd_conv_b"][0].rearrange("(r d) -> r d", d=P)).then_inc(loaded_vec, 16)
                if s == POOL0:
                    load(s, a["pool_w"][0].rearrange("g (i p) o -> p (g i) o", p=P), 8)
                else:
                    load(s, mod_src(mod_no(s)), 4)
            w1, w3, w2 = a["ffn_w1"][0], a["ffn_w3"][0], a["ffn_w2"][0]
            load(FFN0, cols_src(w1, 0), 8)
            load(FFN0 + 1, cols_src(w3, 0), 8)
            with e.Fori(0, FF_BLOCKS // 2) as it:
                for u in range(2):
                    k = FFN0 + 2 + 3 * u
                    c = it * 512 + (1 + u) * 256
                    load((k, it), w1[:, bass.ds(c, 256)].rearrange("(k p) n -> p k n", p=P), 8)
                    load((k + 1, it), w3[:, bass.ds(c, 256)].rearrange("(k p) n -> p k n", p=P), 8)
                    load((k + 2, it), w2[bass.ds(it * 512 + u * 256, 256), :].rearrange("(k p) n -> p k n", p=P), 2)
            load(IN0 - 1, w2[DFF - 256:DFF, :].rearrange("(k p) n -> p k n", p=P), 2)
            inw = a["ssd_in_w"][0]
            load(IN0, cols_src(inw, inw.shape[1] - 256), 8)
            for g in range(NG):
                for j in range(5):
                    k = in_tile(g, j)
                    slot_free(e, k)
                    dst = landing(k).rearrange("p (k b n) -> p b k n", k=KD, b=2)
                    first = DI + (4 * g + j) * P if j < 4 else 2 * DI + g * P
                    second = (4 * g + j) * P if j < 4 else 2 * DI + BC + g * P
                    for b_, c0 in ((0, first), (1, second)):
                        e.dma_start(dst[:, b_], inw[:, c0:c0 + P].rearrange("(k p) n -> p k n", p=P)).then_inc(landed[slot(k)], 16)
            for n in range(2):
                for kq in range(4):
                    load(OUT0 + 4 * n + kq, a["ssd_out_w"][0][kq * 512:(kq + 1) * 512, n * 512:(n + 1) * 512].rearrange("(k p) n -> p k n", p=P), 4)
            def load2(k, i, b, coef, src, kk):
                e.wait_ge(lo2, val2(k + 1, i, b, coef))
                e.dma_start(raw2[:, k % RAW2, :].rearrange("p (k n) -> p k n", k=kk), src).then_inc(landed2[k % RAW2], 16)

            m1 = a["moe_w1"][0].rearrange("e (h k p) n -> e h p k n", h=2, p=P)
            m3 = a["moe_w3"][0].rearrange("e (h k p) n -> e h p k n", h=2, p=P)
            m2 = a["moe_w2"][0].rearrange("e (f k p) n -> e f p k n", k=2, p=P)
            one = lambda x: x.rearrange("o p k n -> p (o k) n")

            def up_tiles(k, i, b, ex, blk):
                for n, m in enumerate((m1, m3)):
                    for half in range(2):
                        cols = bass.ds(blk * 512, 512) if b is not None else slice(blk * 512, blk * 512 + 512)
                        load2(k + 2 * n + half, i, b, 6, one(m[bass.ds(ex, 1), half, :, :, cols]), 4)

            def down_tiles(k, i, b, ex, blk):
                for half in range(2):
                    f = (blk * 2 + half)
                    src = m2[bass.ds(ex, 1), bass.ds(f, 1) if b is not None else slice(f, f + 1)]
                    load2(k + half, i, b, 6, src.rearrange("o f p k n -> p (o f k) n"), 2)

            up_tiles(0, None, None, 0, 0)
            e.wait_ge(tab_ready, 1)
            count = e.value_load(itab[0:1, 12:13], min_val=NE, max_val=MAX_ITEMS)
            with e.Fori(0, count) as i:
                ex = e.value_load(itab[0:1, bass.ds(i, 1)], min_val=0, max_val=NE - 1)
                with e.Fori(0, EB - 1) as b:
                    up_tiles(4, i, b, ex, b + 1)
                    down_tiles(8, i, b, ex, b)
                down_tiles(TPI - 2, i, None, ex, EB - 1)
                ex = e.value_load(itab[0:1, bass.ds(i + 1, 1)], min_val=0, max_val=NE - 1)
                up_tiles(TPI, i, None, ex, 0)
            for t in range(2):
                e.wait_ge(out_ready, t + 1)
                e.dma_start(out[0, t * P:(t + 1) * P, :], acc[:, t, :]).then_inc(out_done, 16)
            e.wait_ge(out_done, 32)

        @block.gpsimd
        def _(e):
            e.memset(ident[:], 0.0)
            e.drain()
            e.affine_select(out=ident[:], in_=ident[:], compare_op=ALU.not_equal, fill=1.0, base=0,
                            pattern=[[-1, P]], channel_multiplier=1)
            e.drain().then_inc(consts_ready, 1)
            e.memset(ones[:], 1.0)
            e.memset(fold[:], 0.0)
            e.memset(sel_row[:], 1.0)
            e.memset(eps_col[:], EPS)
            e.memset(before[:], 1.0)
            e.drain()
            e.affine_select(out=tri_le[:], in_=ones[:], compare_op=ALU.is_ge, fill=0.0, base=0,
                            pattern=[[1, P]], channel_multiplier=-1)
            e.affine_select(out=tri_ge[:], in_=ones[:], compare_op=ALU.is_ge, fill=0.0, base=0,
                            pattern=[[-1, P]], channel_multiplier=1)
            e.affine_select(out=tri_lt[:], in_=ones[:], compare_op=ALU.is_gt, fill=0.0, base=0,
                            pattern=[[1, P]], channel_multiplier=-1)
            e.affine_select(out=tri_gt[:], in_=ones[:], compare_op=ALU.is_gt, fill=0.0, base=0,
                            pattern=[[-1, P]], channel_multiplier=1)
            for kind in range(2):
                for q in (kind, kind + 2, 4):
                    v_ = fold[:, 16 * kind:16 * kind + 16]
                    e.affine_select(out=v_, in_=v_, compare_op=ALU.not_equal, fill=1.0, base=-16 * q,
                                    pattern=[[-1, 16]], channel_multiplier=1)
                    e.drain()
            for q in (1, 3):
                e.affine_select(out=sel_row[:], in_=sel_row[:], compare_op=ALU.not_equal, fill=0.0, base=-q,
                                pattern=[[0, P]], channel_multiplier=1)
                e.drain()
            e.affine_select(out=before[:], in_=before[:], compare_op=ALU.is_gt, fill=0.0, base=0,
                            pattern=[[1, NE], [-1, NE]], channel_multiplier=0)
            e.iota(slot_id[:], pattern=[[1, P]], base=0, channel_multiplier=0, allow_small_or_imprecise_dtypes=True)
            e.iota(expert_id[:], pattern=[[1, NE]], base=0, channel_multiplier=0, allow_small_or_imprecise_dtypes=True)
            e.drain().then_inc(consts_ready, 1)
            for layer in range(2):
                e.dma_start(rb[64:80, layer, :, :], a["ada_b"][layer].rearrange("(p i d) -> i p d", i=16, d=P)).then_inc(loaded_bias, 16)
            e.dma_start(dpar[64:128, 0:1], a["ssd_dt_bias"][0].rearrange("d (h o) -> (d h) o", o=1)).then_inc(loaded_misc, 16)
            e.dma_start(dpar[64:128, 1:2], a["ssd_A_log"][0].rearrange("d (h o) -> (d h) o", o=1)).then_inc(loaded_misc, 16)
            for half in range(2):
                d_ = a["ssd_D"][0].rearrange("(c h) -> h c", h=2)[half:half + 1, :]
                e.dma_start(dcol[64 * half:64 * half + 64, :], d_.to_broadcast([64, 16]), allow_slow_non_contiguous=True).then_inc(loaded_misc, 16)
            e.memset(padded[:], 0.0)
            e.memset(wing[:], 0.0)
            for i, w in enumerate(WINDOWS):
                e.memset(inv_cnt[:, i, :], 1.0 / w)
            e.drain()
            for i, w in enumerate(WINDOWS):
                lo, hi = w // 2, w - 1 - w // 2
                for s, L in ((slice(0, NTOK), GRID_W), (slice(NTOK, NT2), NTOK)):
                    rows = inv_cnt[:, i, s].rearrange("p (r w) -> p r w", w=L)
                    for x in range(lo):
                        e.memset(rows[:, :, x:x + 1], 1.0 / (x + hi + 1))
                    for x in range(hi):
                        e.memset(rows[:, :, L - 1 - x:L - x], 1.0 / (x + lo + 1))
            e.drain().then_inc(pads_zero, 1)

            def keep_rows(layer, p):
                n = layer * 3 + p
                e.wait_ge(mod_row, 4 * (n + 1))
                e.dma_start(scr[layer, p], mrow[:]).then_inc(mod_saved, 16)
                if n > 3:
                    return
                e.wait_ge(mod_saved, 16 * (n + 1))
                e.dma_start(rb[0:64, layer, p, :], scr[layer, p].rearrange("q (i d) -> (q i) d", d=P)).then_inc(mod_back, 16)

            keep_rows(0, 0)
            e.wait_ge(pad_ready, 1)
            for g in (2, 3):
                pool_windows(e, g, wing)
                e.drain().then_inc(pool_g, 1)
                if g == 2:
                    keep_rows(0, 1)
            keep_rows(0, 2)
            for p in range(3):
                keep_rows(1, p)
            e.wait_ge(tn_ready, 2 * KD)
            e.wait_ge(ul_ready, 3 * KD)
            e.wait_ge(mod_saved, 6 * 16)
            e.memset(cp[:], 0.0)
            e.memset(ysum[:], 0.0)
            e.drain().then_inc(pads2, 1)
            e.wait_ge(wdec_ready, 2)
            hv = lambda x: x.rearrange("p (h c) -> p h c", c=64)

            def spread(t, h0):
                return t[:, h0:h0 + HPG].unsqueeze(2).to_broadcast([P, HPG, 64])

            def y_squares(g):
                for c in range(2):
                    e.wait_ge(y_taken, 2 * g + c + 1)
                y2g = y2[:, 4 * g:4 * g + 4, :]
                for i in range(0, 4, 2):
                    e.drain()
                    e.tensor_tensor(ytmp[:].rearrange("p (c n) -> p c n", c=2), y2g[:, i:i + 2, :], y2g[:, i:i + 2, :], ALU.mult)
                    e.drain()
                    for j in range(2):
                        e.tensor_tensor(ysum[:], ysum[:], ytmp[:, j * NTOK:(j + 1) * NTOK], ALU.add)
                        e.drain()

            for g in range(NG):
                q = g % 2
                e.wait_ge(aux_taken, aux_no[("turn", g, 4)] + 1)
                for n, (tile, w) in enumerate(((2, 0), (3, 2), (2, 1), (3, 3), (0, 4), (1, 5))):
                    m = 6 * g + n
                    if n in (2, 3):
                        e.wait_ge(aux_mm, aux_no[("state", g, 0)] + 1)
                    elif n in (4, 5):
                        e.wait_ge(aux_mm, aux_no[("state", g, 1)] + 1)
                    elif g:
                        e.wait_ge(aux_mm, aux_no[("state", g - 1, 3)] + 1)
                    e.tensor_tensor(hv(xdd[m % 2][:]), hv(xs_tok[:, q, tile, :]), spread(wdec[:, w, :], HPG * g),
                                    ALU.mult).then_inc(xdd_ready, 1)
                    if n == 1:
                        if g:
                            e.wait_ge(y_mm, 4 * g)
                        for d in range(2):
                            for c in range(2):
                                e.tensor_tensor(hv(xd[:, d, c, :]), hv(xs_tok[:, q, c, :]),
                                                spread(dt_tok[:, c, :], 32 * d + HPG * g), ALU.mult).then_inc(xd_ready, 1)
                if g:
                    y_squares(g - 1)
            e.wait_ge(y_mm, 4 * NG)
            e.dma_start(mrow5[0:4, 0:2, :], scr[1, 1].rearrange("q (m d) -> q m d", m=2)).then_inc(rows_back, 16)
            e.dma_start(mrow5[0:4, 2:4, :], scr[1, 2].rearrange("q (m d) -> q m d", m=2)).then_inc(rows_back, 16)
            e.dma_start(mrow5[4:5, :, :], a["ada_b"][1:2, 2 * D:6 * D].rearrange("q (m d) -> q m d", m=4)).then_inc(rows_back, 16)
            y_squares(NG - 1)
            e.drain().then_inc(ysum_ready, 1)
            e.wait_ge(y_taken, 2 * NG)
            e.dma_start(nfw[:], a["norm_ffn_w"][1:2, :].to_broadcast([P, D])).then_inc(rows_back, 16)
            e.dma_start(fnw[:], a["final_norm_w"].rearrange("(o d) -> o d", o=1).to_broadcast([P, D])).then_inc(rows_back, 16)
            e.dma_start(rw[:], a["moe_router_w"][0].rearrange("(k p) e -> p k e", p=P)).then_inc(rows_back, 16)

        @block.scalar
        def _(e):
            for kind, src in enumerate((a["x"][0], a["ctx"][0])):
                for i in range(2):
                    e.dma_start(xtok[:, 2 * kind + i, :], src[i * P:(i + 1) * P, :]).then_inc(loaded_x, 16)
            e.wait_ge(cst_ready, 2)
            e.activation(csf[:, 0, 2:3], csf[:, 0, 2:3], ACT.Silu)
            e.wait_ge(vec_t, 1)
            e.activation(va[:, 48:64], bank[7][:, 184:200], ACT.Silu)
            e.drain()
            for kind in range(2):
                e.activation(csf[:, :, kind], va[:, 48 + 8 * kind:56 + 8 * kind], ACT.Copy)
                e.activation(cst[:, :, kind], va[:, 48 + 8 * kind:56 + 8 * kind], ACT.Copy).then_inc(vec_cols, 1)

            def rows_out(n):
                e.wait_ge(used, mod_at(2 * n + 1) + 1)
                p = n // 4
                if p and n % 4 == 0:
                    e.wait_ge(mod_saved, 16 * p)
                e.activation(mrow[:, (n % 4) * 512:(n % 4 + 1) * 512], bank[n % 2][0:4, :], ACT.Copy).then_inc(mod_row, 1)

            def fold_cols(n):
                e.wait_ge(fold_mm, n + 1)
                e.activation(mc[n // 3][:, n % 3].rearrange("p a b k -> p (a b k)"), bank[5][:, 0:32], ACT.Copy).then_inc(mc_ready, 1)

            def squares(k):
                e.activation(sq[:, :, k, :], ht[:, :, k, :], ACT.Square).then_inc(sq_ready, 1)

            def root(n):
                e.wait_ge(ms_ready, n + 1)
                e.activation(rstd[:], bank[MS_BANK[n]][:], ACT.Sqrt, bias=eps_col[:], scale=1.0 / D).then_inc(sd_ready, 1)

            def shifted_hi(n, k):
                pair, one, layer = ((1, 1, 0), (0, 0, 1))[n - 1]
                e.wait_ge(tn_ready, KD * (n - 1) + k + 1)
                for kind in range(2):
                    ins = e.activation(uh[:, k, kind * NTOK:(kind + 1) * NTOK], tn[:, kind, k, :], ACT.Identity,
                                       bias=mc[layer][:, pair, kind, one, k:k + 1])
                ins.then_inc(uh_ready, 1)

            split_hi(e, 0)
            for s in range(FFN0):
                split_hi(e, s + 1)
                if s < KD:
                    e.wait_ge(x_t, s + 1)
                    e.activation(ht[:, :, s, :], two(bank[2 + s % 2][:]), ACT.Copy).then_inc(x_copied, 1)
                    e.drain()
                    squares(s)
                    if s == 4:
                        e.wait_ge(vec_t, 2)
                        e.activation(va[:, 0:48], bank[7][:, 0:48], ACT.Copy)
                        e.activation(vb[:], bank[7][:, 64:184], ACT.Copy).then_inc(vec_cols, 1)
                if s == KD:
                    root(0)
                m = mod_no(s)
                if m is not None and m % 2 == 1 and m >= 3:
                    rows_out(m // 2 - 1)
                if s in (13, 21, 29, 39):
                    fold_cols((13, 21, 29, 39).index(s))
                if s in POOLED_AT:
                    g = POOLED_AT.index(s)
                    if g < 2:
                        e.wait_ge(pool_v, g + 1)
                    else:
                        e.wait_ge(pool_g, g - 1)
                    for k in (2 * g, 2 * g + 1):
                        split_u_hi(e, k)
                if s in (POOL0 + 1, POOL0 + 2):
                    for k in range(4 * (s - POOL0 - 1), 4 * (s - POOL0)):
                        e.wait_ge(pool_added, 2 * (k + 1))
                        squares(k)
                if s == POOL0 + 3:
                    root(1)
                if s in (NORM1_AT, NORM1_AT + 1):
                    for k in range(4 * (s - NORM1_AT), 4 * (s - NORM1_AT) + 4):
                        shifted_hi(1, k)
            rows_out(23)

            def ffn_acts(j, it, pick_silu):
                for c in range(2):
                    if pick_silu:
                        chunk_done(e, ffn_h1, w1_tile(j), j, c, it)
                        if j:
                            e.wait_ge(ffn_g, val(2 * (j - 1) + c + 1, 4, it))
                        e.activation(sg[:, c, :], bank[c][:], ACT.Silu).then_inc(ffn_silu, 1)
                    else:
                        e.wait_ge(ffn_g, val(2 * j + c + 1, 4, it))
                        e.activation(gh[:, j % 2, c, :], gf[:, c, :], ACT.Copy).then_inc(ffn_gh, 1)

            split_hi(e, FFN0 + 1)
            ffn_acts(0, None, True)
            split_hi(e, FFN0 + 2)
            ffn_acts(0, None, False)
            with e.Fori(0, FF_BLOCKS // 2) as it:
                for u in range(2):
                    j, k = 1 + u, FFN0 + 2 + 3 * u
                    split_hi(e, (k + 1, it))
                    split_hi(e, (k + 2, it))
                    ffn_acts(j, it, True)
                    split_hi(e, (k + 3, it))
                    ffn_acts(j, it, False)
            split_hi(e, IN0)
            for k in range(KD):
                e.wait_ge(ffn_added, KD * (FF_BLOCKS - 1) + k + 1)
                squares(k)
            root(2)
            for k in range(KD):
                shifted_hi(2, k)
            split_hi(e, in_tile(0, 0))
            R = slice(64, 128)
            e.wait_ge(loaded_misc, 64)
            e.wait_ge(used, IN0 + 1)
            e.activation(dts[R, 0, :], bank[0][R, :], ACT.Identity, bias=dpar[R, 0:1]).then_inc(in_taken, 1)
            e.activation(dpar[R, 2:3], dpar[R, 1:2], ACT.Exp).then_inc(dt_act, 1)
            split_hi(e, in_tile(0, 1))
            e.wait_ge(dt_steps, 1)
            e.activation(dts[R, 1, :], dts[R, 1, :], ACT.Exp, scale=-1.0).then_inc(dt_act, 1)
            e.wait_ge(dt_steps, 2)
            e.activation(dts[R, 3, :], dts[R, 2, :], ACT.Ln).then_inc(dt_act, 1)

            def take_aux(key):
                n = aux_no[key]
                what, g, i = key
                b = bank[2 + n % 2]
                e.wait_ge(aux_mm, n + 1)
                if what == "dt":
                    e.activation(dt_tok[:].rearrange("p t h -> p (t h)"), b[:, 0:256], ACT.Copy)
                    ins = e.activation(a_tok[:].rearrange("p t h -> p (t h)"), b[:, 256:512], ACT.Copy)
                elif what == "decay":
                    e.activation(wdec[:].rearrange("p t h -> p (t h)"), b[:, 0:256], ACT.Exp)
                    ins = e.activation(acs[:].rearrange("p t h -> p (t h)"), b[:, 256:384], ACT.Copy)
                elif what == "turn":
                    o = b_tok[:, g % 2] if i == 0 else xs_tok[:, g % 2, :, (i - 1) * P:i * P]
                    ins = e.activation(o, b[:].rearrange("p (t n) -> p t n", t=4), ACT.Copy)
                elif what == "cb":
                    ins = e.activation(cb[:, 0].rearrange("p c n -> p (c n)"), b[:, 0:256], ACT.Copy)
                elif what == "state":
                    ins = e.activation(states[:, i, :], b[:], ACT.Copy)
                elif what == "resid":
                    ins = e.activation(hl[:, i // 2, (i % 2) * 512:(i % 2 + 1) * 512], b[:], ACT.Copy)
                elif what == "mods":
                    ins = e.activation(mods[:, i // 2, (i % 2) * 512:(i % 2 + 1) * 512], b[:], ACT.Copy)
                elif what == "v":
                    ins = e.activation(vt[:, 4 * (i % 2):4 * (i % 2) + 4, (i // 2) * P:(i // 2 + 1) * P],
                                       b[:].rearrange("p (k n) -> p k n", k=4), ACT.Copy)
                ins.then_inc(aux_taken, 1)

            def take_in(g, j):
                for c in range(2):
                    if c == 0:
                        e.wait_ge(in_mm, 5 * g + j + 1)
                    else:
                        e.wait_ge(used, in_tile(g, j) + 1)
                    b = bank[in_chunk(g, j, c) % 2]
                    if c == 0 or j == 4:
                        v_ = 6 * g + j + c
                        if v_ >= 2:
                            e.wait_ge(conv_acc, v_ - 1)
                        n = 2 - c
                        e.activation(cp[:, v_ % 2, 0:n, 2:258], two(b[:])[:, 0:n, :], ACT.Copy).then_inc(in_taken, 1)
                    else:
                        if g >= 2 and j == 0:
                            e.wait_ge(y_taken, 2 * (g - 1))
                        e.activation(sz[:, g % 2, j, :], b[:, 0:NTOK], ACT.Silu).then_inc(in_taken, 1)

            def conv_silu(g, j):
                q = g % 2
                for c in range(2 if j == 4 else 1):
                    v_ = 6 * g + j + c
                    e.wait_ge(conv_acc, v_ + 1)
                    o = (bt[:, q, :], ct[:, q, :])[c] if j == 4 else xst[:, q, j, :]
                    ins = e.activation(o, cacc[:, v_ % 2, 0:NTOK], ACT.Silu)
                    if c == 0:
                        ins = e.activation(ccv[:, v_ % 2, :], cacc[:, v_ % 2, NTOK:], ACT.Silu)
                    ins.then_inc(conv_out, 1)

            def exps(g, u):
                n = 4 * g + u
                seg_n, csc_n = unit_bufs(n)
                for d in range(2):
                    e.wait_ge(seg_ready, 2 * n + d + 1)
                    e.activation(seg_n[:, d, :], seg_n[:, d, :], ACT.Exp)
                    e.activation(csc_n[:, d, :], bank[4 + d][:], ACT.Exp).then_inc(exp_ready, 1)

            def y_hi(k0, k1):
                for k in range(k0, k1):
                    e.activation(yh[:, k, :], y2[:, k, :], ACT.Identity, scale=va[:, 32 + k:33 + k]).then_inc(yh_ready, 1)

            e.wait_ge(pads2, 1)
            for g in range(NG):
                for j in range(5):
                    if g and j:
                        exps(g - 1, j - 1)
                    if g and j == 1:
                        take_aux(("state", g - 1, 1))
                    if (g, j) != (0, 0):
                        split_hi(e, in_tile(g, j) + 1)
                    if g and j == 0:
                        take_aux(("turn", g - 1, 0))
                        take_aux(("cb", g - 1, 0))
                    if g and j == 1:
                        take_aux(("state", g - 1, 2))
                        take_aux(("state", g - 1, 3))
                    take_in(g, j)
                    if g and j == 0:
                        take_aux(("state", g - 1, 0))
                    if (g, j) == (0, 1):
                        take_aux(("dt", 0, 0))
                    if (g, j) == (0, 2):
                        take_aux(("decay", 0, 0))
                        e.drain().then_inc(wdec_ready, 1)
                    if j:
                        take_aux(("turn", g, j))
                    conv_silu(g, j)
            split_hi(e, OUT0 + 1)
            take_aux(("turn", NG - 1, 0))
            take_aux(("cb", NG - 1, 0))
            take_aux(("state", NG - 1, 0))
            e.wait_ge(y_taken, 4)
            y_hi(0, 4)
            exps(NG - 1, 0)
            y_hi(4, 8)
            take_aux(("state", NG - 1, 1))
            split_hi(e, OUT0 + 2)
            e.wait_ge(y_taken, 6)
            y_hi(8, 12)
            take_aux(("state", NG - 1, 2))
            take_aux(("state", NG - 1, 3))
            split_hi(e, OUT0 + 3)
            exps(NG - 1, 1)
            split_hi(e, OUT0 + 4)
            for u in (2, 3):
                exps(NG - 1, u)
                for n in (2 * u - 4, 2 * u - 3):
                    take_aux(("resid", 0, n))
            e.drain().then_inc(hl_ready, 1)
            e.wait_ge(y_taken, 2 * NG)
            y_hi(12, 16)
            split_hi(e, OUT0 + 5)
            e.wait_ge(rt_mm, 1)
            e.activation(ry[:, 0:2], bank[6][:, 0:2], ACT.Sqrt, bias=eps_col[:], scale=1.0 / DI).then_inc(ry_root, 1)
            for t in range(6, 8):
                split_hi(e, OUT0 + t)
            for n in range(8):
                take_aux(("mods", 0, n))
            e.drain().then_inc(mods_ready, 1)
            e.wait_ge(h_ready, 1)
            for t in range(2):
                e.activation(sq2[:], hl[:, t, :], ACT.Square, accum_out=stat[:, t:t + 1])
                e.drain()
            e.activation(stat[:, 2:4], stat[:, 0:2], ACT.Sqrt, bias=eps_col[:], scale=1.0 / D).then_inc(hsq_ready, 1)
            for n in range(4):
                take_aux(("v", 0, n))

            def hi_of(k, i, b=None):
                if b is None:
                    e.wait_ge(landed2[k % RAW2], i * (16 * EB) + 16 * (k // RAW2 + 1) if i is not None else 16)
                else:
                    e.wait_ge(landed2[k % RAW2], i * (16 * EB) + b * 16 + 16 * (k // RAW2 + 1))
                e.wait_ge(used2, val2(k + 1, i, b, 6))
                e.activation(whi2[:, k % SPL2, :], raw2[:, k % RAW2, :], ACT.Copy).then_inc(hi2, 1)

            def silu_of(i, blk, b=None):
                e.activation(sge[:], bank[0][:], ACT.Silu).then_inc(silu2, 1)

            def gth_of(i, blk, b=None):
                e.wait_ge(turn_mm, val3(blk + 1, i, b))
                e.activation(gth[:].rearrange("p f n -> p (f n)"), bank[2][:], ACT.Copy).then_inc(gth_ready, 1)

            def xgh_of(n):
                e.wait_ge(gather_mm, n)
                for h in range(2):
                    ins = e.activation(xgh[:, 4 * h:4 * h + 4, :].rearrange("p k n -> p (k n)"), bank[5 + h][:], ACT.Copy)
                ins.then_inc(xgh_ready, 1)

            def block(i, k, blk, b=None):
                hi_of(k + 2, i, b)
                gth_of(i, blk - 1, b)
                hi_of(k + 3, i, b)
                hi_of(k + 4, i, b)
                silu_of(i, blk, b)
                for n in range(5, 8):
                    hi_of(k + n, i, b)

            hi_of(0, None)
            hi_of(1, None)
            e.wait_ge(rt_dve, 1)
            for t in range(2):
                e.activation(gate[:, t, :], lg[:, t, :], ACT.Exp, bias=rsc[:, t:t + 1])
            e.drain().then_inc(rt_act, 1)
            xgh_of(1)
            e.wait_ge(tab_ready, 1)
            count = e.value_load(itab[0:1, 12:13], min_val=NE, max_val=MAX_ITEMS)
            with e.Fori(0, count) as i:
                hi_of(2, i)
                hi_of(3, i)
                hi_of(4, i)
                silu_of(i, 0)
                hi_of(5, i)
                block(i, 4, 1)
                e.wait_ge(put_mm, i + 1)
                e.activation(put[:].rearrange("p t n -> p (t n)"), bank[7][:, 0:256], ACT.Copy).then_inc(put_ready, 1)
                with e.Fori(0, EB - 2) as b:
                    block(i, 10, 2, b)
                hi_of(TPI, i)
                gth_of(i, EB - 1)
                xgh_of(i + 2)
                hi_of(TPI + 1, i)
                e.wait_ge(used2, i * TPI + (TPI + SPL2))
                for n in range(2):
                    e.activation(osh[:, n * 512:(n + 1) * 512], bank[3 + n][:], ACT.Copy).then_inc(osh_ready, 1)
            e.wait_ge(out_sq, 1)
            for t in range(2):
                e.activation(v[:, t, :], hl[:, t, :], ACT.Square, accum_out=stat[:, 8 + t:9 + t])
            e.drain()
            e.activation(stat[:, 10:12], stat[:, 8:10], ACT.Sqrt, bias=eps_col[:], scale=1.0 / D).then_inc(out_sq, 1)

        @block.vector
        def _(e):
            e.memset(csf[:], 0.0).then_inc(cst_ready, 1)
            e.memset(cst[:].bitcast(F32), 0.0).then_inc(cst_ready, 1)
            e.memset(win[:], 0.0)
            e.wait_ge(vec_cols, 2)
            for kind in range(2):
                e.tensor_tensor(cst[:, :, 2 + kind], va[:, 48 + 8 * kind:56 + 8 * kind],
                                cst[:, :, kind].bitcast(F32), ALU.subtract).then_inc(cst_ready, 1)

            def scales(i, layer, src_pair, src_one, w0, plus_one):
                for kind in range(2):
                    e.scalar_tensor_tensor(out=aff[:, i, kind, :], in0=mc[layer][:, src_pair, kind, src_one, :],
                                           scalar=1.0 if plus_one else 0.0, in1=va[:, w0:w0 + KD], op0=ALU.add, op1=ALU.mult)

            def inverse_root(n):
                e.wait_ge(sd_ready, n + 1)
                e.reciprocal(rstd[:], rstd[:])
                e.drain()

            def normalise(n):
                inverse_root(n)
                for k in range(KD):
                    e.tensor_tensor(tn[:, :, k, :], ht[:, :, k, :], two(rstd[:]), ALU.mult)
                e.drain()

            def modulated(i, layer, pair, one, write, chunks=range(KD)):
                for k in chunks:
                    for kind in range(2):
                        ins = write(k, kind, aff[:, i, kind, k:k + 1], mc[layer][:, pair, kind, one, k:k + 1])
                return ins

            def into_padded(k, kind, s, b):
                if kind == 0:
                    c0 = 8 + 4 * (GRID_W + 8)
                    o = padded[:, k, 8:c0].rearrange("p (r w) -> p r w", w=GRID_W + 8)[:, :, 0:GRID_W]
                    i_ = tn[:, 0, k, :].rearrange("p (r w) -> p r w", w=GRID_W)
                else:
                    o, i_ = padded[:, k, 8 + 4 * (GRID_W + 8):PADW - 8], tn[:, 1, k, :]
                return e.tensor_scalar(o, i_, s, b, ALU.mult, ALU.add)

            def scaled(n, k):
                for kind in range(2):
                    ins = e.scalar_tensor_tensor(out=tn[:, kind, k, :], in0=ht[:, kind, k, :], scalar=aff[:, n + 1, kind, k:k + 1],
                                                 in1=rstd[:, kind * NTOK:(kind + 1) * NTOK], op0=ALU.mult, op1=ALU.mult)
                ins.then_inc(tn_ready, 1)

            def shifted_lo(n, k):
                pair, one, layer = ((1, 1, 0), (0, 0, 1))[n - 1]
                e.wait_ge(uh_ready, KD * n + k + 1)
                for kind in range(2):
                    h = slice(kind * NTOK, (kind + 1) * NTOK)
                    ins = e.scalar_tensor_tensor(out=ul[:, k, h], in0=tn[:, kind, k, :], scalar=mc[layer][:, pair, kind, one, k:k + 1],
                                                 in1=uh[:, k, h].bitcast(F32), op0=ALU.add, op1=ALU.subtract)
                ins.then_inc(ul_ready, 1)

            split_lo(e, 0)
            for s in range(FFN0):
                split_lo(e, s + 1)
                if s == 9:
                    normalise(0)
                if s == 13:
                    e.wait_ge(mc_ready, 1)
                    e.wait_ge(vec_cols, 3)
                    scales(0, 0, 0, 1, 0, True)
                    e.drain()
                    e.wait_ge(pads_zero, 1)
                    modulated(0, 0, 0, 0, into_padded).then_inc(pad_ready, 1)
                    e.drain()
                if s in (15, 17):
                    pool_windows(e, (s - 15) // 2, win)
                    e.drain().then_inc(pool_v, 1)
                if s in POOLED_AT:
                    g = POOLED_AT.index(s)
                    if g == 2:
                        e.wait_ge(pool_g, 2)
                    for k in (2 * g, 2 * g + 1):
                        split_u_lo(e, k, 0)
                if s == 22:
                    e.wait_ge(mc_ready, 2)
                    scales(1, 0, 1, 0, 24, False)
                if s in (POOL0, POOL0 + 1):
                    for k in range(4 * (s - POOL0), 4 * (s - POOL0) + 4):
                        if k < KD - 1:
                            e.wait_ge(pool_mm, k + 1)
                        else:
                            e.wait_ge(used, POOL0 + 1)
                        for kind in range(2):
                            e.scalar_tensor_tensor(out=ht[:, kind, k, :], in0=bank[POOL_BANKS[k % 4]][:, kind * NTOK:(kind + 1) * NTOK],
                                                   scalar=aff[:, 1, kind, k:k + 1], in1=ht[:, kind, k, :],
                                                   op0=ALU.mult, op1=ALU.add).then_inc(pool_added, 1)
                if s == 30:
                    e.wait_ge(mc_ready, 3)
                    scales(2, 0, 2, 0, 16, True)
                if s == POOL0 + 4:
                    e.drain()
                    inverse_root(1)
                if s in (NORM1_AT - 1, NORM1_AT):
                    for k in range(4 * (s - NORM1_AT + 1), 4 * (s - NORM1_AT + 2)):
                        scaled(1, k)
                if s in (NORM1_AT + 1, NORM1_AT + 2):
                    for k in range(4 * (s - NORM1_AT - 1), 4 * (s - NORM1_AT)):
                        shifted_lo(1, k)
                if s == 40:
                    e.wait_ge(mc_ready, 4)
                    scales(3, 1, 0, 1, 8, True)
            e.drain()

            def ffn_g_of(j, it):
                for c in range(2):
                    chunk_done(e, ffn_h3, w1_tile(j) + 1, j, c, it)
                    e.wait_ge(ffn_silu, val(2 * j + c + 1, 4, it))
                    if j:
                        e.wait_ge(ffn_gh, val(2 * (j - 1) + c + 1, 4, it))
                    e.tensor_tensor(gf[:, c, :], sg[:, c, :], bank[2 + c][:], ALU.mult).then_inc(ffn_g, 1)

            def ffn_lo(j, it):
                for c in range(2):
                    e.wait_ge(ffn_gh, val(2 * j + c + 1, 4, it))
                    e.tensor_tensor(gl[:, j % 2, c, :], gf[:, c, :], gh[:, j % 2, c, :].bitcast(F32),
                                    ALU.subtract).then_inc(ffn_gl, 1)

            def ffn_add(j, it, ks):
                for k in ks:
                    if k < KD - 1:
                        e.wait_ge(ffn_out, val(7 * j + k + 1, 14, it))
                    else:
                        e.wait_ge(used, val(w2_tile(j) + 1, 6, it))
                    for kind in range(2):
                        ins = e.scalar_tensor_tensor(out=ht[:, kind, k, :], in0=bank[4 + k % 4][:, kind * NTOK:(kind + 1) * NTOK],
                                                     scalar=mc[0][:, 2, kind, 1, k:k + 1], in1=ht[:, kind, k, :],
                                                     op0=ALU.mult, op1=ALU.add)
                    ins.then_inc(ffn_added, 1)

            split_lo(e, FFN0 + 1)
            split_lo(e, FFN0 + 2)
            ffn_g_of(0, None)
            e.drain()
            ffn_lo(0, None)
            with e.Fori(0, FF_BLOCKS // 2) as it:
                for u in range(2):
                    j, k = 1 + u, FFN0 + 2 + 3 * u
                    split_lo(e, (k + 1, it))
                    split_lo(e, (k + 2, it))
                    e.drain()
                    split_lo(e, (k + 3, it))
                    ffn_g_of(j, it)
                    ffn_add(j - 1, it, range(4))
                    e.drain()
                    ffn_lo(j, it)
                    ffn_add(j - 1, it, range(4, 8))
            e.drain()
            ffn_add(FF_BLOCKS - 1, None, range(8))
            e.drain()
            split_lo(e, IN0)
            inverse_root(2)
            for k in range(KD + 2):
                if k < KD:
                    scaled(2, k)
                if k >= 2:
                    shifted_lo(2, k - 2)
            split_lo(e, in_tile(0, 0))
            R = slice(64, 128)
            e.wait_ge(dt_act, 1)
            e.wait_ge(in_taken, 1)
            e.scalar_tensor_tensor(out=dts[R, 1, :], in0=dts[R, 0, :], scalar=-1.0, in1=dts[R, 0, :], op0=ALU.mult, op1=ALU.max).then_inc(dt_steps, 1)
            split_lo(e, in_tile(0, 1))
            e.wait_ge(dt_act, 2)
            e.tensor_scalar(dts[R, 2, :], dts[R, 1, :], 1.0, None, ALU.add).then_inc(dt_steps, 1)
            e.wait_ge(dt_act, 3)
            e.tensor_scalar(dts[R, 2, :], dts[R, 2, :], -1.0, None, ALU.add)
            e.drain()
            e.tensor_scalar(dts[R, 4, :], dts[R, 2, :], 0.0, None, ALU.is_equal)
            e.drain()
            e.tensor_tensor(dts[R, 2, :], dts[R, 2, :], dts[R, 4, :], ALU.add)
            e.tensor_tensor(dts[R, 3, :], dts[R, 3, :], dts[R, 4, :], ALU.add)
            e.drain()
            e.reciprocal(dts[R, 2, :], dts[R, 2, :])
            e.drain()
            e.tensor_tensor(dts[R, 3, :], dts[R, 3, :], dts[R, 2, :], ALU.mult)
            e.drain()
            e.tensor_tensor(dts[R, 3, :], dts[R, 3, :], dts[R, 1, :], ALU.mult)
            e.drain()
            e.scalar_tensor_tensor(out=dts[R, 0, :], in0=dts[R, 0, :], scalar=0.0, in1=dts[R, 3, :], op0=ALU.max, op1=ALU.add)
            e.drain()
            e.tensor_scalar(dts[R, 1, :], dts[R, 0, :], dpar[R, 2:3], -1.0, ALU.mult, ALU.mult)
            e.drain().then_inc(a_ready, 1)

            def conv(g, j):
                for c in range(2 if j == 4 else 1):
                    v_ = 6 * g + j + c
                    ch = 16 + 4 * c + g if j == 4 else 4 * g + j
                    n = 2 - c
                    e.wait_ge(in_taken, in_chunk(g, j, c) + 1)
                    if v_ >= 2:
                        e.wait_ge(conv_out, v_ - 1)
                    src = lambda k: cp[:, v_ % 2, 0:n, k:k + NTOK]
                    o = two(cacc[:, v_ % 2, :])[:, 0:n, :]
                    e.tensor_scalar(o, src(0), vb[:, ch:ch + 1], vb[:, 96 + ch:97 + ch], ALU.mult, ALU.add)
                    for k in range(1, 4):
                        e.drain()
                        ins = e.scalar_tensor_tensor(out=o, in0=src(k), scalar=vb[:, 24 * k + ch:24 * k + ch + 1], in1=o,
                                                     op0=ALU.mult, op1=ALU.add)
                    ins.then_inc(conv_acc, 1)

            def segs(g, u):
                c, q4 = u // 2, u % 2
                n = 4 * g + u
                seg_n, csc_n = unit_bufs(n)
                if n == 4 * (NG - 1) + 1:
                    e.wait_ge(conv_out, 6 * NG)
                elif n > 4 * (NG - 1):
                    e.wait_ge(y_mm, n - 1)
                elif n:
                    e.wait_ge(y_mm, n)
                for d in range(2):
                    e.wait_ge(bc_mm, 2 * n + d + 1)
                    for h in range(4):
                        hh = HPG * g + 4 * q4 + h
                        ins = e.tensor_scalar(seg_n[:, d, h * P:(h + 1) * P], bank[4 + d][:, h * P:(h + 1) * P],
                                              acs[:, 2 * d + c, hh:hh + 1], 0.0, ALU.subtract, ALU.min)
                    ins.then_inc(seg_ready, 1)

            def mixes(g, u):
                c = u // 2
                n = 4 * g + u
                seg_n, csc_n = unit_bufs(n)
                f4 = lambda x: x.rearrange("p (h n) -> p h n", h=4)
                for d in range(2):
                    e.wait_ge(exp_ready, 2 * n + d + 1)
                    e.tensor_tensor(f4(seg_n[:, d, :]), f4(seg_n[:, d, :]), cb[:, d, c, :].unsqueeze(1).to_broadcast([P, 4, P]), ALU.mult)
                    e.tensor_tensor(f4(csc_n[:, d, :]), f4(csc_n[:, d, :]),
                                    ct[:, g % 2, c * P:(c + 1) * P].unsqueeze(1).to_broadcast([P, 4, P]), ALU.mult)
                e.drain().then_inc(mix_ready, 1)

            def masks(g):
                e.wait_ge(aux_taken, aux_no[("cb", g, 0)] + 1)
                for c in range(2):
                    e.tensor_tensor(cb[:, 1, c, :], cb[:, 0, c, :], tri_ge[:], ALU.mult)
                e.drain()
                for c in range(2):
                    e.tensor_tensor(cb[:, 0, c, :], cb[:, 0, c, :], tri_le[:], ALU.mult)
                e.drain()

            def next_states(g):
                e.wait_ge(aux_taken, aux_no[("state", g, 3)] + 1)
                hv = lambda x: x.rearrange("p (h c) -> p h c", c=64)
                sdec = [y2[:, 4 * g + 2 * d:4 * g + 2 * d + 2, :].rearrange("p k n -> p (k n)") for d in range(2)]
                for d in range(2):
                    e.tensor_tensor(hv(sdec[d]), hv(states[:, d, :]),
                                    wdec[:, 6 + d, HPG * g:HPG * g + HPG].unsqueeze(2).to_broadcast([P, HPG, 64]), ALU.mult)
                e.drain()
                for d in range(2):
                    e.tensor_tensor(states[:, 2 + d, :], states[:, 2 + d, :], sdec[d], ALU.add)
                e.drain().then_inc(st_ready, 1)

            def y_out(g, c):
                e.wait_ge(y_mm, 4 * g + 2 * c + 2)
                q = g % 2
                for i in range(4):
                    k = 4 * g + i
                    e.scalar_tensor_tensor(out=y2[:, k, c * P:(c + 1) * P], in0=xst[:, q, i, c * P:(c + 1) * P], scalar=dcol[:, k:k + 1],
                                           in1=bank[6 + c][:, i * P:(i + 1) * P], op0=ALU.mult, op1=ALU.add)
                e.drain()
                o = y2[:, 4 * g:4 * g + 4, c * P:(c + 1) * P]
                e.tensor_tensor(o, o, sz[:, q, :, c * P:(c + 1) * P], ALU.mult).then_inc(y_taken, 1)

            def y_lo(k0, k1):
                for k in range(k0, k1):
                    e.wait_ge(yh_ready, k + 1)
                    e.scalar_tensor_tensor(out=yl[:, k, :], in0=y2[:, k, :], scalar=va[:, 32 + k:33 + k], in1=yh[:, k, :].bitcast(F32),
                                           op0=ALU.mult, op1=ALU.subtract).then_inc(yl_ready, 1)

            e.wait_ge(pads2, 1)
            for g in range(NG):
                for j in range(5):
                    if g and j:
                        segs(g - 1, j - 1)
                    if g and j == 1:
                        masks(g - 1)
                    if g and j:
                        mixes(g - 1, j - 1)
                    if (g, j) != (0, 0):
                        split_lo(e, in_tile(g, j) + 1)
                    if (g, j) == (0, 3):
                        e.wait_ge(wdec_ready, 1)
                        for n, (tile, d) in enumerate(((2, 0), (2, 1), (3, 0), (3, 1), (0, 0), (1, 1))):
                            e.tensor_tensor(wdec[:, n, :], wdec[:, n, :], dt_tok[:, tile, 32 * d:32 * d + 32], ALU.mult)
                        e.drain().then_inc(wdec_ready, 1)
                    if g and j == 1:
                        next_states(g - 1)
                    if g and j == 3:
                        y_out(g - 1, 0)
                    if g >= 2 and j == 0:
                        y_out(g - 2, 1)
                    conv(g, j)
            split_lo(e, OUT0 + 1)
            segs(NG - 1, 0)
            y_lo(0, 4)
            y_out(NG - 2, 1)
            masks(NG - 1)
            mixes(NG - 1, 0)
            y_lo(4, 8)
            split_lo(e, OUT0 + 2)
            y_lo(8, 12)
            next_states(NG - 1)
            split_lo(e, OUT0 + 3)
            segs(NG - 1, 1)
            mixes(NG - 1, 1)
            split_lo(e, OUT0 + 4)
            segs(NG - 1, 2)
            mixes(NG - 1, 2)
            y_out(NG - 1, 0)
            segs(NG - 1, 3)
            mixes(NG - 1, 3)
            e.drain()
            y_out(NG - 1, 1)
            y_lo(12, 16)
            for t in range(5, 8):
                if t == 6:
                    e.wait_ge(ry_root, 1)
                    e.reciprocal(ry[:, 2:4], ry[:, 0:2])
                split_lo(e, OUT0 + t)
            e.drain().then_inc(lo2, 3)
            e.wait_ge(mods_ready, 1)
            e.wait_ge(hl_ready, 1)
            e.wait_ge(rows_back, 6 * 16)
            e.scalar_tensor_tensor(out=mods[:, 2, :], in0=mods[:, 2, :], scalar=1.0, in1=nfw[:], op0=ALU.add, op1=ALU.mult)
            for n in range(2):
                e.wait_ge(used, OUT0 + 4 * n + 4)
                for t in range(2):
                    s = slice(n * 512, (n + 1) * 512)
                    e.scalar_tensor_tensor(out=v[:, t, s], in0=bank[4 * n + t][:], scalar=ry[:, 2 + t:3 + t], in1=mods[:, 0, s],
                                           op0=ALU.mult, op1=ALU.mult)
                    e.drain()
                    e.tensor_tensor(hl[:, t, s], hl[:, t, s], v[:, t, s], ALU.add)
            e.drain().then_inc(h_ready, 1)
            e.drain().then_inc(lo2, 3)
            e.wait_ge(hsq_ready, 1)
            e.reciprocal(stat[:, 4:6], stat[:, 2:4])
            e.drain()
            for t in range(2):
                e.scalar_tensor_tensor(out=v[:, t, :], in0=hl[:, t, :], scalar=stat[:, 4 + t:5 + t], in1=mods[:, 2, :],
                                       op0=ALU.mult, op1=ALU.mult)
                e.drain()
                e.tensor_tensor(v[:, t, :], v[:, t, :], mods[:, 1, :], ALU.add).then_inc(v_ready, 1)
            def lo_of(k, i, b=None):
                e.wait_ge(hi2, val2(k + 1, i, b, 6))
                e.tensor_tensor(wlo2[:, k % SPL2, :], raw2[:, k % RAW2, :], whi2[:, k % SPL2, :].bitcast(F32),
                                ALU.subtract).then_inc(lo2, 1)

            e.memset(acc[:], 0.0)
            e.memset(osh[:].bitcast(F32), 0.0)
            e.memset(osl[:].bitcast(F32), 0.0)
            e.memset(put[:].bitcast(F32), 0.0)
            e.memset(pos_item[:], -1.0)
            e.memset(gate_item[:], 0.0)
            e.memset(ftab[:], 0.0)
            e.drain().then_inc(osl_ready, 2)
            lo_of(0, None)
            lo_of(1, None)
            e.wait_ge(lg_mm, 1)
            e.tensor_copy(lg[:].rearrange("p t x -> p (t x)"), bank[6][:, 16:32])
            e.drain()
            for t in range(2):
                own = lg[:, t, :].unsqueeze(2).to_broadcast([P, NE, NE])
                other = lg[:, t, :].unsqueeze(1).to_broadcast([P, NE, NE])
                e.tensor_tensor(cmp[:, t], other, own, ALU.is_gt)
                e.tensor_tensor(eqs[:, t], other, own, ALU.is_equal)
                e.drain()
                e.tensor_tensor(eqs[:, t], eqs[:, t], before[:], ALU.mult)
                e.drain()
                e.tensor_tensor(cmp[:, t], cmp[:, t], eqs[:, t], ALU.add)
                e.drain()
                e.tensor_reduce(sel[:, t, :], cmp[:, t], AX_X, ALU.add)
                e.tensor_reduce(rsc[:, 2 + t:3 + t], lg[:, t, :], AX_X, ALU.max)
                e.drain()
                e.tensor_scalar(sel[:, t, :], sel[:, t, :], 1.5, None, ALU.is_lt)
                e.tensor_scalar(rsc[:, t:t + 1], rsc[:, 2 + t:3 + t], -1.0, None, ALU.mult)
            e.drain().then_inc(rt_dve, 1)
            e.wait_ge(rt_act, 1)
            for t in range(2):
                e.tensor_tensor(gate[:, t, :], gate[:, t, :], sel[:, t, :], ALU.mult)
                e.drain()
                e.tensor_reduce(rsc[:, 4 + t:5 + t], gate[:, t, :], AX_X, ALU.add)
                e.drain()
                e.reciprocal(rsc[:, 6 + t:7 + t], rsc[:, 4 + t:5 + t])
                e.drain()
                e.tensor_scalar(gate[:, t, :], gate[:, t, :], rsc[:, 6 + t:7 + t], None, ALU.mult)
            e.wait_ge(rt_mm, 2)
            for t in range(2):
                e.scalar_tensor_tensor(out=pos[:, t, :], in0=bank[6][:, 32 + 8 * t:40 + 8 * t], scalar=1.0, in1=sel[:, t, :],
                                       op0=ALU.add, op1=ALU.mult)
            e.tensor_copy(cnt[:], bank[6][:, 48:56])
            e.drain()
            for t in range(2):
                e.tensor_scalar(pos_item[:, t, 0:NE], pos[:, t, :], -1.0, None, ALU.add)
                e.tensor_copy(gate_item[:, t, 1:1 + NE], gate[:, t, :])
            e.drain()

            def pick_of(col):
                for t in range(2):
                    e.tensor_scalar(pick[:, t, :], slot_id[:], pos_item[:, t, col], None, ALU.is_equal)

            pick_of(slice(0, 1))
            e.drain().then_inc(pick_ready, 1)
            e.tensor_scalar(over[:], cnt[:], float(P), None, ALU.is_gt)
            e.drain()
            e.tensor_tensor(cmp[:, 0], over[:].unsqueeze(1).to_broadcast([P, NE, NE]), before[:], ALU.mult)
            e.tensor_reduce(rsc[:, 8:9], over[:], AX_X, ALU.add)
            e.drain()
            e.tensor_reduce(rsc[:, 12:13], over[:], AX_X, ALU.add)
            e.tensor_reduce(cnt[:], cmp[:, 0], AX_X, ALU.add)
            e.drain()
            for m in range(3):
                e.scalar_tensor_tensor(out=more[:, m, :], in0=cnt[:], scalar=float(m), in1=over[:], op0=ALU.is_equal, op1=ALU.mult)
            e.drain()
            bc3 = lambda x: x.unsqueeze(1).to_broadcast([P, 3, NE])
            e.tensor_tensor(tmp3[:], more[:], bc3(expert_id[:]), ALU.mult)
            e.drain()
            e.tensor_copy(ftab[:, 0:NE], expert_id[:])
            e.tensor_reduce(ftab[:, NE:NE + 3], tmp3[:], AX_X, ALU.add)
            e.tensor_scalar(ftab[:, 12:13], rsc[:, 8:9], float(NE), None, ALU.add)
            e.drain()
            e.tensor_copy(itab[:], ftab[0:1, :])
            e.drain().then_inc(tab_ready, 1)
            for t in range(2):
                e.scalar_tensor_tensor(out=tmp3[:], in0=bc3(pos[:, t, :]), scalar=-float(P), in1=more[:], op0=ALU.add, op1=ALU.mult)
                e.drain()
                e.tensor_reduce(pos_item[:, t, NE:NE + 3], tmp3[:], AX_X, ALU.add)
                e.drain()
                e.tensor_scalar(pos_item[:, t, NE:NE + 3], pos_item[:, t, NE:NE + 3], -1.0, None, ALU.add)
                e.tensor_tensor(tmp3[:], bc3(gate[:, t, :]), more[:], ALU.mult)
                e.drain()
                e.tensor_reduce(gate_item[:, t, 1 + NE:4 + NE], tmp3[:], AX_X, ALU.add)
                e.drain()


            def gm_of(i, blk, b=None):
                e.wait_ge(silu2, val3(blk + 1, i, b))
                e.tensor_tensor(gme[:], sge[:], bank[1][:], ALU.mult).then_inc(gm_ready, 1)

            def gtl_of(i, blk, b=None):
                e.wait_ge(gth_ready, val3(blk + 1, i, b))
                e.tensor_tensor(gtl[:].rearrange("p f n -> p (f n)"), bank[2][:], gth[:].bitcast(F32).rearrange("p f n -> p (f n)"),
                                ALU.subtract).then_inc(gtl_ready, 1)

            def xgl_of(n):
                e.wait_ge(xgh_ready, n)
                for h in range(2):
                    ins = e.tensor_tensor(xgl[:, 4 * h:4 * h + 4, :].rearrange("p k n -> p (k n)"), bank[5 + h][:],
                                          xgh[:, 4 * h:4 * h + 4, :].bitcast(F32).rearrange("p k n -> p (k n)"), ALU.subtract)
                ins.then_inc(xgl_ready, 1)

            def block(i, k, blk, b=None):
                lo_of(k + 2, i, b)
                gtl_of(i, blk - 1, b)
                for n in range(3, 7):
                    lo_of(k + n, i, b)
                gm_of(i, blk, b)
                lo_of(k + 7, i, b)

            def scattered(i):
                for n, bk in enumerate(SCATTER_BANKS):
                    t, h = n // 2, n % 2
                    e.wait_ge(scat_mm, i * 4 + (n + 1))
                    o = acc[:, t, h * 512:(h + 1) * 512]
                    e.scalar_tensor_tensor(out=o, in0=bank[bk][:], scalar=gate_item[:, t, bass.ds(i, 1)], in1=o,
                                           op0=ALU.mult, op1=ALU.add).then_inc(acc_added, 1)

            xgl_of(1)
            count = e.value_load(itab[0:1, 12:13], min_val=NE, max_val=MAX_ITEMS)
            with e.Fori(0, count) as i:
                for k in (2, 3, 4, 5):
                    lo_of(k, i)
                e.wait_ge(used2, i * TPI + (4 + SPL2))
                gm_of(i, 0)
                scattered(i)
                block(i, 4, 1)
                e.wait_ge(put_ready, i + 1)
                pick_of(bass.ds(i + 1, 1))
                e.drain().then_inc(pick_ready, 1)
                with e.Fori(0, EB - 2) as b:
                    block(i, 10, 2, b)
                lo_of(TPI, i)
                gtl_of(i, EB - 1)
                xgl_of(i + 2)
                lo_of(TPI + 1, i)
                for n in range(2):
                    h = slice(n * 512, (n + 1) * 512)
                    e.wait_ge(osh_ready, i * 2 + (n + 1))
                    e.tensor_tensor(osl[:, h], bank[3 + n][:], osh[:, h].bitcast(F32), ALU.subtract).then_inc(osl_ready, 1)
            scattered(count)
            e.drain()
            for t in range(2):
                e.tensor_tensor(acc[:, t, :], acc[:, t, :], mods[:, 3, :], ALU.mult)
                e.drain()
                e.tensor_tensor(hl[:, t, :], hl[:, t, :], acc[:, t, :], ALU.add)
            e.drain().then_inc(out_sq, 1)
            e.wait_ge(out_sq, 2)
            e.reciprocal(stat[:, 12:14], stat[:, 10:12])
            e.drain()
            for t in range(2):
                e.scalar_tensor_tensor(out=acc[:, t, :], in0=hl[:, t, :], scalar=stat[:, 12 + t:13 + t], in1=fnw[:],
                                       op0=ALU.mult, op1=ALU.mult).then_inc(out_ready, 1)

        @block.tensor
        def _(e):
            def passes(o, wsl, usl, first, last):
                ins = None
                for n, (i, j) in enumerate(((0, 0), (0, 1), (1, 0))):
                    ins = e.matmul(o, wsl[i], usl[j], start=first and n == 0, stop=last and n == 2)
                return ins

            def wpart(s, view):
                return view(whi[:, s, :]), view(wlo[:, s, :])

            e.wait_ge(loaded_c, 2 * 16)
            e.wait_ge(consts_ready, 1)
            e.transpose(bank[7][:, 184:200], rows_in[0:16, 2, :], ident[0:16, 0:16]).then_inc(vec_t, 1)
            e.wait_ge(vec_cols, 2)

            def mod_tile(m):
                s, plain = mod_at(m), mod_at(m) in PLAIN
                n, kh = m // 2, m % 2
                if plain:
                    e.wait_ge(landed[slot(s)], 16 * dmas_into_slot(s))
                else:
                    s = w_ready(e, s)
                    if m == 2:
                        e.wait_ge(cst_ready, 4)
                if kh == 0 and n >= 2:
                    e.wait_ge(mod_row, n - 1)
                for k in range(4):
                    if plain:
                        ins = e.matmul(bank[n % 2][0:4, :], csf[:, 4 * kh + k, :], landing(s)[:, k * 512:(k + 1) * 512],
                                       start=kh == 0 and k == 0, stop=kh == 1 and k == 3)
                        continue
                    for i, part in enumerate((whi, wlo)):
                        ins = e.matmul(bank[n % 2][:], cst[:, 4 * kh + k, :], part[:, s, k * 512:(k + 1) * 512],
                                       start=kh == 0 and k == 0 and i == 0, stop=kh == 1 and k == 3 and i == 1)
                ins.then_inc(used, 1)

            def fold_pair(n):
                e.wait_ge(mod_back, 16 * (n + 1))
                e.wait_ge(loaded_bias, 32)
                if n:
                    e.wait_ge(mc_ready, n)
                e.matmul(bank[5][:, 0:32], rb[:, n // 3, n % 3, :], fold[:], start=True, stop=True).then_inc(fold_mm, 1)

            def mean_square(n):
                for k in range(KD):
                    e.wait_ge(sq_ready, KD * n + k + 1)
                    ins = e.matmul(bank[MS_BANK[n]][:], ones[:], sq[:, :, k, :], start=k == 0, stop=k == KD - 1)
                ins.then_inc(ms_ready, 1)

            for s in range(FFN0):
                if s == POOL0:
                    t = w_ready(e, POOL0)
                    e.wait_ge(x_copied, KD)
                    for g in range(4):
                        e.wait_ge(ul_ready, 2 * g + 2)
                        for o in range(2):
                            if g >= 2:
                                e.wait_ge(pool_added, 2 * (2 * g + o - 3))
                            for i in range(2):
                                ins = passes(bank[POOL_BANKS[(2 * g + o) % 4]][:],
                                             wpart(t, lambda w: w[:, (2 * g + i) * 256 + o * P:(2 * g + i) * 256 + (o + 1) * P]),
                                             (uh[:, 2 * g + i, :], ul[:, 2 * g + i, :]), i == 0, i == 1)
                            ins.then_inc(used if (g, o) == (3, 1) else pool_mm, 1)
                else:
                    mod_tile(mod_no(s))
                if s < KD:
                    if s == 0:
                        e.wait_ge(loaded_x, 64)
                    if s >= 2:
                        e.wait_ge(x_copied, s - 1)
                    if s == 4:
                        e.wait_ge(loaded_vec, 7 * 16)
                        e.transpose(bank[7][:, 0:48], rows_in[0:48, 0, :], ident[0:48, 0:48])
                        e.transpose(bank[7][:, 64:184], rows_in[0:120, 1, :], ident[0:120, 0:120]).then_inc(vec_t, 1)
                    for i in range(4):
                        ins = e.transpose(bank[2 + s % 2][:, i * P:(i + 1) * P], xtok[:, i, s * P:(s + 1) * P], ident[:])
                    ins.then_inc(x_t, 1)
                if s == KD:
                    e.wait_ge(consts_ready, 2)
                    mean_square(0)
                if s in (12, 20, 28, 38):
                    fold_pair((12, 20, 28, 38).index(s))
                if s == POOL0 + 3:
                    mean_square(1)
            e.wait_ge(mod_row, 24)
            e.wait_ge(mc_ready, 4)
            e.wait_ge(ul_ready, 2 * KD)

            def hidden(t, b0, j, it, free):
                s = w_ready(e, t)
                for c in range(2):
                    if j:
                        e.wait_ge(free, val(2 * (j - 1) + c + 1, 4, it))
                    for k in range(KD):
                        ins = passes(bank[b0 + c][:], wpart(s, lambda w: w[:, k * 256 + c * P:k * 256 + (c + 1) * P]),
                                     (uh[:, k, :], ul[:, k, :]), k == 0, k == KD - 1)
                    ins.then_inc(used if c else (ffn_h3 if b0 else ffn_h1), 1)

            def down(t, j, it):
                s = w_ready(e, t)
                e.wait_ge(ffn_gl, val(2 * j + 2, 4, it))
                for k in range(KD):
                    if 8 * j + k >= 4:
                        e.wait_ge(ffn_added, val(8 * j + k - 3, 16, it))
                    for i in range(2):
                        ins = passes(bank[4 + k % 4][:], wpart(s, lambda w: w[:, i * D + k * P:i * D + (k + 1) * P]),
                                     (gh[:, j % 2, i, :], gl[:, j % 2, i, :]), i == 0, i == 1)
                    ins.then_inc(used if k == KD - 1 else ffn_out, 1)

            hidden(FFN0, 0, 0, None, ffn_silu)
            hidden(FFN0 + 1, 2, 0, None, ffn_g)
            with e.Fori(0, FF_BLOCKS // 2) as it:
                for u in range(2):
                    j, k = 1 + u, FFN0 + 2 + 3 * u
                    hidden((k, it), 0, j, it, ffn_silu)
                    hidden((k + 1, it), 2, j, it, ffn_g)
                    down((k + 2, it), j - 1, it)
            down(IN0 - 1, FF_BLOCKS - 1, None)
            e.wait_ge(ffn_g, 2 * FF_BLOCKS)
            mean_square(2)
            def project(t, c0, q, n, done):
                s = w_ready(e, t)
                if q >= 2:
                    e.wait_ge(in_taken, q - 1)
                for k in range(KD):
                    if q == 0:
                        e.wait_ge(ul_ready, 2 * KD + k + 1)
                    ins = passes(bank[q % 2][:, 0:n], wpart(s, lambda w: w[:, k * 256 + c0:k * 256 + c0 + P]),
                                 (uh[:, k, 0:n], ul[:, k, 0:n]), k == 0, k == KD - 1)
                ins.then_inc(done, 1)

            def aux_bank(key):
                n = aux_no[key]
                if n >= 2:
                    e.wait_ge(aux_taken, n - 1)
                return bank[2 + n % 2]

            project(IN0, P, 0, NT2, used)
            def dt_by_tokens():
                e.wait_ge(a_ready, 1)
                b = aux_bank(("dt", 0, 0))
                for i in range(2):
                    for t in range(4):
                        ins = e.transpose(b[:, i * 256 + t * 64:i * 256 + (t + 1) * 64], dts[64:128, i, t * P:(t + 1) * P], ident[64:128, 64:128])
                ins.then_inc(aux_mm, 1)

            def decay_sums():
                b = aux_bank(("decay", 0, 0))
                e.wait_ge(aux_taken, 1)
                F, B = slice(0, 32), slice(32, 64)
                sums = [[(tri_gt, 2, F), (ones, 3, F)], [(tri_lt, 2, B)], [(tri_gt, 3, F)], [(tri_lt, 3, B), (ones, 2, B)],
                        [(tri_gt, 0, F)], [(tri_lt, 1, B)], [(ones, 0, F)], [(ones, 1, B)],
                        [(tri_le, 0, F)], [(tri_le, 1, F)], [(tri_ge, 0, B)], [(tri_ge, 1, B)]]
                for n, terms in enumerate(sums):
                    for i, (w, t, s) in enumerate(terms):
                        ins = e.matmul(b[:, n * 32:(n + 1) * 32], w[:], a_tok[:, t, s], start=i == 0, stop=i == len(terms) - 1)
                ins.then_inc(aux_mm, 1)

            def turn(g, i):
                v_ = 6 * g + (4 if i == 0 else i - 1)
                b = aux_bank(("turn", g, i))
                e.wait_ge(conv_out, v_ + 1)
                lat = bt[:, g % 2, :] if i == 0 else xst[:, g % 2, i - 1, :]
                con = ccv[:, v_ % 2, :]
                for t in range(4):
                    src = lat[:, t * P:(t + 1) * P] if t < 2 else con[:, (t - 2) * P:(t - 1) * P]
                    ins = e.transpose(b[:, t * P:(t + 1) * P], src, ident[:])
                ins.then_inc(aux_mm, 1)

            def products(g):
                b = aux_bank(("cb", g, 0))
                e.wait_ge(conv_out, 6 * g + 6)
                for c in range(2):
                    s = slice(c * P, (c + 1) * P)
                    ins = e.matmul(b[:, s], bt[:, g % 2, s], ct[:, g % 2, s], start=True, stop=True)
                ins.then_inc(aux_mm, 1)

            def state(g, i):
                terms = (((2, 0), (3, 1)), ((2, 2), (3, 3)), ((0, 4),), ((1, 5),))[i]
                b = aux_bank(("state", g, i))
                for n, (t, m) in enumerate(terms):
                    e.wait_ge(xdd_ready, 6 * g + m + 1)
                    ins = e.matmul(b[:], b_tok[:, g % 2, t, :], xdd[m % 2][:], start=n == 0, stop=n == len(terms) - 1)
                ins.then_inc(aux_mm, 1)

            def cumulative(g, u):
                c, q4 = u // 2, u % 2
                for d, tri in enumerate((tri_le, tri_ge)):
                    for h in range(4):
                        hh = 32 * d + HPG * g + 4 * q4 + h
                        ins = e.matmul(bank[4 + d][:, h * P:(h + 1) * P], a_tok[:, c, hh:hh + 1].to_broadcast([P, P]), tri[:],
                                       start=True, stop=True)
                    ins.then_inc(bc_mm, 1)

            def heads(g, u):
                c, q4 = u // 2, u % 2
                n = 4 * g + u
                seg_n, csc_n = unit_bufs(n)
                if q4 == 0 and g:
                    e.wait_ge(y_taken, 2 * (g - 1) + c + 1)
                e.wait_ge(xd_ready, 4 * (g + 1))
                e.wait_ge(st_ready, g + 1)
                e.wait_ge(mix_ready, n + 1)
                for h in range(4):
                    hg = 4 * q4 + h
                    o = bank[6 + c][64 * (h % 2):64 * (h % 2) + 64, (hg // 2) * P:(hg // 2 + 1) * P]
                    hs, ms = slice(hg * 64, hg * 64 + 64), slice(h * P, (h + 1) * P)
                    st = (0 if c == 0 else 2, 3 if c == 0 else 1)
                    for d in range(2):
                        e.matmul(o, xd[:, d, c, hs], seg_n[:, d, ms], start=d == 0, stop=False)
                    for d in range(2):
                        ins = e.matmul(o, states[:, st[d], hs], csc_n[:, d, ms], start=False, stop=d == 1)
                ins.then_inc(y_mm, 1)

            def out_tile(n, kq):
                s = w_ready(e, OUT0 + 4 * n + kq)
                e.wait_ge(yl_ready, 4 * (kq + 1))
                if (n, kq) == (0, 0):
                    e.wait_ge(in_taken, 1 + 10 * NG)
                for t in range(2):
                    for k in range(4):
                        ts = slice(t * P, (t + 1) * P)
                        c = 4 * kq + k
                        ins = passes(bank[4 * n + t][:], (yh[:, c, ts], yl[:, c, ts]),
                                     wpart(s, lambda w: w[:, k * 512:(k + 1) * 512]), kq == 0 and k == 0, kq == 3 and k == 3)
                ins.then_inc(used, 1)

            for g in range(NG):
                for j in range(5):
                    for c in range(2):
                        project(in_tile(g, j), c * P, in_chunk(g, j, c), NTOK if c else NT2, used if c else in_mm)
                        if g and (j, c) == (0, 0):
                            turn(g - 1, 0)
                            products(g - 1)
                        if g and (j, c) == (1, 0):
                            state(g - 1, 2)
                            state(g - 1, 3)
                    if (g, j) == (0, 1):
                        dt_by_tokens()
                    if (g, j) == (0, 2):
                        decay_sums()
                    if g and j == 0:
                        state(g - 1, 0)
                    if j:
                        turn(g, j)
                    if g and j:
                        heads(g - 1, j - 1)
                    if g and j < 4:
                        cumulative(g - 1, j)
                    if g and j == 0:
                        state(g - 1, 1)
            turn(NG - 1, 0)
            cumulative(NG - 1, 0)
            products(NG - 1)
            state(NG - 1, 0)
            out_tile(0, 0)
            state(NG - 1, 1)
            out_tile(0, 1)
            state(NG - 1, 2)
            state(NG - 1, 3)
            for u in range(4):
                if u < 3:
                    e.wait_ge(exp_ready, 2 * (4 * (NG - 1) + u) + 2)
                    cumulative(NG - 1, u + 1)
                heads(NG - 1, u)
                if u == 0:
                    out_tile(0, 2)
                if u in (1, 2):
                    for n in (2 * u - 2, 2 * u - 1):
                        b = aux_bank(("resid", 0, n))
                        t, half = n // 2, n % 2
                        for k in range(4):
                            ins = e.transpose(b[:, k * P:(k + 1) * P], ht[:, 0, 4 * half + k, t * P:(t + 1) * P], ident[:])
                        ins.then_inc(aux_mm, 1)
            for n, kq in [(0, 3)] + [(1, kq) for kq in range(4)]:
                if (n, kq) == (1, 3):
                    e.wait_ge(rows_back, 6 * 16)
                    for i in range(8):
                        b = aux_bank(("mods", 0, i))
                        e.matmul(b[:], sel_row[:], mrow5[:, i // 2, (i % 2) * 512:(i % 2 + 1) * 512], start=True, stop=True).then_inc(aux_mm, 1)
                out_tile(n, kq)
                if (n, kq) == (0, 3):
                    e.wait_ge(ysum_ready, 1)
                    for t in range(2):
                        ins = e.matmul(bank[6][:, t:t + 1], ysum[:, t * P:(t + 1) * P], ones[:, 0:1], start=True, stop=True)
                    ins.then_inc(rt_mm, 1)
            e.drain().then_inc(used2, SPL2)
            for n in range(4):
                t, half = n // 2, n % 2
                e.wait_ge(v_ready, t + 1)
                b = aux_bank(("v", 0, n))
                for k in range(4):
                    ins = e.transpose(b[:, k * P:(k + 1) * P], v[:, t, (4 * half + k) * P:(4 * half + k + 1) * P], ident[:])
                ins.then_inc(aux_mm, 1)
            e.wait_ge(aux_taken, len(aux))
            for t in range(2):
                for k in range(KD):
                    ins = e.matmul(bank[6][:, 16 + 8 * t:24 + 8 * t], vt[:, k, t * P:(t + 1) * P], rw[:, k, :], start=k == 0, stop=k == KD - 1)
            ins.then_inc(lg_mm, 1)
            e.wait_ge(rt_dve, 1)
            e.matmul(bank[6][:, 32:40], tri_lt[:], sel[:, 0, :], start=True, stop=True)
            e.matmul(bank[6][:, 40:48], tri_lt[:], sel[:, 1, :], start=True, stop=False)
            e.matmul(bank[6][:, 40:48], ones[:], sel[:, 0, :], start=False, stop=True)
            e.matmul(bank[6][:, 48:56], ones[:], sel[:, 0, :], start=True, stop=False)
            e.matmul(bank[6][:, 48:56], ones[:], sel[:, 1, :], start=False, stop=True).then_inc(rt_mm, 1)

            def gather(n):
                e.wait_ge(pick_ready, n)
                for k in range(KD):
                    for t in range(2):
                        ins = e.matmul(bank[5 + k // 4][:, (k % 4) * P:(k % 4 + 1) * P], v[:, t, k * P:(k + 1) * P], pick[:, t, :],
                                       start=t == 0, stop=t == 1)
                ins.then_inc(gather_mm, 1)

            def tile2(k, i, b=None):
                e.wait_ge(lo2, val2(RAW2 + k + 1, i, b, 6))
                return k % SPL2

            def up(i, k, bk, b=None):
                for half in range(2):
                    s = tile2(k + half, i, b)
                    for kk in range(4):
                        c = 4 * half + kk
                        w = slice(kk * 512, (kk + 1) * 512)
                        ins = passes(bank[bk][:], (xgh[:, c, :], xgl[:, c, :]), (whi2[:, s, w], wlo2[:, s, w]), c == 0, c == KD - 1)
                    ins.then_inc(used2, 1)

            def down2(i, k, blk, first, last, b=None):
                e.wait_ge(gtl_ready, val3(blk + 1, i, b))
                for half in range(2):
                    s = tile2(k + half, i, b)
                    for f in range(2):
                        ff = 2 * half + f
                        for n in range(2):
                            w = slice(f * D + n * 512, f * D + (n + 1) * 512)
                            ins = passes(bank[3 + n][:], (gth[:, ff, :], gtl[:, ff, :]), (whi2[:, s, w], wlo2[:, s, w]),
                                         first and ff == 0, last and ff == 3)
                    ins.then_inc(used2, 1)

            def turn2(i, blk, b=None):
                e.wait_ge(gm_ready, val3(blk + 1, i, b))
                for f in range(4):
                    ins = e.transpose(bank[2][:, f * P:(f + 1) * P], gme[:, f * P:(f + 1) * P], ident[:])
                ins.then_inc(turn_mm, 1)

            def scatter(i):
                e.wait_ge(osl_ready, i * 2 + 2)
                for n, bk in enumerate(SCATTER_BANKS):
                    t, h = n // 2, slice(n % 2 * 512, (n % 2 + 1) * 512)
                    e.matmul(bank[bk][:], put[:, t, :], osh[:, h], start=True, stop=False)
                    e.matmul(bank[bk][:], put[:, t, :], osl[:, h], start=False, stop=True).then_inc(scat_mm, 1)

            gather(1)
            e.wait_ge(tab_ready, 1)
            count = e.value_load(itab[0:1, 12:13], min_val=NE, max_val=MAX_ITEMS)
            with e.Fori(0, count) as i:
                e.wait_ge(xgl_ready, i + 1)
                up(i, 0, 0)
                up(i, 2, 1)
                scatter(i)
                e.wait_ge(acc_added, i * 4 + 1)
                turn2(i, 0)
                up(i, 4, 0)
                e.wait_ge(acc_added, i * 4 + 4)
                for t in range(2):
                    ins = e.transpose(bank[7][:, t * P:(t + 1) * P], pick[:, t, :], ident[:])
                ins.then_inc(put_mm, 1)
                up(i, 6, 1)
                e.wait_ge(osl_ready, i * 2 + 2)
                down2(i, 8, 0, True, False)
                turn2(i, 1)
                with e.Fori(0, EB - 2) as b:
                    up(i, 10, 0, b)
                    up(i, 12, 1, b)
                    down2(i, 14, 1, False, False, b)
                    turn2(i, 2, b)
                gather(i + 2)
                down2(i, TPI - 2, EB - 1, False, True)
            e.wait_ge(put_ready, count)
            scatter(count)


_INS = ['x', 'c', 'ctx', 'c_ctx', 'ada_w', 'ada_b', 'norm_mix_w', 'norm_ffn_w',
        'pool_w', 'pool_scale', 'ssd_in_w', 'ssd_conv_w', 'ssd_conv_b', 'ssd_A_log', 'ssd_dt_bias', 'ssd_D',
        'ssd_norm_w', 'ssd_out_w', 'ffn_w1', 'ffn_w3', 'ffn_w2', 'moe_router_w', 'moe_w1', 'moe_w3',
        'moe_w2', 'final_norm_w']
_OUTS = [((1, 256, 1024), 'float32')]


def kernel(**inputs):
    import numpy as _np
    import concourse.bacc as _bacc
    from concourse import mybir as _mybir
    from concourse.bass_utils import run_bass_kernel_spmd as _run

    nc = _bacc.Bacc("TRN2", target_bir_lowering=False, num_devices=1)
    arrays, args = {}, {}
    for name in _INS:
        a = _np.ascontiguousarray(inputs[name])
        arrays[f"in_{name}_dram"] = a
        args[name] = nc.dram_tensor(f"in_{name}_dram", a.shape, _mybir.dt.from_np(a.dtype), kind="ExternalInput").ap()
    shape, dtype = _OUTS[0]
    out = nc.dram_tensor("out_0_dram", shape, _mybir.dt.from_np(_np.dtype(dtype)), kind="ExternalOutput").ap()
    hybrid_backbone(nc, args, out)
    r = _run(nc, [arrays], core_ids=[0])
    return r.results[0]["out_0_dram"]
```
